# Optimizing a Trainium2 kernel written in Bass

```python
import jax
import jax.numpy as jnp
from jax import lax
import numpy as np

D_MODEL = 1024
BATCH = 1
SEQ = 1024
DEPTH = 1
DEC_BATCH = 8
DEC_SEQ = 8
PAST_LEN = 256
PAGE_SIZE = 128

HEAD_DIM = 64
N_HEADS = D_MODEL // HEAD_DIM
H_A = (3 * N_HEADS) // 8
G_B = N_HEADS // 4
H_C = N_HEADS - H_A - G_B
W_A = H_A * HEAD_DIM
W_B = G_B * HEAD_DIM
W_C = H_C * HEAD_DIM
MIX_WIDTH = W_A + W_B + W_C
GDN_CONV = 4
GDN_CHUNK = 64
CHUNK = 128
FOX_QBLOCK = 128
D_FF = 2816
FFN_CONV = 3
N_IN = 4 * W_A + 2 * H_A + 2 * W_B + 3 * W_C + H_C
EPS = 1e-6
NEG_INF = -1e30

kernel_name = 'hymba_gdn_gmlp_fox_convffn_step'

def rmsnorm(x, g):
    x32 = x.astype(jnp.float32)
    y = x32 * lax.rsqrt(jnp.mean(x32 * x32, axis=-1, keepdims=True) + EPS)
    return y * g.astype(jnp.float32)

def layernorm(x, g, b):
    x32 = x.astype(jnp.float32)
    mu = jnp.mean(x32, axis=-1, keepdims=True)
    xc = x32 - mu
    var = jnp.mean(xc * xc, axis=-1, keepdims=True)
    return xc * lax.rsqrt(var + EPS) * g.astype(jnp.float32) + b.astype(jnp.float32)

def l2norm(x):
    return x * lax.rsqrt(jnp.sum(x * x, axis=-1, keepdims=True) + EPS)

def causal_dwconv(x, prev, w):
    width, L = w.shape[0], x.shape[1]
    xp = jnp.concatenate([prev.astype(x.dtype), x], axis=1)
    y = xp[:, 0:L] * w[0]
    for i in range(1, width):
        y = y + xp[:, i:i + L] * w[i]
    return y, xp[:, L:]

def gated_delta_rule(q, k, v, beta, g, S0):
    B, L, H, dk = q.shape
    dv = v.shape[-1]
    C = min(GDN_CHUNK, L)
    n = -(-L // C)
    pad = n * C - L

    def to_chunks(t):
        t = jnp.pad(t, [(0, 0), (0, pad)] + [(0, 0)] * (t.ndim - 2))
        return jnp.moveaxis(t.reshape((B, n, C) + t.shape[2:]), 3, 1)

    q, k, v, beta, g = (to_chunks(t) for t in (q * dk ** -0.5, k, v, beta, g))
    gc = jnp.cumsum(g, axis=-1)
    idx = jnp.arange(C)
    tri = idx[:, None] >= idx[None, :]
    strict = idx[:, None] > idx[None, :]
    diff = gc[..., :, None] - gc[..., None, :]
    decay = jnp.where(tri, jnp.exp(jnp.where(tri, diff, 0.0)), 0.0)
    kb = k * beta[..., None]
    lower = jnp.where(strict, jnp.einsum('bhncd,bhnsd->bhncs', kb, k) * decay, 0.0)
    rhs = jnp.concatenate([v * beta[..., None], kb * jnp.exp(gc)[..., None]], axis=-1)
    sol = lax.linalg.triangular_solve(lower + jnp.eye(C, dtype=lower.dtype), rhs, left_side=True, lower=True)
    u, w = sol[..., :dv], sol[..., dv:]
    attn = jnp.einsum('bhncd,bhnsd->bhncs', q, k) * decay
    q_in = q * jnp.exp(gc)[..., None]
    k_out = k * jnp.exp(gc[..., -1:] - gc)[..., None]
    g_last = jnp.exp(gc[..., -1])

    def step(S, xs):
        q_c, k_c, u_c, w_c, a_c, gl = xs
        v_new = u_c - jnp.einsum('bhck,bhkv->bhcv', w_c, S)
        o = jnp.einsum('bhck,bhkv->bhcv', q_c, S) + jnp.einsum('bhcs,bhsv->bhcv', a_c, v_new)
        S = S * gl[..., None, None] + jnp.einsum('bhck,bhcv->bhkv', k_c, v_new)
        return S, o

    xs = tuple(jnp.moveaxis(t, 2, 0) for t in (q_in, k_out, u, w, attn, g_last))
    S, o = lax.scan(step, S0, xs)
    o = jnp.moveaxis(o, 0, 2).reshape(B, H, n * C, dv)
    return jnp.swapaxes(o, 1, 2)[:, :L], S

def chunk_spatial_gate(u, v, w_s, b_s):
    B, L, _ = u.shape
    n = -(-L // CHUNK)
    pad = n * CHUNK - L
    vc = jnp.pad(v, ((0, 0), (0, pad), (0, 0))).reshape(B, n, CHUNK, G_B, HEAD_DIM)
    mix = jnp.einsum('gts,bnsgc->bntgc', jnp.tril(w_s.astype(jnp.float32)), vc)
    mix = mix + jnp.swapaxes(b_s.astype(jnp.float32), 0, 1)[:, :, None]
    return u * mix.reshape(B, n * CHUNK, W_B)[:, :L]

def forgetting_attention(q, k, v, dq, dk, qpos, kpos):
    B, Lq, H, d = q.shape
    QB = min(FOX_QBLOCK, Lq)
    nb = -(-Lq // QB)
    pad = nb * QB - Lq
    qb = jnp.moveaxis(jnp.pad(q, ((0, 0), (0, pad), (0, 0), (0, 0))).reshape(B, nb, QB, H, d), 1, 0)
    dqb = jnp.moveaxis(jnp.pad(dq, ((0, 0), (0, pad), (0, 0))).reshape(B, nb, QB, H), 1, 0)
    pb = jnp.pad(qpos, (0, pad), mode='edge').reshape(nb, QB)
    dk_t = jnp.swapaxes(dk, 1, 2)
    scale = d ** -0.5

    def one_block(args):
        qi, dqi, pi = args
        s = jnp.einsum('bqhd,bkhd->bhqk', qi, k) * scale + jnp.swapaxes(dqi, 1, 2)[..., None] - dk_t[:, :, None, :]
        s = jnp.where(kpos[None, :] <= pi[:, None], s, NEG_INF)
        p = jax.nn.softmax(s, axis=-1)
        return jnp.einsum('bhqk,bkhd->bqhd', p, v)

    o = lax.map(one_block, (qb, dqb, pb))
    return jnp.moveaxis(o, 0, 1).reshape(B, nb * QB, H, d)[:, :Lq]

def block(x, c, l, P, gdn_conv_prev, gdn_S0, fox_past, ffn_conv_prev):
    f32 = jnp.float32
    B, L, _ = x.shape
    mod = (jax.nn.silu(c.astype(f32)) @ P['w_ada'][l].astype(f32) + P['b_ada'][l].astype(f32)).reshape(B, 6, D_MODEL)
    shift1, scale1, gate1, shift2, scale2, gate2 = [mod[:, i, None, :] for i in range(6)]

    h = (rmsnorm(x, P['g_pre_mix'][l]) * (1.0 + scale1) + shift1).astype(x.dtype)
    z = h @ P['w_in'][l]
    offs = [3 * W_A, 3 * W_A + H_A, 3 * W_A + 2 * H_A, 4 * W_A + 2 * H_A,
            4 * W_A + 2 * H_A + 2 * W_B, 4 * W_A + 2 * H_A + 2 * W_B + 3 * W_C]
    qkv_a, beta_raw, a_raw, gate_a, uv_b, qkv_c, f_raw = jnp.split(z, offs, axis=-1)

    qkv_a, gdn_conv_new = causal_dwconv(qkv_a, gdn_conv_prev, P['gdn_conv_w'][l])
    qkv_a = jax.nn.silu(qkv_a.astype(f32))
    qa, ka, va = [t.reshape(B, L, H_A, HEAD_DIM) for t in jnp.split(qkv_a, 3, axis=-1)]
    beta = jax.nn.sigmoid(beta_raw.astype(f32))
    g = -jnp.exp(P['gdn_A_log'][l].astype(f32)) * jax.nn.softplus(a_raw.astype(f32) + P['gdn_dt_bias'][l].astype(f32))
    oa, S_new = gated_delta_rule(l2norm(qa), l2norm(ka), va, beta, g, gdn_S0.astype(f32))
    oa = rmsnorm(oa, P['gdn_norm_g'][l]) * jax.nn.silu(gate_a.astype(f32)).reshape(B, L, H_A, HEAD_DIM)
    oa = oa.reshape(B, L, W_A)

    ub, vb = jnp.split(jax.nn.gelu(uv_b.astype(f32)), 2, axis=-1)
    vb = layernorm(vb, P['chunk_ln_g'][l], P['chunk_ln_b'][l])
    ob = chunk_spatial_gate(ub, vb, P['chunk_w_s'][l], P['chunk_b_s'][l])

    qc, kc, vc = [t.astype(f32).reshape(B, L, H_C, HEAD_DIM) for t in jnp.split(qkv_c, 3, axis=-1)]
    logf = jax.nn.log_sigmoid(f_raw.astype(f32) + P['fox_f_bias'][l].astype(f32))
    if fox_past is None:
        k_all, v_all, lf_all = kc, vc, logf
        kpos = jnp.arange(L)
        qpos = kpos
    else:
        pk, pv, plf = fox_past
        past = pk.shape[1]
        k_all = jnp.concatenate([pk.astype(f32), kc], axis=1)
        v_all = jnp.concatenate([pv.astype(f32), vc], axis=1)
        lf_all = jnp.concatenate([plf.astype(f32), logf], axis=1)
        kpos = jnp.arange(past + L)
        qpos = past + jnp.arange(L)
    d_all = jnp.cumsum(lf_all, axis=1)
    oc = forgetting_attention(qc, k_all, v_all, d_all[:, -L:], d_all, qpos, kpos).reshape(B, L, W_C)

    mixed = jnp.concatenate([oa, ob, oc], axis=-1).astype(x.dtype)
    o = mixed @ P['w_out'][l]
    x = x + (gate1 * rmsnorm(o, P['g_post_mix'][l])).astype(x.dtype)

    h = (rmsnorm(x, P['g_pre_ffn'][l]) * (1.0 + scale2) + shift2).astype(x.dtype)
    up = h @ P['w_up'][l]
    up, ffn_conv_new = causal_dwconv(up, ffn_conv_prev, P['ffn_conv_w'][l])
    a, b = jnp.split(up.astype(f32), 2, axis=-1)
    y = (jax.nn.gelu(a) * b).astype(x.dtype) @ P['w_down'][l]
    x = x + (gate2 * rmsnorm(y, P['g_post_ffn'][l])).astype(x.dtype)
    return x, gdn_conv_new, S_new, kc, vc, logf, vb, ffn_conv_new

def setup_inputs(seed: int = 0) -> dict:
    key = jax.random.key(seed)
    ks = iter(jax.random.split(key, 48))
    f32 = jnp.float32
    n_pages = PAST_LEN // PAGE_SIZE
    n_used = DEC_BATCH * n_pages
    n_pool = n_used + n_used // 4

    def nrm(shape, s=1.0):
        return s * jax.random.normal(next(ks), shape, f32)

    def unif(shape, lo, hi):
        return jax.random.uniform(next(ks), shape, f32, lo, hi)

    x_prompt = nrm((BATCH, SEQ, D_MODEL))
    x_sample = nrm((DEC_BATCH, DEC_SEQ, D_MODEL))
    state_gdn_conv = nrm((DEPTH, DEC_BATCH, GDN_CONV - 1, 3 * W_A))
    state_gdn_S = nrm((DEPTH, DEC_BATCH, H_A, HEAD_DIM, HEAD_DIM), 0.1)
    cache_fox_k = nrm((DEPTH, n_pool, PAGE_SIZE, H_C, HEAD_DIM))
    cache_fox_v = nrm((DEPTH, n_pool, PAGE_SIZE, H_C, HEAD_DIM))
    cache_fox_logf = jax.nn.log_sigmoid(nrm((DEPTH, n_pool, PAGE_SIZE, H_C)) + 2.5)
    state_ffn_conv = nrm((DEPTH, DEC_BATCH, FFN_CONV - 1, 2 * D_FF))
    page_table = jax.random.permutation(next(ks), n_pool)[:n_used].reshape(DEC_BATCH, n_pages).astype(jnp.int32)
    c_prompt = nrm((BATCH, D_MODEL))
    c_sample = nrm((DEC_BATCH, D_MODEL))

    dt = jnp.exp(unif((DEPTH, H_A), float(np.log(1e-3)), float(np.log(1e-1))))
    return {
        'x_prompt': x_prompt,
        'x_sample': x_sample,
        'state_gdn_conv': state_gdn_conv,
        'state_gdn_S': state_gdn_S,
        'cache_fox_k': cache_fox_k,
        'cache_fox_v': cache_fox_v,
        'cache_fox_logf': cache_fox_logf,
        'state_ffn_conv': state_ffn_conv,
        'page_table': page_table,
        'c_prompt': c_prompt,
        'c_sample': c_sample,
        'w_ada': nrm((DEPTH, D_MODEL, 6 * D_MODEL), D_MODEL ** -0.5),
        'b_ada': nrm((DEPTH, 6 * D_MODEL), 0.02),
        'g_pre_mix': 1.0 + nrm((DEPTH, D_MODEL), 0.05),
        'g_post_mix': 1.0 + nrm((DEPTH, D_MODEL), 0.05),
        'g_pre_ffn': 1.0 + nrm((DEPTH, D_MODEL), 0.05),
        'g_post_ffn': 1.0 + nrm((DEPTH, D_MODEL), 0.05),
        'w_in': nrm((DEPTH, D_MODEL, N_IN), D_MODEL ** -0.5),
        'w_out': nrm((DEPTH, MIX_WIDTH, D_MODEL), MIX_WIDTH ** -0.5),
        'gdn_conv_w': nrm((DEPTH, GDN_CONV, 3 * W_A), GDN_CONV ** -0.5),
        'gdn_A_log': jnp.log(unif((DEPTH, H_A), 1.0, 16.0)),
        'gdn_dt_bias': dt + jnp.log(-jnp.expm1(-dt)),
        'gdn_norm_g': 1.0 + nrm((DEPTH, HEAD_DIM), 0.05),
        'chunk_ln_g': 1.0 + nrm((DEPTH, W_B), 0.05),
        'chunk_ln_b': nrm((DEPTH, W_B), 0.02),
        'chunk_w_s': nrm((DEPTH, G_B, CHUNK, CHUNK), CHUNK ** -0.5),
        'chunk_b_s': 1.0 + nrm((DEPTH, G_B, CHUNK), 0.1),
        'fox_f_bias': unif((DEPTH, H_C), 1.0, 4.0),
        'w_up': nrm((DEPTH, D_MODEL, 2 * D_FF), D_MODEL ** -0.5),
        'ffn_conv_w': nrm((DEPTH, FFN_CONV, 2 * D_FF), FFN_CONV ** -0.5),
        'w_down': nrm((DEPTH, D_FF, D_MODEL), D_FF ** -0.5),
    }

def reference(x_prompt, x_sample, state_gdn_conv, state_gdn_S, cache_fox_k, cache_fox_v, cache_fox_logf,
              state_ffn_conv, page_table, c_prompt, c_sample, w_ada, b_ada, g_pre_mix, g_post_mix, g_pre_ffn,
              g_post_ffn, w_in, w_out, gdn_conv_w, gdn_A_log, gdn_dt_bias, gdn_norm_g, chunk_ln_g, chunk_ln_b,
              chunk_w_s, chunk_b_s, fox_f_bias, w_up, ffn_conv_w, w_down):
    P = {'w_ada': w_ada, 'b_ada': b_ada, 'g_pre_mix': g_pre_mix, 'g_post_mix': g_post_mix,
         'g_pre_ffn': g_pre_ffn, 'g_post_ffn': g_post_ffn, 'w_in': w_in, 'w_out': w_out,
         'gdn_conv_w': gdn_conv_w, 'gdn_A_log': gdn_A_log, 'gdn_dt_bias': gdn_dt_bias, 'gdn_norm_g': gdn_norm_g,
         'chunk_ln_g': chunk_ln_g, 'chunk_ln_b': chunk_ln_b, 'chunk_w_s': chunk_w_s, 'chunk_b_s': chunk_b_s,
         'fox_f_bias': fox_f_bias, 'w_up': w_up, 'ffn_conv_w': ffn_conv_w, 'w_down': w_down}
    Bp, Lp, _ = x_prompt.shape
    Bs = x_sample.shape[0]
    n_pages = page_table.shape[1]
    past = n_pages * cache_fox_k.shape[2]

    p_conv, p_S, p_k, p_v, p_lf, p_ffn = [], [], [], [], [], []
    s_conv, s_S, s_k, s_v, s_lf, s_cv, s_ffn = [], [], [], [], [], [], []
    xp, xs = x_prompt, x_sample
    for l in range(DEPTH):
        xp, a_conv, a_S, kc, vc, lf, _, f_conv = block(
            xp, c_prompt, l, P,
            jnp.zeros((Bp, GDN_CONV - 1, 3 * W_A), xp.dtype),
            jnp.zeros((Bp, H_A, HEAD_DIM, HEAD_DIM), jnp.float32),
            None,
            jnp.zeros((Bp, FFN_CONV - 1, 2 * D_FF), xp.dtype))
        p_conv.append(a_conv)
        p_S.append(a_S)
        p_k.append(kc.reshape(Bp, Lp // PAGE_SIZE, PAGE_SIZE, H_C, HEAD_DIM))
        p_v.append(vc.reshape(Bp, Lp // PAGE_SIZE, PAGE_SIZE, H_C, HEAD_DIM))
        p_lf.append(lf.reshape(Bp, Lp // PAGE_SIZE, PAGE_SIZE, H_C))
        p_ffn.append(f_conv)

        pk = cache_fox_k[l][page_table].reshape(Bs, past, H_C, HEAD_DIM)
        pv = cache_fox_v[l][page_table].reshape(Bs, past, H_C, HEAD_DIM)
        plf = cache_fox_logf[l][page_table].reshape(Bs, past, H_C)
        xs, a_conv, a_S, kc, vc, lf, vrows, f_conv = block(
            xs, c_sample, l, P, state_gdn_conv[l], state_gdn_S[l], (pk, pv, plf), state_ffn_conv[l])
        s_conv.append(a_conv)
        s_S.append(a_S)
        s_k.append(kc)
        s_v.append(vc)
        s_lf.append(lf)
        s_cv.append(vrows)
        s_ffn.append(f_conv)

    return (xp, xs,
            jnp.stack(p_conv), jnp.stack(p_S), jnp.stack(p_k), jnp.stack(p_v), jnp.stack(p_lf), jnp.stack(p_ffn),
            jnp.stack(s_conv), jnp.stack(s_S), jnp.stack(s_k), jnp.stack(s_v), jnp.stack(s_lf), jnp.stack(s_cv),
            jnp.stack(s_ffn))


_drawn_inputs = setup_inputs


def setup_inputs(seed=0):
    import zlib

    import numpy as np

    out = dict(_drawn_inputs(seed))
    spreads = {}
    factors = {}
    for name, (base, spread) in spreads.items():
        noise = np.random.default_rng([zlib.crc32(name.encode()), seed]).standard_normal(out[name].shape)
        drawn = base * np.exp(spread * noise) if base else spread * noise
        out[name] = jnp.asarray(drawn.astype(out[name].dtype))
    for name, factor in factors.items():
        out[name] = (out[name] * factor).astype(out[name].dtype)
    return out
```

```python
from contextlib import ExitStack

import concourse.bass as bass
import numpy as np
from concourse import mybir

F32 = mybir.dt.float32
BF16 = mybir.dt.bfloat16
I32 = mybir.dt.int32
ACT = mybir.ActivationFunctionType
ALU = mybir.AluOpType
AX = mybir.AxisListType

P = 128
D = 1024
KD = D // P
SEQ = 1024
NT = SEQ // P
NBATCH = 8
SSEQ = 8
NSAMP = NBATCH * SSEQ
TOK = SEQ + NSAMP
HD = 64
H_A, G_B, H_C = 6, 4, 6
W_A, W_B, W_C = H_A * HD, G_B * HD, H_C * HD
PAIRS = H_A // 2
PAGE = 128
NPAGE = 2
NPOOL = 20
PAST = NPAGE * PAGE
D_FF = 2816
KF = D_FF // P
TAPS_A, TAPS_F = 4, 3
EPS = 1e-6
NSEQ = 1 + NBATCH
NGRP = 6 * D // 512
LEVELS = 7
FT_A = 3 * W_A // P
FT_C = 2 * W_C // P
FT = FT_A + FT_C + 1
TM_COLS = W_A + 2 * W_B + W_C
NEG = -1e30

C_ID = 0
C_MASK = C_ID + P
C_TRI = C_MASK + P
C_LVL = C_TRI + P
C_TRI8 = C_LVL + LEVELS * P
C_HEAD = C_TRI8 + NSAMP
C_PAIR = C_HEAD + H_A * P
C_ROW48 = C_PAIR + PAIRS * P
C_CAUS = C_ROW48 + H_C * SSEQ
C_OWN = C_CAUS + NBATCH * NSAMP
C_PICK = C_OWN + W_C
C_BLK = C_PICK + SSEQ
C_END = C_BLK + NBATCH


def constants():
    c = np.zeros((P, C_END), np.float32)
    c[:, C_MASK:C_MASK + P] = np.where(np.arange(P)[None, :] <= np.arange(P)[:, None], 0.0, NEG)
    i, j = np.arange(P)[:, None], np.arange(P)[None, :]
    c[:, C_ID:C_ID + P] = i == j
    c[:, C_TRI:C_TRI + P] = j >= i
    for n in range(LEVELS):
        s = 1 << n
        c[:, C_LVL + n * P:C_LVL + (n + 1) * P] = ((j // s) % 2 == 1) & (i // s == j // s - 1)
    c[:, C_TRI8:C_TRI8 + NSAMP] = ((j >= i) & (j // SSEQ == i // SSEQ))[:, :NSAMP]
    for q in range(4):
        for h in range(H_A):
            c[32 * q + h, C_HEAD + h * P:C_HEAD + (h + 1) * P] = 1
            o = C_PAIR + (h // 2) * P + (h % 2) * HD
            c[32 * q + h, o:o + HD] = 1
            c[32 * q + h, C_ROW48 + h * SSEQ:C_ROW48 + (h + 1) * SSEQ] = 1
    for h in range(H_C):
        for q in range(SSEQ):
            r = h * SSEQ + q
            caus = np.full((NBATCH, NBATCH, SSEQ), NEG, np.float32)
            for b in range(NBATCH):
                caus[b, b, :q + 1] = 0
            c[r, C_CAUS:C_CAUS + NBATCH * NSAMP] = caus.reshape(-1)
            c[r, C_OWN + h * HD:C_OWN + (h + 1) * HD] = 1
            c[r, C_PICK + q] = 1
    for t in range(NSAMP):
        c[t, C_BLK + t // SSEQ] = 1
    return c


def reset_rows():
    r = np.ones((2 * H_A, TOK), np.float32)
    r[:H_A, 0:SEQ:P] = 0
    r[:, SEQ::SSEQ] = 0
    r[H_A:, 0] = 0
    return r


class Chain:

    def __init__(self, eng, sem, base=0):
        self.eng, self.sem, self.base, self.n = eng, sem, base, 0

    def link(self, ins, K=None):
        self.n += 1
        ins.then_inc(self.sem, 1)
        if K:
            wait_apart(self.eng, K, (self.sem, self.base + self.n))
        else:
            self.eng.wait_ge(self.sem, self.base + self.n)


def wait_apart(eng, K, *waits):
    waits = [(sem, n if isinstance(n, int) else eng.snap(eng.to_reg(n))) for sem, n in waits]
    eng.wait_ge(K.cst_in, 32)
    for sem, n in waits:
        eng.wait_ge(sem, n)


def after(eng, sem, n):
    if not (isinstance(n, int) and n <= 0):
        eng.wait_ge(sem, n)


def stage_semaphores(nc, own):
    taken = []

    def clear():
        nc.clear_and_free_semaphores(taken)
        nc.all_engine_barrier()

    own.callback(clear)

    def sem(name, ahead=0):
        taken.append(nc.alloc_semaphore(name=name))
        if ahead:
            nc.sync.sem_inc(taken[-1], ahead)
        return taken[-1]

    return sem


def flat(ap):
    return ap.rearrange("p a n -> p (a n)")


class Kernel:
    pass


def modulation(nc, ctx, K):
    with ExitStack() as own:
        sem = stage_semaphores(nc, own)
        sb = lambda n, s, d=F32: own.enter_context(nc.sbuf_tensor(n, s, d))
        wa = sb("wa", [P, 2, KD, 512])
        ba = sb("ba", [1, 2, 512])
        ones = sb("mod_ones", [1, NSEQ])
        cT = sb("cT", [P, KD, NSEQ])
        csT = sb("csT", [P, KD, NSEQ])
        mr = sb("mr", [NSEQ, 2, 512])
        modT = sb("modT", [P, 6 * KD, NSEQ])
        ps = [own.enter_context(nc.psum_tensor(f"mod_ps{i}", [P, 512], F32)) for i in range(2)]
        psT = own.enter_context(nc.psum_tensor("mod_psT", [P, 512], F32))
        c_in, c_silu = sem("c_in"), sem("c_silu")
        wa_in = [sem("wa_in0"), sem("wa_in1")]
        mod_mm, mod_out, modT_mm, modT_out = sem("mod_mm"), sem("mod_out"), sem("modT_mm"), sem("modT_out")
        scr_out = [sem("scr_out0"), sem("scr_out1")]
        g_done, ones_set = sem("g_done"), sem("mod_ones_set")
        block = own.enter_context(nc.Block())

        @block.sync
        def _(sp):
            sp.dma_start(cT[:], K.cT).then_inc(c_in, 16)

            def load(g, k):
                sp.dma_start(wa[:, k], K.w_ada[bass.ds(g, 1)].rearrange("a p k n -> (a p) k n")).then_inc(wa_in[k], 16)
                sp.dma_start(ba[:, k], K.b_ada[bass.ds(g, 1)]).then_inc(wa_in[k], 16)

            for k in range(2):
                load(k, k)
            sp.dma_start(K.cst[:], K.cst_d).then_inc(K.cst_in, 16)
            sp.dma_start(K.gpre[:], K.gpre_d).then_inc(K.cst_in, 16)
            with sp.Fori(1, NGRP // 2) as i:
                for k in range(2):
                    sp.wait_ge(mod_mm, 2 * i + k - 1)
                    load(2 * i + k, k)
            sp.dma_start(K.w_tm[:], K.w_tm_d).then_inc(K.w_tm_in, 16)

        @block.gpsimd
        def _(pool):
            pool.memset(ones[:], 1.0).then_inc(ones_set, 1)
            with pool.Fori(0, NGRP // 2) as i:
                for k in range(2):
                    pool.wait_ge(mod_out, 2 * i + k + 1)
                    pool.dma_start(K.scr[:, bass.ds((2 * i + k) * 512, 512)], mr[:, k]).then_inc(scr_out[k], 16)
            for k in range(2):
                pool.wait_ge(scr_out[k], 16 * (NGRP // 2))

        @block.tensor
        def _(pe):
            def project(g, k, first):
                pe.wait_ge(wa_in[k], 16 * (g - k) + 32)
                if not first:
                    pe.wait_ge(mod_out, g - 1)
                for kk in range(KD):
                    pe.matmul(ps[k][0:NSEQ, :], csT[:, kk, :], wa[:, k, kk, :], start=(kk == 0), stop=False)
                pe.matmul(ps[k][0:NSEQ, :], ones[:], ba[:, k, :], start=False, stop=True).then_inc(mod_mm, 1)

            def turn(g, k, first=False):
                wait_apart(pe, K, (mod_out, g + 1), *([] if first else [(modT_out, g)]))
                for c in range(4):
                    last = pe.transpose(psT[:, c * NSEQ:(c + 1) * NSEQ], mr[:, k, c * P:(c + 1) * P],
                                        K.ident[0:NSEQ, 0:NSEQ])
                last.then_inc(modT_mm, 1)

            pe.wait_ge(c_silu, 1)
            pe.wait_ge(ones_set, 1)
            project(0, 0, True)
            project(1, 1, True)
            pe.wait_ge(K.cst_in, 32)
            turn(0, 0, True)
            with pe.Fori(1, NGRP // 2) as i:
                for k in range(2):
                    project(2 * i + k, k, False)
                    turn(2 * i + k - 1, 1 - k)
            turn(NGRP - 1, 1)

        @block.scalar
        def _(act):
            act.wait_ge(c_in, 16)
            act.activation(csT[:], cT[:], ACT.Silu).then_inc(c_silu, 1)

            def evict(g, k, first):
                act.wait_ge(mod_mm, g + 1)
                if not first:
                    act.wait_ge(modT_mm, g - 1)
                    act.wait_ge(scr_out[k], 8 * (g - k))
                act.activation(mr[:, k], ps[k][0:NSEQ, :], ACT.Copy).then_inc(mod_out, 1)

            evict(0, 0, True)
            evict(1, 1, True)
            with act.Fori(1, NGRP // 2) as i:
                for k in range(2):
                    evict(2 * i + k, k, False)

        @block.vector
        def _(dve):
            with dve.Fori(0, NGRP) as g:
                dve.wait_ge(modT_mm, g + 1)
                dve.tensor_copy(modT[:, bass.ds(4 * g, 4), :],
                                psT[:, 0:4 * NSEQ].rearrange("p (c n) -> p c n", c=4)).then_inc(modT_out, 1)
            dve.wait_ge(modT_out, NGRP)
            dve.wait_ge(K.cst_in, 32)
            for n, (shift, scale) in enumerate(((0, 1), (3, 4))):
                dve.scalar_tensor_tensor(
                    K.gain[:, n], modT[:, scale * KD:(scale + 1) * KD, :], 1.0,
                    K.gpre[:, n, :].unsqueeze(2).broadcast_to([P, KD, NSEQ]), ALU.add, ALU.mult).then_inc(g_done, 1)
                dve.tensor_copy(K.shift[:, n], modT[:, shift * KD:(shift + 1) * KD, :]).then_inc(g_done, 1)
            dve.wait_ge(g_done, 4)



def gain_shift(dve, K, n, psx, out, rows):
    if rows == P:
        for k in range(KD):
            last = dve.tensor_scalar(out[:, k, 0:P], psx[:, k, :], K.gain[:, n, k, 0:1], K.shift[:, n, k, 0:1],
                                     ALU.mult, ALU.add)
        return [last]
    steps = []
    for k in range(0, KD, 4):
        o = out[:, k:k + 4, 0:NSAMP].rearrange("p k (b s) -> p k b s", s=SSEQ)
        x = psx[:, k:k + 4, 0:NSAMP].rearrange("p k (b s) -> p k b s", s=SSEQ)
        for kk in range(4):
            g = K.gain[:, n, k + kk, 1:NSEQ].unsqueeze(2).broadcast_to([P, NBATCH, SSEQ])
            steps.append((o[:, kk], x[:, kk], g, ALU.mult))
    for k in range(KD):
        o = out[:, k, 0:NSAMP].rearrange("p (b s) -> p b s", s=SSEQ)
        s = K.shift[:, n, k, 1:NSEQ].unsqueeze(2).broadcast_to([P, NBATCH, SSEQ])
        steps.append((o, o, s, ALU.add))
    return steps


def token_projection(nc, ctx, K):
    with ExitStack() as own:
        sem = stage_semaphores(nc, own)
        sb = lambda n, s, d=F32: own.enter_context(nc.sbuf_tensor(n, s, d))
        xt = sb("tp_x", [P, 2, D])
        junk = sb("tp_junk", [P, D])
        hs = sb("tp_hs", [P, 2, KD, P])
        uv = sb("tp_uv", [P, 2, 2 * W_B])
        ss = sb("tp_ss", [P, 2, 4])
        mhalf = sb("tp_mhalf", [P, 1])
        st = sb("tp_st", [P, 6])
        mv = sb("tp_mv", [P, 4])
        gn = sb("tp_gn", [P, HD])
        lng = sb("tp_lng", [P, W_B])
        lnb = sb("tp_lnb", [P, W_B])
        wsT = sb("tp_wsT", [P, G_B, P])
        wsT8 = sb("tp_wsT8", [NSAMP, G_B, NSAMP])
        bs = sb("tp_bs", [P, 2, G_B])
        psX = own.enter_context(nc.psum_tensor("tp_psX", [P, KD, P], F32))
        psG = own.enter_context(nc.psum_tensor("tp_psG", [P, 512], F32))
        psU = own.enter_context(nc.psum_tensor("tp_psU", [P, 512], F32))
        psV = own.enter_context(nc.psum_tensor("tp_psV", [P, 512], F32))
        psM = own.enter_context(nc.psum_tensor("tp_psM", [P, 512], F32))
        x_in = [sem("x_in0"), sem("x_in1")]
        small_in = sem("tp_small_in")
        sumsq, ms_set, r_set, xn_set, x_turned = sem("sumsq"), sem("ms_set"), sem("r_set"), sem("xn_set"), sem("x_turned")
        h_set, h_chain, h_copied = sem("h_set"), sem("h_chain"), sem("h_copied")
        uv_mm, gate_mm, vc_mm, mix_mm = sem("uv_mm"), sem("gate_mm"), sem("vc_mm"), sem("mix_mm")
        uv_set, gate_set, vc_set = sem("uv_set"), sem("gate_set"), sem("vc_set")
        ln_chain, ln_var, ln_v, ln_r, vln_set, ob_set = (sem("ln_chain"), sem("ln_var"), sem("ln_v"), sem("ln_r"),
                                                         sem("vln_set"), sem("ob_set"))
        half_set, ws_set, v_out, cv_out = sem("half_set"), sem("ws_set"), sem("v_out"), sem("cv_out")
        block = own.enter_context(nc.Block())

        @block.sync
        def _(sp):
            def load(t, k, rows=P):
                sp.dma_start(xt[0:rows, k], K.x[bass.ds(t * P, rows)]).then_inc(x_in[k], 16)

            load(0, 0)
            for dst, src in ((gn[:], K.gn_d.broadcast_to([P, HD])), (lng[:], K.lng_d.broadcast_to([P, W_B])),
                             (lnb[:], K.lnb_d.broadcast_to([P, W_B])), (wsT[:], K.wsT_d), (wsT8[:], K.wsT8_d),
                             (bs[:], K.bs_d)):
                sp.dma_start(dst, src).then_inc(small_in, 16)
            load(1, 1)

            def step(t, k, rows, nxt):
                if nxt:
                    sp.wait_ge(x_turned, t + 1)
                    load(t + 2, k, nxt)
                sp.wait_ge(vc_set, t + 1)
                sp.dma_start(K.v_out[bass.ds(t * P, rows)], K.vc[0:rows, bass.ds(t, 1)].rearrange("p a n -> p (a n)"))\
                    .then_inc(v_out, 16)

            with sp.Fori(0, NT // 2 - 1) as i:
                for k in range(2):
                    step(2 * i + k, k, P, P)
            step(NT - 2, 0, P, NSAMP)
            step(NT - 1, 1, P, 0)
            step(NT, 0, NSAMP, 0)
            sp.wait_ge(vln_set, NT + 1)
            sp.dma_start(K.chunk_v, uv[0:NSAMP, 0, W_B:2 * W_B]).then_inc(cv_out, 16)
            sp.wait_ge(cv_out, 16)
            sp.wait_ge(v_out, 16 * (NT + 1))

        def tiles(eng, stage, step):
            stage(0, 0, P)
            step(0, 0, P, P)
            step(1, 1, P, P)
            with eng.Fori(1, NT // 2 - 1) as i:
                for k in range(2):
                    step(2 * i + k, k, P, P)
            step(NT - 2, 0, P, P)
            step(NT - 1, 1, P, NSAMP)
            step(NT, 0, NSAMP, 0)

        @block.gpsimd
        def _(pool):
            pool.memset(mhalf[:], -0.5).then_inc(half_set, 1)
            pool.wait_ge(small_in, 96)
            pool.tensor_tensor(wsT[:], wsT[:], K.tri.unsqueeze(1).broadcast_to([P, G_B, P]), ALU.mult).then_inc(ws_set, 1)
            pool.tensor_tensor(wsT8[:], wsT8[:], K.tri8.unsqueeze(1).broadcast_to([NSAMP, G_B, NSAMP]), ALU.mult)\
                .then_inc(ws_set, 1)
            pool.wait_ge(half_set, 1)

            def stage(t, k, rows):
                wait_apart(pool, K, (sumsq, t + 1))
                pool.tensor_scalar(ss[0:rows, k, 1:2], ss[0:rows, k, 0:1], 1.0 / D, EPS, ALU.mult, ALU.add).then_inc(ms_set, 1)
                pool.wait_ge(ms_set, t + 1)
                pool.tensor_tensor(ss[0:rows, k, 2:3], ss[0:rows, k, 1:2], mhalf[0:rows], ALU.pow).then_inc(r_set, 1)

            def copy_h(t, k, rows):
                pool.wait_ge(h_set, t + 1)
                pool.tensor_copy(K.hT[:, :, bass.ds(t * P, rows)], hs[:, k, :, 0:rows]).then_inc(h_copied, 1)

            def step(t, k, rows, nxt):
                if nxt:
                    stage(t + 1, 1 - k, nxt)
                wait_apart(pool, K, (ln_var, t + 1))
                pool.tensor_scalar(mv[0:rows, 2:3], mv[0:rows, 1:2], EPS, None, ALU.add).then_inc(ln_v, 1)
                pool.wait_ge(ln_v, t + 1)
                pool.tensor_tensor(mv[0:rows, 3:4], mv[0:rows, 2:3], mhalf[0:rows], ALU.pow).then_inc(ln_r, 1)
                copy_h(t, k, rows)

            tiles(pool, stage, step)

        @block.scalar
        def _(act):
            def stage(t, k, rows):
                act.wait_ge(x_in[k], 8 * (t - k) + 16)
                act.activation(junk[0:rows], xt[0:rows, k], ACT.Square, accum_out=ss[0:rows, k, 0:1]).then_inc(sumsq, 1)
                act.wait_ge(r_set, t + 1)
                act.activation(xt[0:rows, k], xt[0:rows, k], ACT.Copy, scale=ss[0:rows, k, 2:3]).then_inc(xn_set, 1)

            def step(t, k, rows, nxt):
                if nxt:
                    stage(t + 1, 1 - k, nxt)
                act.wait_ge(uv_mm, t + 1)
                after(act, ob_set, t - 1)
                act.activation(uv[0:rows, k], psU[0:rows, :], ACT.Gelu_apprx_tanh).then_inc(uv_set, 1)
                act.wait_ge(gate_mm, t + 1)
                act.activation(K.tok[0:rows, bass.ds(t, 1), 0:W_A].rearrange("p a n -> p (a n)"), psG[0:rows, 0:W_A],
                               ACT.Silu).then_inc(gate_set, 1)
                act.wait_ge(vc_mm, t + 1)
                act.activation(K.vc[0:rows, bass.ds(t, 1)].rearrange("p a n -> p (a n)"), psV[0:rows, 0:W_C],
                               ACT.Copy).then_inc(vc_set, 1)

            tiles(act, stage, step)

        @block.vector
        def _(dve):
            def stage(t, k, rows):
                dve.wait_ge(x_turned, t + 1)
                after(dve, vc_mm, t - 1)
                after(dve, h_copied, t - 1)
                made = gain_shift(dve, K, 0, psX, hs[:, k], rows)
                if rows == P:
                    made[0].then_inc(h_set, 1)
                else:
                    chain = Chain(dve, h_chain)
                    half = len(made) // 2
                    for n, (o, a, b, op) in enumerate(made):
                        ins = dve.tensor_tensor(o, a, b, op)
                        if n == half - 1:
                            chain.link(ins)
                    ins.then_inc(h_set, 1)

            def step(t, k, rows, nxt):
                if nxt:
                    stage(t + 1, 1 - k, nxt)
                chain = Chain(dve, ln_chain, t * 4)
                v = uv[0:rows, k, W_B:2 * W_B]
                dve.wait_ge(uv_set, t + 1)
                chain.link(dve.bn_stats(st[0:rows], v), K)
                dve.bn_aggr(mv[0:rows, 0:2], st[0:rows]).then_inc(ln_var, 1)
                gate = K.tok[0:rows, bass.ds(t, 1), 0:W_A].rearrange("p a (h d) -> p (a h) d", d=HD)
                dve.wait_ge(gate_set, t + 1)
                dve.tensor_tensor(gate, gate, gn[0:rows].unsqueeze(1).broadcast_to([rows, H_A, HD]), ALU.mult)
                dve.wait_ge(ln_r, t + 1)
                chain.link(dve.tensor_scalar(v, v, mv[0:rows, 0:1], mv[0:rows, 3:4], ALU.subtract, ALU.mult))
                chain.link(dve.tensor_tensor(v, v, lng[0:rows], ALU.mult))
                dve.tensor_tensor(v, v, lnb[0:rows], ALU.add).then_inc(vln_set, 1)
                ob = K.tok[0:rows, bass.ds(t, 1), W_A:W_A + W_B].rearrange("p a n -> p (a n)")
                b = bs[0:rows, 0 if rows == P else 1, :].unsqueeze(2).broadcast_to([rows, G_B, HD])
                dve.wait_ge(mix_mm, t + 1)
                chain.link(dve.tensor_tensor(ob.rearrange("p (g d) -> p g d", g=G_B),
                                             psM[0:rows, 0:W_B].rearrange("p (g d) -> p g d", g=G_B), b, ALU.add))
                dve.tensor_tensor(ob, ob, uv[0:rows, k, 0:W_B], ALU.mult).then_inc(ob_set, 1)

            dve.wait_ge(small_in, 96)
            tiles(dve, stage, step)

        @block.tensor
        def _(pe):
            def stage(t, k, rows):
                pe.wait_ge(xn_set, t + 1)
                after(pe, h_set, t)
                for kk in range(KD):
                    last = pe.transpose(psX[:, kk, 0:rows], xt[0:rows, k, kk * P:(kk + 1) * P],
                                        K.ident[0:rows, 0:rows])
                last.then_inc(x_turned, 1)

            def gemm(ps, k, rows, c0, n, sem_):
                for kk in range(KD):
                    last = pe.matmul(ps[0:rows, 0:n], hs[:, k, kk, 0:rows], K.w_tm[:, kk, c0:c0 + n],
                                     start=(kk == 0), stop=(kk == KD - 1))
                last.then_inc(sem_, 1)

            def step(t, k, rows, nxt):
                pe.wait_ge(h_set, t + 1)
                after(pe, uv_set, t)
                gemm(psU, k, rows, W_A, 2 * W_B, uv_mm)
                if nxt:
                    stage(t + 1, 1 - k, nxt)
                after(pe, gate_set, t)
                gemm(psG, k, rows, 0, W_A, gate_mm)
                after(pe, vc_set, t)
                gemm(psV, k, rows, W_A + 2 * W_B, W_C, vc_mm)
                pe.wait_ge(vln_set, t + 1)
                after(pe, ob_set, t)
                for g in range(G_B):
                    w = wsT[:, g, :] if rows == P else wsT8[:, g, :]
                    last = pe.matmul(psM[0:rows, g * HD:(g + 1) * HD], w,
                                     uv[0:rows, k, W_B + g * HD:W_B + (g + 1) * HD], start=True, stop=True)
                last.then_inc(mix_mm, 1)

            pe.wait_ge(K.w_tm_in, 16)
            pe.wait_ge(ws_set, 2)
            tiles(pe, stage, step)


def feature_projection(nc, ctx, K):
    with ExitStack() as own:
        sem = stage_semaphores(nc, own)
        sb = lambda n, s, d=F32: own.enter_context(nc.sbuf_tensor(n, s, d))
        RING = 4
        wf = sb("fp_w", [P, RING, KD, P])
        zp = sb("fp_zp", [P, 2, TAPS_A - 1 + SEQ])
        zs = sb("fp_zs", [P, 2, NBATCH, TAPS_A - 1 + SSEQ])
        prev = sb("fp_prev", [P, FT_A, NBATCH, TAPS_A - 1])
        cw = sb("fp_cw", [P, FT_A, TAPS_A])
        pst = sb("fp_pst", [P, FT_A, TAPS_A - 1])
        sst = sb("fp_sst", [P, FT_A, NBATCH, TAPS_A - 1])
        bias = sb("fp_bias", [P, 2])
        nexpA = sb("fp_nexpA", [P, 1])
        reset = sb("fp_reset", [P, TOK])
        rowx = sb("fp_rowx", [P, TOK])
        rowe = sb("fp_rowe", [P, TOK])
        logf = sb("fp_logf", [P, TOK])
        ps = [own.enter_context(nc.psum_tensor(f"fp_ps{i}", [P, 3, 512], F32)) for i in range(2)]
        psR = own.enter_context(nc.psum_tensor("fp_psR", [P, 512], F32))
        w_in = [sem(f"fp_w_in{k}") for k in range(RING)]
        small_in, fm_mm, fm_out, halo_set = sem("fp_small_in"), sem("fm_mm"), sem("fm_out"), sem("halo_set")
        conv_chain, conv_set, silu_set, st_copied, st_out = (sem("conv_chain"), sem("conv_set"), sem("silu_set"),
                                                             sem("st_copied"), sem("st_out"))
        zero_set, row_act, row_dve, row_mm, row_tm, fin = (sem("zero_set"), sem("row_act"), sem("row_dve"), sem("row_mm"),
                                                           sem("row_tm"), sem("fp_fin"))
        k_out = sem("k_out")
        block = own.enter_context(nc.Block())

        @block.sync
        def _(sp):
            for k in range(RING):
                sp.dma_start(wf[:, k], K.w_fm_d[k]).then_inc(w_in[k], 16)
            for dst, src in ((prev[:], K.gprev_d), (cw[:], K.gconv_d), (bias[:], K.bias_d), (reset[32:32 + H_A], K.reset_d[0:H_A]),
                             (reset[64:64 + H_A], K.reset_d[H_A:])):
                sp.dma_start(dst, src).then_inc(small_in, 16)
            with sp.Fori(1, FT // RING) as i:
                for k in range(RING):
                    sp.wait_ge(fm_mm, RING * (i - 1) + k + 1)
                    sp.dma_start(wf[:, k], K.w_fm_d[bass.ds(RING * i + k, 1)].rearrange("a p k n -> (a p) k n"))\
                        .then_inc(w_in[k], 16)
            sp.wait_ge(st_copied, 2 * FT_A)
            sp.dma_start(K.p_gconv, pst[:]).then_inc(st_out, 16)
            sp.dma_start(K.s_gconv, sst[:]).then_inc(st_out, 16)
            sp.wait_ge(fm_out, FT - 1)
            sp.dma_start(K.k_out, K.qkc[:, PAIRS:2 * PAIRS]).then_inc(k_out, 16)
            sp.wait_ge(row_dve, 9)
            sp.dma_start(K.logf_out, logf[64:64 + H_C]).then_inc(k_out, 16)
            sp.wait_ge(st_out, 32)
            sp.wait_ge(k_out, 32)

        @block.tensor
        def _(pe):
            def tile(i, slot, turn):
                pe.wait_ge(w_in[slot], 4 * (i - slot) + 16)
                after(pe, fm_out, i - 1)
                for kk in range(KD):
                    for n, (c, w) in enumerate(((0, 512), (512, 512), (SEQ, NSAMP))):
                        last = pe.matmul(ps[turn][:, n, 0:w], wf[:, slot, kk, :], K.hT[:, kk, c:c + w],
                                         start=(kk == 0), stop=(kk == KD - 1))
                last.then_inc(fm_mm, 1)

            for i in range(RING):
                tile(i, i, i % 2)
            with pe.Fori(1, FT // RING) as i:
                for k in range(RING):
                    tile(RING * i + k, k, k % 2)
            pe.wait_ge(row_dve, 9)
            for t in range(NT + 1):
                n = P if t < NT else NSAMP
                after(pe, row_tm, t)
                pe.transpose(psR[0:n, 0:P], K.rows[:, t * P:t * P + n], K.ident).then_inc(row_mm, 1)
            pe.wait_ge(row_tm, NT + 1)
            for j in range(PAIRS):
                w = K.cst[32:32 + H_A, C_PAIR + j * P:C_PAIR + (j + 1) * P]
                pe.matmul(psR[:, 16 * j:16 * j + NT], w, K.rows[32:32 + H_A, P - 1:SEQ:P], start=True, stop=True)
                last = pe.matmul(psR[:, 16 * j + 8:16 * j + 16], w, K.rows[32:32 + H_A, SEQ + SSEQ - 1:TOK:SSEQ],
                                 start=True, stop=True)
            last.then_inc(row_mm, 1)

        @block.gpsimd
        def _(pool):
            for k in range(2):
                pool.memset(zp[:, k, 0:TAPS_A - 1], 0.0).then_inc(zero_set, 1)
            pool.wait_ge(zero_set, 2)
            pool.memset(K.tm[NSAMP:P, NT], 0.0).then_inc(zero_set, 1)
            pool.wait_ge(zero_set, 3)
            pool.wait_ge(small_in, 80)

            def tile(i, k):
                after(pool, conv_set, i - 1)
                pool.tensor_copy(zs[:, k, :, 0:TAPS_A - 1], prev[:, bass.ds(i, 1)].rearrange("p a b n -> p (a b) n"))\
                    .then_inc(halo_set, 1)
                pool.wait_ge(fm_out, i + 1)
                pool.tensor_copy(flat(pst[:, bass.ds(i, 1)]), zp[:, k, SEQ:SEQ + TAPS_A - 1]).then_inc(st_copied, 1)
                pool.tensor_copy(sst[:, bass.ds(i, 1)].rearrange("p a b n -> p (a b) n"), zs[:, k, :, SSEQ:])\
                    .then_inc(st_copied, 1)

            tile(0, 0)
            tile(1, 1)
            with pool.Fori(1, FT_A // 2) as i:
                for k in range(2):
                    tile(2 * i + k, k)
            tile(FT_A - 1, 0)

        @block.scalar
        def _(act):
            act.wait_ge(zero_set, 3)

            def evict(i, k):
                act.wait_ge(fm_mm, i + 1)
                after(act, conv_set, i - 1)
                after(act, st_copied, 2 * (i - 1))
                act.activation(zp[:, k, TAPS_A - 1:], ps[k][:, 0:2, :].rearrange("p a n -> p (a n)"), ACT.Copy)
                act.activation(zs[:, k, :, TAPS_A - 1:], ps[k][:, 2, 0:NSAMP].rearrange("p (b s) -> p b s", s=SSEQ),
                               ACT.Copy).then_inc(fm_out, 1)

            def silu(i):
                act.wait_ge(conv_set, i + 1)
                act.activation(flat(K.qkv[:, bass.ds(i, 1)]), flat(K.qkv[:, bass.ds(i, 1)]), ACT.Silu).then_inc(silu_set, 1)

            act.wait_ge(small_in, 80)
            evict(0, 0)
            evict(1, 1)
            silu(0)
            with act.Fori(1, FT_A // 2) as i:
                for k in range(2):
                    evict(2 * i + k, k)
                    silu(2 * i + k - 1)
            evict(FT_A - 1, 0)
            silu(FT_A - 2)
            silu(FT_A - 1)
            for c in range(FT_C):
                i = FT_A + c
                act.wait_ge(fm_mm, i + 1)
                scale = HD ** -0.5 if c < PAIRS else 1.0
                act.activation(K.qkc[:, c, 0:SEQ], ps[i % 2][:, 0:2, :].rearrange("p a n -> p (a n)"), ACT.Copy, scale=scale)
                act.activation(K.qkc[:, c, SEQ:TOK], ps[i % 2][:, 2, 0:NSAMP], ACT.Copy, scale=scale).then_inc(fm_out, 1)
            i = FT - 1
            act.wait_ge(fm_mm, i + 1)
            act.wait_ge(fm_out, FT - 1)
            chain = Chain(act, row_act)
            x, e = rowx[:], rowe[:]
            p2 = ps[i % 2][:, 0:2, :].rearrange("p a n -> p (a n)")
            act.activation(K.rows[0:32, 0:SEQ], p2[0:32], ACT.Sigmoid)
            act.activation(K.rows[0:32, SEQ:TOK], ps[i % 2][0:32, 2, 0:NSAMP], ACT.Sigmoid)
            act.activation(x[:, 0:SEQ], p2, ACT.Identity, bias=bias[:, 0:1])
            chain.link(act.activation(x[:, SEQ:TOK], ps[i % 2][:, 2, 0:NSAMP], ACT.Identity, bias=bias[:, 0:1]))
            chain.link(act.activation(e, x, ACT.Abs))
            chain.link(act.activation(e, e, ACT.Exp, scale=-1.0))
            act.activation(nexpA[32:64], bias[32:64, 1:2], ACT.Exp)
            chain.link(act.activation(e, e, ACT.Ln, bias=1.0))
            act.wait_ge(row_tm, NT + 1)
            act.activation(K.ec[:, 0], K.tm[:, :, 1, :], ACT.Exp)
            act.activation(K.ec[:, 1], K.tm[:, :, 3, :], ACT.Exp)
            act.wait_ge(row_mm, NT + 2)
            act.activation(K.gl[:], psR[:, 0:PAIRS * 16].rearrange("p (j n) -> p j n", j=PAIRS), ACT.Exp).then_inc(fin, 1)

        @block.vector
        def _(dve):
            dve.wait_ge(small_in, 80)

            def conv(i, k):
                chain = Chain(dve, conv_chain, i * 6)
                yp = flat(K.qkv[:, bass.ds(i, 1), 0:SEQ])
                ys = K.qkv[:, bass.ds(i, 1), SEQ:TOK].rearrange("p a (b s) -> p (a b) s", s=SSEQ)
                dve.wait_ge(fm_out, i + 1)
                dve.wait_ge(halo_set, i + 1)
                for tap in range(TAPS_A):
                    w = flat(cw[:, bass.ds(i, 1), tap:tap + 1])
                    a, b = zp[:, k, tap:tap + SEQ], zs[:, k, :, tap:tap + SSEQ]
                    if tap == 0:
                        one = dve.tensor_scalar(yp, a, w, None, ALU.mult)
                        two = dve.tensor_scalar(ys, b, w, None, ALU.mult)
                    else:
                        one = dve.scalar_tensor_tensor(yp, a, w, yp, ALU.mult, ALU.add)
                        two = dve.scalar_tensor_tensor(ys, b, w, ys, ALU.mult, ALU.add)
                    if tap < TAPS_A - 1:
                        one.then_inc(conv_chain, 1)
                        chain.n += 1
                        chain.link(two)
                two.then_inc(conv_set, 1)

            conv(0, 0)
            conv(1, 1)
            with dve.Fori(1, FT_A // 2) as i:
                for k in range(2):
                    conv(2 * i + k, k)
            conv(FT_A - 1, 0)
            chain = Chain(dve, row_dve)
            x, e = rowx[:], rowe[:]
            r = slice(32, 32 + H_A)
            f = slice(64, 64 + H_C)
            dve.wait_ge(row_act, 4)
            dve.memset(K.rows[96:128, :], 0.0)
            chain.link(dve.scalar_tensor_tensor(K.rows[32:64, :], x[32:64], 0.0, e[32:64], ALU.max, ALU.add))
            chain.link(dve.scalar_tensor_tensor(logf[64:96], x[64:96], 0.0, e[64:96], ALU.min, ALU.subtract))
            chain.link(dve.tensor_scalar(K.rows[32:64, :], K.rows[32:64, :], nexpA[32:64], -1.0, ALU.mult, ALU.mult))
            chain.link(dve.tensor_scalar(K.rows[64:96, :], logf[64:96], -1.0, None, ALU.mult))
            chain.link(dve.tensor_copy(x[32:32 + H_A], K.rows[r, :]))
            chain.link(dve.tensor_copy(x[64:64 + H_C], K.rows[f, :]))
            chain.link(dve.tensor_tensor_scan(K.rows[r, :], reset[r], x[r], 0.0, ALU.mult, ALU.add))
            chain.link(dve.tensor_tensor_scan(K.rows[f, :], reset[f], x[f], 0.0, ALU.mult, ALU.add))
            g = K.rows[r, 0:SEQ].rearrange("p (t n) -> p t n", n=P)
            dve.tensor_tensor(K.rows[96:96 + H_A, 0:SEQ].rearrange("p (t n) -> p t n", n=P),
                              g[:, :, P - 1:P].broadcast_to([H_A, NT, P]), g, ALU.subtract)
            g = K.rows[r, SEQ:TOK].rearrange("p (t n) -> p t n", n=SSEQ)
            chain.link(dve.tensor_tensor(K.rows[96:96 + H_A, SEQ:TOK].rearrange("p (t n) -> p t n", n=SSEQ),
                                         g[:, :, SSEQ - 1:SSEQ].broadcast_to([H_A, NBATCH, SSEQ]), g, ALU.subtract))
            for t in range(NT + 1):
                n = P if t < NT else NSAMP
                dve.wait_ge(row_mm, t + 1)
                dve.tensor_copy(K.tm[0:n, t], psR[0:n, 0:P].rearrange("p (q h) -> p q h", q=4)[:, :, 0:H_A])\
                    .then_inc(row_tm, 1)


def forgetting_attention(nc, ctx, K):
    with ExitStack() as own:
        sem = stage_semaphores(nc, own)
        sb = lambda n, s, d=F32: own.enter_context(nc.sbuf_tensor(n, s, d))
        U = 2 * NT
        FAR = NT - 4
        qs = sb("fa_q", [P, SEQ])
        ks = sb("fa_k", [P, SEQ])
        sel = sb("fa_sel", [H_C, 2, P])
        nb = sb("fa_nb", [P, 2, SEQ])
        pb = sb("fa_p", [P, 2, SEQ])
        pt = sb("fa_pt", [P, 2, NT, P])
        st = sb("fa_st", [P, 4, 4])
        ost = sb("fa_o", [P, 2, P])
        c16 = sb("fa_c16", [P, 2 * P], BF16)
        psS = [own.enter_context(nc.psum_tensor(f"fa_psS{i}", [P, SEQ], F32)) for i in range(2)]
        psT = own.enter_context(nc.psum_tensor("fa_psT", [P, NT, P], F32))
        psO = own.enter_context(nc.psum_tensor("fa_psO", [P, 512], F32))
        psOT = own.enter_context(nc.psum_tensor("fa_psOT", [P, 512], F32))
        staged, nb_mm, nb_set, s_mm, p_set = (sem("fa_" + n) for n in "staged nb_mm nb_set s_mm p_set".split())
        max_set, t_mm, near_set, far_set, pv_mm, o_set, ot_mm, ot_set = (
            sem("fa_" + n, 1) for n in "max_set t_mm near_set far_set pv_mm o_set ot_mm ot_set".split())
        at_chain, nd_set = sem("at_chain"), sem("nd_set")
        block = own.enter_context(nc.Block())

        @block.gpsimd
        def _(pool):
            def stage(j):
                after(pool, s_mm, j * U)
                pool.tensor_copy(sel[:], K.cst[0:H_C, bass.ds(j * 2 * P + C_HEAD, 2 * P)].rearrange("p (a n) -> p a n", a=2))
                pool.tensor_copy(qs[:], flat(K.qkc[:, bass.ds(j, 1), 0:SEQ]))
                pool.tensor_copy(ks[:], flat(K.qkc[:, bass.ds(j + PAIRS, 1), 0:SEQ])).then_inc(staged, 1)

            stage(0)
            with pool.Fori(1, PAIRS) as j:
                stage(j)

        @block.tensor
        def _(pe):
            pe.wait_ge(nd_set, 1)
            with pe.Fori(0, PAIRS) as j:
                pe.wait_ge(staged, j + 1)
                pe.wait_ge(max_set, U * j + 1)
                for hh in range(2):
                    for c in range(0, SEQ, 512):
                        last = pe.matmul(psS[hh][:, c:c + 512], sel[:, hh, :], K.nd[:, c:c + 512], start=True, stop=True)
                    last.then_inc(nb_mm, 1)

                def scores(u):
                    i, hh = u // 2, u % 2
                    r = slice(hh * HD, (hh + 1) * HD)
                    if u < 2:
                        pe.wait_ge(nb_set, 2 * j + hh + 1)
                    else:
                        pe.wait_ge(max_set, U * j + u)
                    n = (i + 1) * P
                    for c in range(0, n, 512):
                        w = min(512, n - c)
                        pe.matmul(psS[hh][:, c:c + w], qs[r, i * P:(i + 1) * P], ks[r, c:c + w], start=True,
                                  stop=(c + w < n))
                    pe.matmul(psS[hh][:, i * P:n], c16[:, 0:P], c16[:, P:2 * P], start=False, stop=True)\
                        .then_inc(s_mm, 1)

                def turn(u):
                    i = u // 2
                    pe.wait_ge(p_set, U * j + u + 1)
                    pe.wait_ge(near_set, U * j + u + 1)
                    if i >= 4:
                        pe.wait_ge(far_set, 2 * FAR * j + u - 7)
                    for b in range(i + 1):
                        last = pe.transpose(psT[:, b, :], pb[:, u % 2, b * P:(b + 1) * P], K.ident)
                    last.then_inc(t_mm, 1)

                def values(u):
                    i, hh = u // 2, u % 2
                    pe.wait_ge(near_set, U * j + u + 2)
                    if i >= 4:
                        pe.wait_ge(far_set, 2 * FAR * j + u - 6)
                    pe.wait_ge(o_set, U * j + u + 1)
                    for b in range(i + 1):
                        last = pe.matmul(psO[:, 0:HD], pt[:, u % 2, b, :],
                                         K.vc[:, b, bass.ds(j * P + hh * HD, HD)], start=(b == 0), stop=(b == i))
                    last.then_inc(pv_mm, 1)
                    if hh:
                        pe.wait_ge(o_set, U * j + u + 2)
                        pe.wait_ge(ot_set, NT * j + i + 1)
                        pe.transpose(psOT[:, 0:P], ost[:, i % 2, :], K.ident).then_inc(ot_mm, 1)

                scores(0)
                for u in range(U):
                    if u + 1 < U:
                        scores(u + 1)
                    turn(u)
                    if u:
                        values(u - 1)
                values(U - 1)

        @block.scalar
        def _(act):
            with act.Fori(0, PAIRS) as j:
                for hh in range(2):
                    act.wait_ge(nb_mm, 2 * j + hh + 1)
                    act.activation(nb[:, hh], psS[hh][:], ACT.Copy).then_inc(nb_set, 1)

                def out(i):
                    act.wait_ge(ot_mm, NT * j + i + 2)
                    act.activation(flat(K.hT[:, bass.ds(j + 5, 1), i * P:(i + 1) * P]), psOT[:, 0:P], ACT.Copy)\
                        .then_inc(ot_set, 1)

                for u in range(U):
                    i = u // 2
                    n = (i + 1) * P
                    act.wait_ge(max_set, U * j + u + 2)
                    p = pb[:, u % 2, 0:n]
                    act.activation(p, p, ACT.Exp, bias=st[:, u % 4, 1:2], accum_out=st[:, u % 4, 2:3]).then_inc(p_set, 1)
                    act.wait_ge(t_mm, U * j + u + 2)
                    if u < 2:
                        act.wait_ge(pv_mm, U * j + 1)
                    else:
                        act.wait_ge(pv_mm, U * j + u)
                    b = min(i + 1, 4)
                    act.activation(pt[:, u % 2, 0:b, :], psT[:, 0:b, :], ACT.Copy).then_inc(near_set, 1)
                    if u % 2 == 1 and u > 1:
                        out(i - 1)
                out(NT - 1)

        @block.vector
        def _(dve):
            dve.tensor_copy(c16[:], K.cst[:, C_ID:C_ID + 2 * P])
            dve.tensor_copy(K.nd[:], K.rows[64:64 + H_C, :]).then_inc(nd_set, 1)
            with dve.Fori(0, PAIRS) as j:
                chain = Chain(dve, at_chain, j * (2 * U))

                def maximum(u):
                    i, hh = u // 2, u % 2
                    n = (i + 1) * P
                    wait_apart(dve, K, (s_mm, U * j + u + 1), (t_mm, U * j + max(0, u - 1) + 1),
                               *([(nb_set, 2 * j + hh + 1)] if u < 2 else []))
                    chain.link(dve.tensor_tensor_reduce(pb[:, u % 2, 0:n], psS[hh][:, 0:n], nb[:, hh, 0:n], 1.0, -3e38,
                                                        ALU.add, ALU.max, st[:, u % 4, 0:1]))
                    dve.tensor_scalar(st[:, u % 4, 1:2], st[:, u % 4, 0:1], -1.0, None, ALU.mult).then_inc(max_set, 1)

                def far(u):
                    i = u // 2
                    if i >= 4:
                        dve.wait_ge(t_mm, U * j + u + 2)
                        dve.wait_ge(pv_mm, U * j + u)
                        dve.tensor_copy(pt[:, u % 2, 4:i + 1, :], psT[:, 4:i + 1, :]).then_inc(far_set, 1)

                def output(u):
                    i, hh = u // 2, u % 2
                    dve.wait_ge(p_set, U * j + u + 1)
                    chain.link(dve.reciprocal(st[:, u % 4, 3:4], st[:, u % 4, 2:3]))
                    dve.wait_ge(pv_mm, U * j + u + 2)
                    if hh == 0 and i >= 2:
                        dve.wait_ge(ot_mm, NT * j + i)
                    elif hh == 0:
                        dve.wait_ge(ot_mm, NT * j + 1)
                    dve.tensor_scalar(ost[:, i % 2, hh * HD:(hh + 1) * HD], psO[:, 0:HD], st[:, u % 4, 3:4], None, ALU.mult)\
                        .then_inc(o_set, 1)

                maximum(0)
                for u in range(U):
                    if u + 1 < U:
                        maximum(u + 1)
                    far(u)
                    if u:
                        output(u - 1)
                output(U - 1)


def cached_attention(nc, ctx, K):
    with ExitStack() as own:
        sem = stage_semaphores(nc, own)
        sb = lambda n, s, d=F32: own.enter_context(nc.sbuf_tensor(n, s, d))
        R = H_C * SSEQ
        KEYS = PAST + NSAMP
        table = sb("ca_table", [1, NBATCH * NPAGE], I32)
        kp = sb("ca_k", [P, 2, PAIRS, PAST])
        vp = sb("ca_v", [P, 2, NPAGE, W_C])
        lf = sb("ca_lf", [H_C, 2, PAST])
        one = sb("ca_one", [H_C, PAST])
        dn = sb("ca_dn", [H_C, 2, KEYS])
        qb = sb("ca_q", [P, 2, PAIRS, R])
        mk = sb("ca_mk", [R, 2, KEYS])
        pb = sb("ca_p", [R, 2, KEYS])
        pt = sb("ca_pt", [P, 2, 3, R])
        om = sb("ca_om", [R, 2, W_C])
        st = sb("ca_st", [R, 2, 4])
        psS = [own.enter_context(nc.psum_tensor(f"ca_psS{i}", [P, 512], F32)) for i in range(2)]
        psT = [own.enter_context(nc.psum_tensor(f"ca_psT{i}", [P, 512], F32)) for i in range(2)]
        psV = [own.enter_context(nc.psum_tensor(f"ca_psV{i}", [P, 512], F32)) for i in range(2)]
        psO = [own.enter_context(nc.psum_tensor(f"ca_psO{i}", [P, 512], F32)) for i in range(2)]
        table_in, halves = sem("table_in"), sem("halves")
        page_in = [sem("page_in0"), sem("page_in1")]
        clear, clear_d, q_set, d_set, ca_exp, ca_norm, ca_chain = (
            sem("ca_" + n) for n in "clear clear_d q_set d_set exp norm chain".split())
        ca_s, ca_p, ca_t, ca_pt, ca_v, ca_om, ca_o, ca_out = (
            sem("ca_" + n, 1) for n in "s p t pt v om o out".split())
        block = own.enter_context(nc.Block())

        @block.sync
        def _(sp):
            sp.dma_start(table[:], K.page_table).then_inc(table_in, 16)
            sp.wait_ge(table_in, 16)

            def load(b, k):
                after(sp, ca_v, b)
                for pg in range(NPAGE):
                    v = sp.value_load(table[0:1, bass.ds(b * NPAGE + pg, 1)], min_val=0, max_val=NPOOL - 1)
                    rows = slice(pg * PAGE, (pg + 1) * PAGE)
                    sp.dma_start(kp[:, k, :, rows], K.ckT[bass.ds(v, 1)].rearrange("a p j n -> (a p) j n")).then_inc(page_in[k], 16)
                    sp.dma_start(vp[:, k, pg, :], K.cv[bass.ds(v, 1)].rearrange("a p n -> (a p) n")).then_inc(page_in[k], 16)
                    sp.dma_start(lf[:, k, rows], K.clf[bass.ds(v, 1)].rearrange("a p n -> (a p) n")).then_inc(page_in[k], 16)

            load(0, 0)
            load(1, 1)
            with sp.Fori(1, NBATCH // 2) as i:
                for k in range(2):
                    load(2 * i + k, k)

        LOADS = 3 * NPAGE * 16

        @block.gpsimd
        def _(pool):
            pool.memset(qb[:], 0.0)
            pool.memset(mk[:], 0.0).then_inc(clear, 1)
            pool.wait_ge(clear, 1)

            def stage(b, k):
                after(pool, ca_s, b)
                after(pool, ca_p, b)
                for e in range(2):
                    r = slice(e * HD, (e + 1) * HD)
                    for j in range(PAIRS):
                        h = 2 * j + e
                        last = pool.tensor_copy(qb[r, k, j, h * SSEQ:(h + 1) * SSEQ],
                                                K.qkc[r, j, bass.ds(b * SSEQ + SEQ, SSEQ)])
                    last.then_inc(halves, 1)
                    pool.wait_ge(halves, 2 * b + e + 1)
                pool.tensor_copy(mk[:, k, PAST:KEYS], K.cst[0:R, bass.ds(b * NSAMP + C_CAUS, NSAMP)]).then_inc(q_set, 1)

            stage(0, 0)
            stage(1, 1)
            with pool.Fori(1, NBATCH // 2) as i:
                for k in range(2):
                    stage(2 * i + k, k)

        @block.tensor
        def _(pe):
            with pe.Fori(0, NBATCH // 2) as i:
                for k in range(2):
                    b = 2 * i + k
                    pe.wait_ge(page_in[k], LOADS * i + LOADS)
                    pe.wait_ge(q_set, b + 1)
                    pe.wait_ge(d_set, b + 1)
                    pe.wait_ge(ca_p, 2 * i + 1)
                    s = psS[k][0:R, 0:KEYS]
                    pe.matmul(s, K.cst[0:H_C, C_ROW48:C_ROW48 + R], dn[:, k, :], start=True, stop=False)
                    for j in range(PAIRS):
                        pe.matmul(s[:, 0:PAST], qb[:, k, j, :], kp[:, k, j, :], start=False, stop=False)
                        last = pe.matmul(s[:, PAST:KEYS], qb[:, k, j, :], K.qkc[:, PAIRS + j, SEQ:TOK], start=False,
                                         stop=(j == PAIRS - 1))
                    last.then_inc(ca_s, 1)
                for k in range(2):
                    b = 2 * i + k
                    wait_apart(pe, K, (ca_norm, b + 1), (ca_pt, 2 * i + 1))
                    for c in range(3):
                        n = P if c < NPAGE else NSAMP
                        last = pe.transpose(psT[k][0:n, c * R:(c + 1) * R], pb[:, k, c * P:c * P + n], K.ident[0:R, 0:R])
                    last.then_inc(ca_t, 1)
                for k in range(2):
                    b = 2 * i + k
                    pe.wait_ge(ca_pt, b + 2)
                    pe.wait_ge(ca_om, 2 * i + 1)
                    for c in range(NPAGE):
                        pe.matmul(psV[k][0:R, 0:W_C], pt[:, k, c, :], vp[:, k, c, :], start=(c == 0), stop=False)
                    pe.matmul(psV[k][0:R, 0:W_C], pt[0:NSAMP, k, NPAGE, :], K.vc[0:NSAMP, NT, :], start=False, stop=True)\
                        .then_inc(ca_v, 1)
                for k in range(2):
                    b = 2 * i + k
                    pe.wait_ge(ca_om, b + 2)
                    pe.wait_ge(ca_out, 2 * i + 1)
                    for j in range(PAIRS):
                        last = pe.matmul(psO[k][:, j * SSEQ:(j + 1) * SSEQ], om[:, k, j * P:(j + 1) * P],
                                         K.cst[0:R, C_PICK:C_PICK + SSEQ], start=True, stop=True)
                    last.then_inc(ca_o, 1)

        @block.scalar
        def _(act):
            with act.Fori(0, NBATCH // 2) as i:
                for k in range(2):
                    b = 2 * i + k
                    act.wait_ge(ca_p, b + 2)
                    act.activation(pb[:, k], pb[:, k], ACT.Exp, bias=st[:, k, 1:2], accum_out=st[:, k, 2:3]).then_inc(ca_exp, 1)
                for k in range(2):
                    b = 2 * i + k
                    act.wait_ge(ca_t, b + 2)
                    act.wait_ge(ca_v, 2 * i + 1)
                    act.activation(pt[:, k, 0:NPAGE, :], psT[k][:, 0:NPAGE * R].rearrange("p (c r) -> p c r", c=NPAGE), ACT.Copy)
                    act.activation(pt[0:NSAMP, k, NPAGE, :], psT[k][0:NSAMP, NPAGE * R:3 * R], ACT.Copy).then_inc(ca_pt, 1)
                for k in range(2):
                    b = 2 * i + k
                    act.wait_ge(ca_o, b + 2)
                    act.activation(K.hT[:, 5:8, bass.ds(b * SSEQ + SEQ, SSEQ)],
                                   psO[k][:, 0:PAIRS * SSEQ].rearrange("p (j s) -> p j s", j=PAIRS), ACT.Copy)\
                        .then_inc(ca_out, 1)

        @block.vector
        def _(dve):
            dve.memset(one[:], 1.0).then_inc(clear_d, 1)
            dve.wait_ge(clear_d, 1)
            with dve.Fori(0, NBATCH // 2) as i:
                chain = Chain(dve, ca_chain, i * 6)
                for k in range(2):
                    b = 2 * i + k
                    dve.wait_ge(page_in[k], LOADS * i + LOADS)
                    dve.wait_ge(ca_s, 2 * i + 1)
                    chain.link(dve.tensor_tensor_scan(dn[:, k, 0:PAST], one[:], lf[:, k], 0.0, ALU.mult, ALU.subtract))
                    dve.tensor_scalar(dn[:, k, PAST:KEYS], K.nd[:, SEQ:TOK], dn[:, k, PAST - 1:PAST], None, ALU.add)\
                        .then_inc(d_set, 1)
                for k in range(2):
                    b = 2 * i + k
                    wait_apart(dve, K, (ca_s, b + 2), (q_set, b + 1), (ca_t, 2 * i + 1))
                    chain.link(dve.tensor_tensor_reduce(pb[:, k], psS[k][0:R, 0:KEYS], mk[:, k], 1.0, -3e38, ALU.add, ALU.max,
                                                        st[:, k, 0:1]))
                    dve.tensor_scalar(st[:, k, 1:2], st[:, k, 0:1], -1.0, None, ALU.mult).then_inc(ca_p, 1)
                for k in range(2):
                    b = 2 * i + k
                    dve.wait_ge(ca_exp, b + 1)
                    chain.link(dve.reciprocal(st[:, k, 3:4], st[:, k, 2:3]))
                    dve.tensor_scalar(pb[:, k], pb[:, k], st[:, k, 3:4], None, ALU.mult).then_inc(ca_norm, 1)
                for k in range(2):
                    b = 2 * i + k
                    dve.wait_ge(ca_v, b + 2)
                    dve.wait_ge(ca_o, 2 * i + 1)
                    dve.tensor_tensor(om[:, k], psV[k][0:R, 0:W_C], K.cst[0:R, C_OWN:C_OWN + W_C], ALU.mult).then_inc(ca_om, 1)


def delta_rule(nc, ctx, K):
    with ExitStack() as own:
        sem = stage_semaphores(nc, own)
        sb = lambda n, s, d=F32: own.enter_context(nc.sbuf_tensor(n, s, d))
        H, G3 = H_A, 3
        stg = sb("dr_stg", [P, FT_A, P])
        obs = sb("dr_obs", [P, W_B])
        sm = sb("dr_sm", [P, 5, H])
        sq = sb("dr_sq", [P, 2, H, HD])
        ss = sb("dr_ss", [P, 3, 2 * H])
        mhalf = sb("dr_mhalf", [P, 2 * H])
        qk = sb("dr_qk", [P, 2, H, HD])
        kx = sb("dr_kx", [P, 5, H, HD])
        tr = sb("dr_tr", [P, 4, PAIRS, P])
        ex = sb("dr_ex", [P, H, P])
        lt = sb("dr_lt", [P, H, P])
        at = sb("dr_at", [P, H, P])
        ot = sb("dr_ot", [P, 2, H, P])
        T = sb("dr_T", [P, H, P])
        TT = sb("dr_TT", [P, H, P])
        X = sb("dr_X", [P, H, P])
        wT = sb("dr_wT", [P, PAIRS, P])
        vn = sb("dr_vn", [P, H, HD])
        oo = sb("dr_oo", [P, H, HD])
        S = sb("dr_S", [P, PAIRS, HD])
        S2 = sb("dr_S2", [P, PAIRS, HD])
        S0 = sb("dr_S0", [P, PAIRS, NBATCH, HD])
        pick = sb("dr_pick", [NSAMP, 2, NBATCH, HD])
        sel = sb("dr_selv", [NSAMP, 2, H, HD])
        A = [own.enter_context(nc.psum_tensor(f"dr_A{g}", [P, 512], F32)) for g in range(2)]
        B = [own.enter_context(nc.psum_tensor(f"dr_B{g}", [P, 512], F32)) for g in range(2)]
        C = [own.enter_context(nc.psum_tensor(f"dr_C{g}", [P, 512], F32)) for g in range(2)]
        M = [own.enter_context(nc.psum_tensor(f"dr_M{g}", [P, 512], F32)) for g in range(2)]
        (g_staged, sq_set, ss_set, ms_set, rn_set, vb_set, qk_set, kb_set, kx_set, gcb_mm, dd_set, e_set, tr_mm,
         tra_set, trd_set, lt_mm, lt_set, ata_set, at_set, ot_set, t1_mm, x_mm, x_set, y_mm, t_set, w_mm, w_set, vn_mm, vn_set,
         o_mm, s_mm, osq_set, oms_set, orn_set, chain_s, own_chain_s, scaled, gr_set, init, s0_in,
         own_mm, own_set, s_out) = (sem("dr_" + n) for n in (
             "staged sq_set ss_set ms_set rn_set vb_set qk_set kb_set kx_set gcb_mm dd_set e_set tr_mm tra_set "
             "trd_set lt_mm lt_set ata_set at_set ot_set t1_mm x_mm x_set y_mm t_set w_mm w_set vn_mm vn_set o_mm s_mm "
             "osq_set oms_set orn_set chain own_chain scaled gr_set init s0_in own_mm own_set s_out"
         ).split())
        qkv_turned, s_set, oo_set, ot2_mm, mixed_set = (
            sem("dr_" + n, 1) for n in "qkv_turned s_set oo_set ot2_mm mixed_set".split())
        LV = LEVELS
        LV8 = 3
        block = own.enter_context(nc.Block())

        def heads(ap, n):
            return ap.rearrange("p (h c) -> p h c", h=G3)

        @block.sync
        def _(sp):
            sp.dma_start(S0[:], K.s0_d).then_inc(s0_in, 16)
            sp.wait_ge(s_set, NT + 1)
            sp.dma_start(K.p_S, S[:]).then_inc(s_out, 16)
            sp.wait_ge(s_set, NT + H + 1)
            sp.dma_start(K.s_S, S0[:]).then_inc(s_out, 16)
            sp.wait_ge(s_out, 32)

        @block.gpsimd
        def _(pool):
            pool.memset(mhalf[:], -0.5)
            pool.memset(S[:], 0.0).then_inc(init, 1)
            pool.wait_ge(init, 1)

            def tile(t, n, nl, tri):
                after(pool, qkv_turned, 3 * t + 1)
                after(pool, ot2_mm, t + 1)
                after(pool, oo_set, t + 1)
                pool.tensor_copy(stg[:, :, 0:n], K.qkv[:, :, bass.ds(t * P, n)])
                pool.tensor_copy(obs[0:n], flat(K.tok[0:n, bass.ds(t, 1), W_A:W_A + W_B]))
                pool.tensor_copy(sm[0:n, 0], flat(K.tm[0:n, bass.ds(t, 1), 0, :]))
                pool.tensor_copy(sm[0:n, 1], flat(K.tm[0:n, bass.ds(t, 1), 1, :]))
                pool.tensor_copy(sm[0:n, 2], flat(K.ec[0:n, 0, bass.ds(t, 1), :]))
                pool.tensor_copy(sm[0:n, 3], flat(K.ec[0:n, 1, bass.ds(t, 1), :])).then_inc(g_staged, 1)
                wait_apart(pool, K, (g_staged, t + 1))
                pool.tensor_scalar(sm[0:n, 4], sm[0:n, 2], -1.0, None, ALU.mult)
                wait_apart(pool, K, (ss_set, t + 1))
                pool.tensor_scalar(ss[0:n, 1], ss[0:n, 0], EPS, None, ALU.add).then_inc(ms_set, 1)
                pool.wait_ge(ms_set, 2 * t + 1)
                pool.tensor_tensor(ss[0:n, 2], ss[0:n, 1], mhalf[0:n], ALU.pow).then_inc(ms_set, 1)
                wait_apart(pool, K, (ms_set, 2 * t + 2))
                pool.tensor_scalar(ss[0:n, 2, 0:H], ss[0:n, 2, 0:H], HD ** -0.5, None, ALU.mult).then_inc(rn_set, 1)

                def by(i):
                    return sm[0:n, i, :].unsqueeze(2).broadcast_to([n, H, HD])

                pool.wait_ge(qk_set, t + 1)
                pool.tensor_tensor(kx[0:n, 0], qk[0:n, 1], by(0), ALU.mult).then_inc(kb_set, 1)
                pool.tensor_tensor(kx[0:n, 1], qk[0:n, 0], by(2), ALU.mult).then_inc(kb_set, 1)
                pool.wait_ge(kb_set, 2 * t + 2)
                pool.tensor_tensor(kx[0:n, 2], kx[0:n, 0], by(4), ALU.mult)
                pool.tensor_tensor(kx[0:n, 3], qk[0:n, 1], by(3), ALU.mult).then_inc(kx_set, 1)
                pool.wait_ge(lt_set, 2 * t + 2)
                for l in range(nl):
                    if l >= 2:
                        pool.wait_ge(x_mm, 2 * (LV - 1) * t + max(1, 2 * (l - 2)))
                    mask = K.cst[0:n, C_LVL + l * P:C_LVL + l * P + n].unsqueeze(1).broadcast_to([n, H, n])
                    pool.tensor_tensor(ot[0:n, l % 2, :, 0:n], lt[0:n, :, 0:n], mask, ALU.mult).then_inc(ot_set, 1)
                    if l == 1:
                        pool.wait_ge(ata_set, t + 1)
                        pool.tensor_tensor(at[0:n, :, 0:n], at[0:n, :, 0:n], tri.unsqueeze(1).broadcast_to([n, H, n]), ALU.mult)\
                            .then_inc(at_set, 1)
                wait_apart(pool, K, (osq_set, 2 * t + 2))
                pool.tensor_scalar(ss[0:n, 1, 0:H], ss[0:n, 0, 0:H], 1.0 / HD, EPS, ALU.mult, ALU.add).then_inc(oms_set, 1)
                pool.wait_ge(oms_set, t + 1)
                pool.tensor_tensor(ss[0:n, 2, 0:H], ss[0:n, 1, 0:H], mhalf[0:n, 0:H], ALU.pow).then_inc(orn_set, 1)

            with pool.Fori(0, NT) as t:
                tile(t, P, LV, K.tri)
            tile(NT, NSAMP, LV8, K.tri8)

        @block.tensor
        def _(pe):
            def intra(t, n, nl):
                pe.wait_ge(g_staged, t + 1)
                pe.wait_ge(mixed_set, 2 * t + 1)
                pe.wait_ge(s_set, t + 1)
                for i, bank in enumerate((A[0], A[1], B[0])):
                    for j in range(PAIRS):
                        last = pe.transpose(bank[0:n, j * P:(j + 1) * P], stg[:, PAIRS * i + j, 0:n], K.ident)
                    last.then_inc(qkv_turned, 1)
                for h in range(H):
                    last = pe.matmul(M[h % 2][0:n, (h // 2) * n:(h // 2 + 1) * n],
                                     K.cst[0:H, C_HEAD + h * P:C_HEAD + h * P + n], K.gr[:, bass.ds(t * P, n)],
                                     start=True, stop=True)
                last.then_inc(gcb_mm, 1)
                for i, (src, bank, s, v) in enumerate(((qk[0:n, 0], B[1], qk_set, t + 1), (qk[0:n, 1], C[0], qk_set, t + 1),
                                                       (kx[0:n, 0], C[1], kb_set, 2 * t + 1), (kx[0:n, 1], B[0], kb_set, 2 * t + 2))):
                    pe.wait_ge(s, v)
                    if i == 3:
                        pe.wait_ge(vb_set, t + 1)
                    x = src.rearrange("p h d -> p (h d)")
                    for j in range(PAIRS):
                        last = pe.transpose(bank[:, j * n:(j + 1) * n], x[:, j * P:(j + 1) * P], K.ident[0:n, 0:n])
                    last.then_inc(tr_mm, 1)
                pe.wait_ge(tra_set, 2 * t + 2)
                pe.wait_ge(trd_set, 2 * t + 1)
                pe.wait_ge(dd_set, t + 1)
                for dst, rhs in ((A, 2), (M, 0)):
                    for g in range(2):
                        for x in range(G3):
                            h = 2 * x + g
                            r = slice((h % 2) * HD, (h % 2 + 1) * HD)
                            last = pe.matmul(dst[g][0:n, x * n:(x + 1) * n], tr[r, 1, h // 2, 0:n], tr[r, rhs, h // 2, 0:n],
                                             start=True, stop=True)
                        last.then_inc(lt_mm, 1)
                pe.wait_ge(ot_set, LV * t + 1)
                for g in range(2):
                    for x in range(G3):
                        last = pe.transpose(A[g][0:n, x * n:(x + 1) * n], ot[0:n, 0, 2 * x + g, 0:n], K.ident[0:n, 0:n])
                    last.then_inc(t1_mm, 1)
                X0 = 2 * (LV - 1) * t
                for l in range(1, nl):
                    pe.wait_ge(ot_set, LV * t + l + 1)
                    for g in range(2):
                        pe.wait_ge(t_set, 2 * LV * t + 2 * l + g - 1)
                        for x in range(G3):
                            h = 2 * x + g
                            last = pe.matmul(A[g][0:n, x * n:(x + 1) * n], ot[0:n, l % 2, h, 0:n], T[0:n, h, 0:n],
                                             start=True, stop=True)
                        last.then_inc(x_mm, 1)
                    for g in range(2):
                        pe.wait_ge(x_set, X0 + 2 * (l - 1) + g + 1)
                        for x in range(G3):
                            h = 2 * x + g
                            c = slice(x * n, (x + 1) * n)
                            if l < nl - 1:
                                pe.matmul(B[g][0:n, c], TT[0:n, h, 0:n], X[0:n, h, 0:n], start=True, stop=True)
                            last = pe.matmul(C[g][0:n, c], X[0:n, h, 0:n], TT[0:n, h, 0:n], start=True, stop=True)
                        last.then_inc(y_mm, 1)

            def weights(t, n, nl):
                pe.wait_ge(t_set, 2 * LV * t + 2 * nl)
                pe.wait_ge(kx_set, t + 1)
                pe.wait_ge(ata_set, t + 1)
                for h in range(H):
                    r = slice((h % 2) * HD, (h % 2 + 1) * HD)
                    last = pe.matmul(M[0][r, (h // 2) * n:(h // 2 + 1) * n], kx[0:n, 2, h, :], TT[0:n, h, 0:n],
                                     start=True, stop=True)
                last.then_inc(w_mm, 1)

            def finish(t, n):
                pe.wait_ge(oo_set, t + 2)
                o = oo[0:n].rearrange("p h d -> p (h d)")
                for j in range(PAIRS):
                    last = pe.transpose(B[0][:, j * n:(j + 1) * n], o[:, j * P:(j + 1) * P], K.ident[0:n, 0:n])
                for j in range(2):
                    last = pe.transpose(B[1][:, j * n:(j + 1) * n], obs[0:n, j * P:(j + 1) * P], K.ident[0:n, 0:n])
                last.then_inc(ot2_mm, 1)

            pe.wait_ge(gr_set, 1)
            pe.wait_ge(init, 1)
            with pe.Fori(0, NT) as t:
                intra(t, P, LV)
                weights(t, P, LV)
                pe.wait_ge(w_set, t + 1)
                for h in range(H):
                    r = slice((h % 2) * HD, (h % 2 + 1) * HD)
                    c = slice((h // 2) * HD, (h // 2 + 1) * HD)
                    bank = (M[1], B[0])[h % 2]
                    pe.matmul(bank[:, c], TT[:, h, :], kx[:, 4, h, :], start=True, stop=False)
                    last = pe.matmul(bank[:, c], wT[r, h // 2, :], S[r, h // 2, :], start=False, stop=True)
                last.then_inc(vn_mm, 1)
                pe.wait_ge(vn_set, t + 1)
                pe.wait_ge(at_set, t + 1)
                pe.wait_ge(trd_set, 2 * t + 2)
                for h in range(H):
                    r = slice((h % 2) * HD, (h % 2 + 1) * HD)
                    c = slice((h // 2) * HD, (h // 2 + 1) * HD)
                    pe.matmul(A[h % 2][:, c], tr[r, 3, h // 2, :], S[r, h // 2, :], start=True, stop=False)
                    last = pe.matmul(A[h % 2][:, c], at[:, h, :], vn[:, h, :], start=False, stop=True)
                last.then_inc(o_mm, 1)
                for h in range(H):
                    r = slice((h % 2) * HD, (h % 2 + 1) * HD)
                    last = pe.matmul(C[0][r, (h // 2) * HD:(h // 2 + 1) * HD], kx[:, 3, h, :], vn[:, h, :],
                                     start=True, stop=True)
                last.then_inc(s_mm, 1)
                finish(t, P)

            t, n = NT, NSAMP
            intra(t, n, LV8)
            weights(t, n, LV8)
            for h in range(H):
                last = pe.matmul(M[1][0:n, h * HD:(h + 1) * HD], TT[0:n, h, 0:n], kx[0:n, 4, h, :], start=True, stop=True)
            last.then_inc(vn_mm, 1)
            pe.wait_ge(w_set, t + 1)
            pe.wait_ge(trd_set, 2 * t + 2)
            pe.wait_ge(s0_in, 16)
            banks = (B[0], B[1])
            for m in range(2 * H):
                h, src = m % H, (wT[:] if m < H else tr[:, 3])
                r = slice((h % 2) * HD, (h % 2 + 1) * HD)
                if m >= 2:
                    pe.wait_ge(own_set, m - 1)
                pe.matmul(banks[m % 2][0:n, :], src[r, h // 2, 0:n], S0[r, h // 2].rearrange("p b v -> p (b v)"),
                          start=True, stop=True).then_inc(own_mm, 1)
            pe.wait_ge(vn_set, t + 1)
            pe.wait_ge(at_set, t + 1)
            for h in range(H):
                last = pe.matmul(A[0][0:n, h * HD:(h + 1) * HD], at[0:n, h, 0:n], vn[0:n, h, :], start=True, stop=True)
            last.then_inc(o_mm, 1)
            for h in range(H):
                r = slice((h % 2) * HD, (h % 2 + 1) * HD)
                pe.wait_ge(own_set, 2 * H + h + 1)
                if h >= 2:
                    pe.wait_ge(s_set, NT + h)
                pe.matmul(C[h % 2][r, :], kx[0:n, 3, h, :], pick[:, h % 2].rearrange("p b v -> p (b v)"),
                          start=True, stop=True).then_inc(s_mm, 1)
            finish(t, n)

        @block.scalar
        def _(act):
            def tile(t, n, nl):
                for i in range(2):
                    act.wait_ge(qkv_turned, 3 * t + i + 2)
                    last = act.activation(sq[0:n, i].rearrange("p h d -> p (h d)"), A[i][0:n, 0:W_A], ACT.Square)
                last.then_inc(sq_set, 1)
                act.wait_ge(dd_set, t + 1)
                act.activation(ex[0:n, :, 0:n], ex[0:n, :, 0:n], ACT.Exp).then_inc(e_set, 1)
                for i, bank in ((0, B[1]), (2, C[1])):
                    act.wait_ge(tr_mm, 4 * t + i + 1)
                    act.activation(tr[:, i, :, 0:n], bank[:, 0:PAIRS * n].rearrange("p (j c) -> p j c", j=PAIRS), ACT.Copy)\
                        .then_inc(tra_set, 1)
                X0 = 2 * (LV - 1) * t
                for l in range(1, nl):
                    for g in range(2):
                        act.wait_ge(x_mm, X0 + 2 * (l - 1) + g + 1)
                        act.activation(X[0:n, g::2, 0:n], heads(A[g][0:n, 0:G3 * n], n), ACT.Copy)\
                            .then_inc(x_set, 1)
                act.wait_ge(w_mm, t + 1)
                act.activation(wT[:, :, 0:n], M[0][:, 0:PAIRS * n].rearrange("p (j c) -> p j c", j=PAIRS), ACT.Copy)\
                    .then_inc(w_set, 1)

            def finish(t, n):
                act.wait_ge(ot2_mm, t + 2)
                act.activation(K.hT[:, 0:3, bass.ds(t * P, n)], B[0][:, 0:3 * n].rearrange("p (j c) -> p j c", j=3), ACT.Copy)\
                    .then_inc(mixed_set, 1)
                act.activation(K.hT[:, 3:5, bass.ds(t * P, n)], B[1][:, 0:2 * n].rearrange("p (j c) -> p j c", j=2), ACT.Copy)\
                    .then_inc(mixed_set, 1)

            with act.Fori(0, NT) as t:
                tile(t, P, LV)
                act.wait_ge(vn_mm, t + 1)
                for g, bank in enumerate((M[1], B[0])):
                    last = act.activation(vn[:, g::2, :], heads(bank[:, 0:G3 * HD], P), ACT.Copy)
                last.then_inc(vn_set, 1)
                act.wait_ge(o_mm, t + 1)
                for g in range(2):
                    last = act.activation(sq[:, 0, g::2, :], heads(A[g][:, 0:G3 * HD], P), ACT.Square)
                last.then_inc(osq_set, 1)
                finish(t, P)
            tile(NT, NSAMP, LV8)
            act.wait_ge(scaled, 1)
            act.activation(sq[0:NSAMP, 0], oo[0:NSAMP], ACT.Square).then_inc(osq_set, 1)
            finish(NT, NSAMP)

        @block.vector
        def _(dve):
            dve.tensor_copy(K.gr[:], K.rows[32:32 + H, :]).then_inc(gr_set, 1)

            def intra(t, n, nl):
                chain = Chain(dve, chain_s, 4 * t)

                dve.wait_ge(sq_set, t + 1)
                dve.tensor_reduce(ss[0:n, 0], sq[0:n].rearrange("p a h d -> p (a h) d"), AX.X, ALU.add).then_inc(ss_set, 1)
                dve.wait_ge(qkv_turned, 3 * t + 4)
                dve.wait_ge(g_staged, t + 1)
                dve.tensor_tensor(kx[0:n, 4], B[0][0:n, 0:W_A].rearrange("p (h d) -> p h d", h=H),
                                  sm[0:n, 0, :].unsqueeze(2).broadcast_to([n, H, HD]), ALU.mult).then_inc(vb_set, 1)
                dve.wait_ge(rn_set, t + 1)
                for i in range(2):
                    r = ss[0:n, 2, i * H:(i + 1) * H].unsqueeze(2).broadcast_to([n, H, HD])
                    last = dve.tensor_tensor(qk[0:n, i], A[i][0:n, 0:W_A].rearrange("p (h d) -> p h d", h=H), r, ALU.mult)
                last.then_inc(qk_set, 1)
                dve.wait_ge(gcb_mm, t + 1)
                for g in range(2):
                    gc = sm[0:n, 1, g::2].unsqueeze(2).broadcast_to([n, G3, n])
                    ins = dve.tensor_tensor(ex[0:n, g::2, 0:n], heads(M[g][0:n, 0:G3 * n], n), gc, ALU.subtract)
                chain.link(ins)
                dve.tensor_scalar(ex[0:n, :, 0:n], ex[0:n, :, 0:n], 0.0, None, ALU.min).then_inc(dd_set, 1)
                for i, bank in ((1, C[0]), (3, B[0])):
                    dve.wait_ge(tr_mm, 4 * t + i + 1)
                    dve.tensor_copy(tr[:, i, :, 0:n], bank[:, 0:PAIRS * n].rearrange("p (j c) -> p j c", j=PAIRS))\
                        .then_inc(trd_set, 1)
                dve.wait_ge(e_set, t + 1)
                for g in range(2):
                    hs = slice(g, H, 2)
                    dve.wait_ge(lt_mm, 4 * t + g + 1)
                    dve.tensor_tensor(lt[0:n, hs, 0:n], heads(A[g][0:n, 0:G3 * n], n), ex[0:n, hs, 0:n], ALU.mult)\
                        .then_inc(lt_set, 1)
                for g in range(2):
                    hs = slice(g, H, 2)
                    dve.wait_ge(lt_mm, 4 * t + g + 3)
                    ins = dve.tensor_tensor(at[0:n, hs, 0:n], heads(M[g][0:n, 0:G3 * n], n), ex[0:n, hs, 0:n], ALU.mult)
                ins.then_inc(ata_set, 1)
                dve.wait_ge(ot_set, LV * t + 1)
                eye = K.ident[0:n, 0:n].unsqueeze(1)
                chain.link(dve.tensor_tensor(TT[0:n, :, 0:n], eye.broadcast_to([n, H, n]), ot[0:n, 0, :, 0:n], ALU.subtract))
                for g in range(2):
                    hs = slice(g, H, 2)
                    dve.wait_ge(t1_mm, 2 * t + g + 1)
                    dve.tensor_tensor(T[0:n, hs, 0:n], eye.broadcast_to([n, G3, n]), heads(A[g][0:n, 0:G3 * n], n),
                                      ALU.subtract).then_inc(t_set, 1)
                X0 = 2 * (LV - 1) * t
                for l in range(1, nl):
                    for g in range(2):
                        hs = slice(g, H, 2)
                        dve.wait_ge(y_mm, X0 + 2 * (l - 1) + g + 1)
                        if l < nl - 1:
                            dve.tensor_tensor(T[0:n, hs, 0:n], T[0:n, hs, 0:n], heads(B[g][0:n, 0:G3 * n], n), ALU.subtract)
                        dve.tensor_tensor(TT[0:n, hs, 0:n], TT[0:n, hs, 0:n], heads(C[g][0:n, 0:G3 * n], n), ALU.subtract)\
                            .then_inc(t_set, 1)
                return chain

            def finish(t, n, chain, src):
                dve.wait_ge(osq_set, 2 * t + 1)
                dve.tensor_reduce(ss[0:n, 0, 0:H], sq[0:n, 0], AX.X, ALU.add).then_inc(osq_set, 1)
                dve.wait_ge(orn_set, t + 1)
                for g, x in enumerate(src):
                    r = ss[0:n, 2, g:H:2].unsqueeze(2).broadcast_to([n, G3, HD])
                    ins = dve.tensor_tensor(oo[0:n, g::2, :], x, r, ALU.mult)
                chain.link(ins)
                dve.tensor_tensor(oo[0:n].rearrange("p h d -> p (h d)"), oo[0:n].rearrange("p h d -> p (h d)"),
                                  flat(K.tok[0:n, bass.ds(t, 1), 0:W_A]), ALU.mult).then_inc(oo_set, 1)

            dve.wait_ge(init, 1)
            with dve.Fori(0, NT) as t:
                chain = intra(t, P, LV)
                gl = K.gl[:, :, bass.ds(t, 1)].broadcast_to([P, PAIRS, HD])
                chain.link(dve.tensor_tensor(S2[:], S[:], gl, ALU.mult))
                dve.wait_ge(o_mm, t + 1)
                dve.wait_ge(s_mm, t + 1)
                dve.tensor_tensor(S[:], S2[:], C[0][:, 0:PAIRS * HD].rearrange("p (j v) -> p j v", j=PAIRS), ALU.add)\
                    .then_inc(s_set, 1)
                finish(t, P, chain, [heads(A[g][:, 0:G3 * HD], P) for g in range(2)])

            t, n = NT, NSAMP
            intra(t, n, LV8)
            blk = K.cst[0:n, C_BLK:C_BLK + NBATCH].unsqueeze(2).broadcast_to([n, NBATCH, HD])
            banks = (B[0], B[1])
            own_chain = Chain(dve, own_chain_s)
            for m in range(2 * H):
                dve.wait_ge(own_mm, m + 1)
                own_chain.link(dve.tensor_tensor(pick[:, m % 2], banks[m % 2][0:n, :].rearrange("p (b v) -> p b v", b=NBATCH),
                                                 blk, ALU.mult))
                dve.tensor_reduce(sel[:, m // H, m % H], pick[:, m % 2].rearrange("p b v -> p v b"), AX.X, ALU.add)\
                    .then_inc(own_set, 1)
            dve.wait_ge(own_set, 2 * H)
            dve.wait_ge(vn_mm, t + 1)
            dve.tensor_tensor(vn[0:n], M[1][0:n, 0:W_A].rearrange("p (h d) -> p h d", h=H), sel[:, 0], ALU.add)\
                .then_inc(vn_set, 1)
            dve.wait_ge(vn_set, t + 1)
            for h in range(H):
                r = slice((h % 2) * HD, (h % 2 + 1) * HD)
                if h >= 2:
                    dve.wait_ge(s_mm, NT + h - 1)
                dve.tensor_tensor(pick[:, h % 2], vn[0:n, h, :].unsqueeze(1).broadcast_to([n, NBATCH, HD]), blk, ALU.mult)\
                    .then_inc(own_set, 1)
                gl = K.gl[r, h // 2, 8:16].unsqueeze(2).broadcast_to([HD, NBATCH, HD])
                own_chain.link(dve.tensor_tensor(S0[r, h // 2], S0[r, h // 2], gl, ALU.mult))
                dve.wait_ge(s_mm, NT + h + 1)
                dve.tensor_tensor(S0[r, h // 2], S0[r, h // 2], C[h % 2][r, :].rearrange("p (b v) -> p b v", b=NBATCH), ALU.add)\
                    .then_inc(s_set, 1)
            dve.wait_ge(o_mm, t + 1)
            dve.tensor_tensor(oo[0:n], A[0][0:n, 0:W_A].rearrange("p (h d) -> p h d", h=H), sel[:, 1], ALU.add)\
                .then_inc(scaled, 1)
            finish(t, n, own_chain, [oo[0:n, g::2, :] for g in range(2)])


def output_projection(nc, ctx, K):
    with ExitStack() as own:
        sem = stage_semaphores(nc, own)
        sb = lambda n, s, d=F32: own.enter_context(nc.sbuf_tensor(n, s, d))
        wo = sb("op_w", [P, KD, D])
        ms = sb("op_m", [P, 2, KD, P])
        xt = sb("op_x", [P, 2, D])
        x1 = sb("op_x1", [P, 2, D])
        xn = sb("op_xn", [P, 2, D])
        junk = sb("op_junk", [P, D])
        ss = sb("op_ss", [P, 2, 8])
        mhalf = sb("op_mhalf", [P, 1])
        gg = sb("op_gg", [P, 2, D])
        gp = sb("op_gp", [P, D])
        psO = [own.enter_context(nc.psum_tensor(f"op_psO{i}", [P, D], F32)) for i in range(2)]
        psX = own.enter_context(nc.psum_tensor("op_psX", [P, KD, P], F32))
        (w_in, g_in, staged, mm, sq_set, r_chain, r_set, x1_chain, x1_set, sq1_set, r1_set, xn_set, turned, h2_set, h2_chain,
         gg_set, half_set) = (sem("op_" + n) for n in (
             "w_in g_in staged mm sq_set r_chain r_set x1_chain x1_set sq1_set r1_set xn_set turned h2_set h2_chain gg_set "
             "half_set").split())
        x_in = [sem("op_x_in0"), sem("op_x_in1")]
        x1_out = [sem("op_x1_out0"), sem("op_x1_out1")]
        block = own.enter_context(nc.Block())

        def tiles(eng, step):
            step(0, 0, P)
            step(1, 1, P)
            with eng.Fori(1, NT // 2) as i:
                for k in range(2):
                    step(2 * i + k, k, P)
            step(NT, 0, NSAMP)

        @block.sync
        def _(sp):
            sp.dma_start(wo[:], K.w_out_d).then_inc(w_in, 16)
            sp.dma_start(gp[:], K.gpost_d[0:1].broadcast_to([P, D])).then_inc(g_in, 16)
            sp.dma_start(gg[:, 0], K.scr[0:1, 2 * D:3 * D].broadcast_to([P, D])).then_inc(g_in, 16)
            for b in range(NBATCH):
                sp.dma_start(gg[b * SSEQ:(b + 1) * SSEQ, 1], K.scr[b + 1:b + 2, 2 * D:3 * D].broadcast_to([SSEQ, D]))\
                    .then_inc(g_in, 16)

            def step(t, k, rows):
                after(sp, x1_set, t - 1)
                sp.dma_start(xt[0:rows, k], K.x[bass.ds(t * P, rows)]).then_inc(x_in[k], 16)

            tiles(sp, step)

        @block.gpsimd
        def _(pool):
            pool.memset(mhalf[:], -0.5).then_inc(half_set, 1)
            pool.wait_ge(half_set, 1)

            def stage(t, k, rows):
                after(pool, mm, t - 1)
                pool.tensor_copy(ms[:, k, :, 0:rows], K.hT[:, :, bass.ds(t * P, rows)]).then_inc(staged, 1)

            def step(t, k, rows):
                for i, (ready, out) in enumerate(((sq_set, r_set), (sq1_set, r1_set))):
                    c = 4 * i
                    wait_apart(pool, K, (ready, t + 1))
                    pool.tensor_scalar(ss[0:rows, k, c + 1:c + 2], ss[0:rows, k, c:c + 1], 1.0 / D, EPS, ALU.mult, ALU.add)\
                        .then_inc(r_chain, 1)
                    pool.wait_ge(r_chain, 2 * t + i + 1)
                    pool.tensor_tensor(ss[0:rows, k, c + 2:c + 3], ss[0:rows, k, c + 1:c + 2], mhalf[0:rows], ALU.pow)\
                        .then_inc(out, 1)

            stage(0, 0, P)
            stage(1, 1, P)
            with pool.Fori(0, NT // 2 - 1) as i:
                for k in range(2):
                    step(2 * i + k, k, P)
                    stage(2 * i + k + 2, k, P)
            step(NT - 2, 0, P)
            stage(NT, 0, NSAMP)
            step(NT - 1, 1, P)
            step(NT, 0, NSAMP)

        @block.tensor
        def _(pe):
            pe.wait_ge(w_in, 16)

            def gemm(t, k, rows):
                pe.wait_ge(staged, t + 1)
                after(pe, x1_chain, t - 1)
                for c in range(0, D, 512):
                    for kk in range(KD):
                        last = pe.matmul(psO[k][0:rows, c:c + 512], ms[:, k, kk, 0:rows], wo[:, kk, c:c + 512],
                                         start=(kk == 0), stop=(kk == KD - 1))
                last.then_inc(mm, 1)

            def turn(t, k, rows):
                pe.wait_ge(xn_set, t + 1)
                after(pe, h2_set, t)
                for kk in range(KD):
                    last = pe.transpose(psX[:, kk, 0:rows], xn[0:rows, k, kk * P:(kk + 1) * P], K.ident[0:rows, 0:rows])
                last.then_inc(turned, 1)

            gemm(0, 0, P)
            gemm(1, 1, P)
            turn(0, 0, P)
            with pe.Fori(1, NT // 2) as i:
                for k in range(2):
                    gemm(2 * i + k, k, P)
                    turn(2 * i + k - 1, 1 - k, P)
            gemm(NT, 0, NSAMP)
            turn(NT - 1, 1, P)
            turn(NT, 0, NSAMP)

        @block.scalar
        def _(act):
            def step(t, k, rows):
                act.wait_ge(mm, t + 1)
                act.activation(junk[0:rows], psO[k][0:rows, :], ACT.Square, accum_out=ss[0:rows, k, 0:1]).then_inc(sq_set, 1)
                act.wait_ge(x1_set, t + 1)
                act.activation(junk[0:rows], x1[0:rows, k], ACT.Square, accum_out=ss[0:rows, k, 4:5]).then_inc(sq1_set, 1)
                act.dma_start(K.scr_x[bass.ds(t * P, rows)], x1[0:rows, k]).then_inc(x1_out[k], 16)
                act.wait_ge(r1_set, t + 1)
                after(act, turned, t - 1)
                act.activation(xn[0:rows, k], x1[0:rows, k], ACT.Copy, scale=ss[0:rows, k, 6:7]).then_inc(xn_set, 1)

            tiles(act, step)
            act.wait_ge(x1_out[0], 16 * (NT // 2 + 1))
            act.wait_ge(x1_out[1], 16 * (NT // 2))

        @block.vector
        def _(dve):
            dve.wait_ge(g_in, 16 * (2 + NBATCH))
            dve.tensor_tensor(gg[:, 0], gg[:, 0], gp[:], ALU.mult)
            dve.tensor_tensor(gg[0:NSAMP, 1], gg[0:NSAMP, 1], gp[0:NSAMP], ALU.mult).then_inc(gg_set, 1)
            dve.wait_ge(gg_set, 1)

            def residual(t, k, rows):
                dve.wait_ge(r_set, t + 1)
                after(dve, xn_set, t - 1)
                if not isinstance(t, int) or t >= 2:
                    dve.wait_ge(x1_out[k], 8 * (t - k))
                g = gg[0:rows, 0 if rows == P else 1]
                dve.scalar_tensor_tensor(x1[0:rows, k], psO[k][0:rows, :], ss[0:rows, k, 2:3], g, ALU.mult, ALU.mult)\
                    .then_inc(x1_chain, 1)
                dve.wait_ge(x1_chain, t + 1)
                dve.wait_ge(x_in[k], 8 * (t - k) + 16)
                dve.tensor_tensor(x1[0:rows, k], x1[0:rows, k], xt[0:rows, k], ALU.add).then_inc(x1_set, 1)

            def h2(t, k, rows):
                dve.wait_ge(turned, t + 1)
                dve.wait_ge(staged, t + 1)
                made = gain_shift(dve, K, 1, psX, K.hT[:, :, bass.ds(t * P, rows)], rows)
                if rows == P:
                    made[0].then_inc(h2_set, 1)
                else:
                    chain = Chain(dve, h2_chain)
                    for n, (o, a, b, op) in enumerate(made):
                        ins = dve.tensor_tensor(o, a, b, op)
                        if n == len(made) // 2 - 1:
                            chain.link(ins)
                    ins.then_inc(h2_set, 1)

            residual(0, 0, P)
            residual(1, 1, P)
            h2(0, 0, P)
            with dve.Fori(1, NT // 2) as i:
                for k in range(2):
                    residual(2 * i + k, k, P)
                    h2(2 * i + k - 1, 1 - k, P)
            residual(NT, 0, NSAMP)
            h2(NT - 1, 1, P)
            h2(NT, 0, NSAMP)


def ffn_up(nc, ctx, K, yT):
    with ExitStack() as own:
        sem = stage_semaphores(nc, own)
        sb = lambda n, s, d=F32: own.enter_context(nc.sbuf_tensor(n, s, d))
        RING = 4
        NTILE = 2 * KF
        wu = sb("fu_w", [P, RING, KD, P])
        zp = sb("fu_zp", [P, 2, TAPS_F - 1 + SEQ])
        zs = sb("fu_zs", [P, 2, NBATCH, TAPS_F - 1 + SSEQ])
        cb = sb("fu_cb", [P, TOK])
        prev = sb("fu_prev", [P, NTILE, NBATCH, TAPS_F - 1])
        cw = sb("fu_cw", [P, NTILE, TAPS_F])
        pst = sb("fu_pst", [P, NTILE, TAPS_F - 1])
        sst = sb("fu_sst", [P, NTILE, NBATCH, TAPS_F - 1])
        ps = [own.enter_context(nc.psum_tensor(f"fu_ps{i}", [P, 3, 512], F32)) for i in range(2)]
        w_in = [sem(f"fu_w_in{k}") for k in range(RING)]
        small_in, mm, out, halo, chain_s, conv_set, copied, gelu_set, y_set, zero_set, st_out = (sem("fu_" + n) for n in (
            "small_in mm out halo chain conv_set copied gelu_set y_set zero_set st_out").split())
        block = own.enter_context(nc.Block())

        @block.sync
        def _(sp):
            for k in range(RING):
                sp.dma_start(wu[:, k], K.w_up_d[k]).then_inc(w_in[k], 16)
            sp.dma_start(prev[:], K.fprev_d).then_inc(small_in, 16)
            sp.dma_start(cw[:], K.fconv_d).then_inc(small_in, 16)
            with sp.Fori(1, NTILE // RING) as i:
                for k in range(RING):
                    sp.wait_ge(mm, RING * (i - 1) + k + 1)
                    sp.dma_start(wu[:, k], K.w_up_d[bass.ds(RING * i + k, 1)].rearrange("a p k n -> (a p) k n"))\
                        .then_inc(w_in[k], 16)
            sp.wait_ge(copied, 2 * NTILE)
            sp.dma_start(K.p_fconv, pst[:]).then_inc(st_out, 16)
            sp.dma_start(K.s_fconv, sst[:]).then_inc(st_out, 16)
            sp.wait_ge(st_out, 32)

        @block.tensor
        def _(pe):
            def tile(i, slot, turn):
                pe.wait_ge(w_in[slot], 4 * (i - slot) + 16)
                after(pe, out, i - 1)
                for kk in range(KD):
                    for n, (c, w) in enumerate(((0, 512), (512, 512), (SEQ, NSAMP))):
                        last = pe.matmul(ps[turn][:, n, 0:w], wu[:, slot, kk, :], K.hT[:, kk, c:c + w],
                                         start=(kk == 0), stop=(kk == KD - 1))
                last.then_inc(mm, 1)

            for i in range(RING):
                tile(i, i, i % 2)
            with pe.Fori(1, NTILE // RING) as i:
                for k in range(RING):
                    tile(RING * i + k, k, k % 2)

        def pairs(eng, tile):
            for k in range(2):
                tile(k, k)
            with eng.Fori(1, KF) as i:
                for k in range(2):
                    tile(2 * i + k, k)

        @block.gpsimd
        def _(pool):
            for k in range(2):
                pool.memset(zp[:, k, 0:TAPS_F - 1], 0.0).then_inc(zero_set, 1)
            pool.wait_ge(small_in, 32)

            def tile(i, k):
                after(pool, conv_set, i - 1)
                pool.tensor_copy(zs[:, k, :, 0:TAPS_F - 1], prev[:, bass.ds(i, 1)].rearrange("p a b n -> p (a b) n"))\
                    .then_inc(halo, 1)
                pool.wait_ge(out, i + 1)
                pool.tensor_copy(flat(pst[:, bass.ds(i, 1)]), zp[:, k, SEQ:SEQ + TAPS_F - 1]).then_inc(copied, 1)
                pool.tensor_copy(sst[:, bass.ds(i, 1)].rearrange("p a b n -> p (a b) n"), zs[:, k, :, SSEQ:])\
                    .then_inc(copied, 1)

            pairs(pool, tile)

        @block.scalar
        def _(act):
            act.wait_ge(zero_set, 2)

            def evict(i, k):
                act.wait_ge(mm, i + 1)
                after(act, conv_set, i - 1)
                after(act, copied, 2 * (i - 1))
                act.activation(zp[:, k, TAPS_F - 1:], ps[k][:, 0:2, :].rearrange("p a n -> p (a n)"), ACT.Copy)
                act.activation(zs[:, k, :, TAPS_F - 1:], ps[k][:, 2, 0:NSAMP].rearrange("p (b s) -> p b s", s=SSEQ),
                               ACT.Copy).then_inc(out, 1)

            def gelu(j):
                act.wait_ge(conv_set, 2 * j + 1)
                act.activation(flat(yT[:, bass.ds(j, 1)]), flat(yT[:, bass.ds(j, 1)]), ACT.Gelu_apprx_tanh).then_inc(gelu_set, 1)

            evict(0, 0)
            evict(1, 1)
            gelu(0)
            with act.Fori(1, KF) as j:
                evict(2 * j, 0)
                evict(2 * j + 1, 1)
                gelu(j)

        @block.vector
        def _(dve):
            dve.wait_ge(small_in, 32)

            def conv(j, k):
                i = 2 * j + k
                chain = Chain(dve, chain_s, i * 4)
                y = yT[:, bass.ds(j, 1)] if k == 0 else cb[:].unsqueeze(1)
                yp = flat(y[:, :, 0:SEQ])
                ys = y[:, :, SEQ:TOK].rearrange("p a (b s) -> p (a b) s", s=SSEQ)
                dve.wait_ge(out, i + 1)
                dve.wait_ge(halo, i + 1)
                for tap in range(TAPS_F):
                    w = flat(cw[:, bass.ds(i, 1), tap:tap + 1])
                    a, b = zp[:, k, tap:tap + SEQ], zs[:, k, :, tap:tap + SSEQ]
                    if tap == 0:
                        one = dve.tensor_scalar(yp, a, w, None, ALU.mult)
                        two = dve.tensor_scalar(ys, b, w, None, ALU.mult)
                    else:
                        one = dve.scalar_tensor_tensor(yp, a, w, yp, ALU.mult, ALU.add)
                        two = dve.scalar_tensor_tensor(ys, b, w, ys, ALU.mult, ALU.add)
                    if tap < TAPS_F - 1:
                        one.then_inc(chain_s, 1)
                        chain.n += 1
                        chain.link(two)
                two.then_inc(conv_set, 1)

            def pair(j):
                conv(j, 0)
                conv(j, 1)
                dve.wait_ge(conv_set, 2 * j + 2)
                dve.wait_ge(gelu_set, j + 1)
                y = flat(yT[:, bass.ds(j, 1)])
                dve.tensor_tensor(y, y, cb[:], ALU.mult).then_inc(y_set, 1)

            pair(0)
            with dve.Fori(1, KF) as j:
                pair(j)


def ffn_down(nc, ctx, K, yT):
    with ExitStack() as own:
        sem = stage_semaphores(nc, own)
        sb = lambda n, s, d=F32: own.enter_context(nc.sbuf_tensor(n, s, d))
        RING = 4
        NPASS, TP = 3, 3
        W = TP * P
        wd = sb("fd_w", [P, RING, D])
        ys = sb("fd_y", [P, 2, W])
        x1 = sb("fd_x1", [P, TP, D])
        yo = sb("fd_yo", [P, 2, D])
        junk = sb("fd_junk", [P, D])
        ss = sb("fd_ss", [P, 2, 4])
        mhalf = sb("fd_mhalf", [P, 1])
        gg = sb("fd_gg", [P, 2, D])
        gp = sb("fd_gp", [P, D])
        ps = [own.enter_context(nc.psum_tensor(f"fd_ps{i}", [P, D], F32)) for i in range(TP)]
        w_in = [sem(f"fd_w_in{k}") for k in range(RING)]
        (g_in, x_in, staged, mm, acc, sq_set, r_chain, r_set, out_chain, out_set, gg_set, half_set) = (
            sem("fd_" + n) for n in "g_in x_in staged mm acc sq_set r_chain r_set out_chain out_set gg_set half_set".split())
        y_out = [sem("fd_y_out0"), sem("fd_y_out1")]
        block = own.enter_context(nc.Block())

        def width(p):
            sizes = [P if TP * p + n < NT else NSAMP for n in range(TP)]
            return sum(sizes), sizes

        @block.sync
        def _(sp):
            for k in range(RING):
                sp.dma_start(wd[:, k], K.w_down_d[k]).then_inc(w_in[k], 16)
            sp.dma_start(gp[:], K.gpost_d[1:2].broadcast_to([P, D])).then_inc(g_in, 16)
            sp.dma_start(gg[:, 0], K.scr[0:1, 5 * D:6 * D].broadcast_to([P, D])).then_inc(g_in, 16)
            for b in range(NBATCH):
                sp.dma_start(gg[b * SSEQ:(b + 1) * SSEQ, 1], K.scr[b + 1:b + 2, 5 * D:6 * D].broadcast_to([SSEQ, D]))\
                    .then_inc(g_in, 16)
            for p in range(NPASS):
                _, sizes = width(p)
                for n, rows in enumerate(sizes):
                    t = TP * p + n
                    after(sp, out_set, t - TP + 1)
                    sp.dma_start(x1[0:rows, n], K.scr_x[t * P:t * P + rows]).then_inc(x_in, 16)
                first, end = KF * p, KF * (p + 1)
                for g in range(max(first, RING), end):
                    sp.wait_ge(mm, g - RING + 1)
                    sp.dma_start(wd[:, g % RING], K.w_down_d[g % KF]).then_inc(w_in[g % RING], 16)

        @block.gpsimd
        def _(pool):
            pool.memset(mhalf[:], -0.5).then_inc(half_set, 1)
            pool.wait_ge(half_set, 1)
            for p in range(NPASS):
                w, sizes = width(p)

                def stage(f, k, g):
                    after(pool, mm, g - 1)
                    pool.tensor_copy(ys[:, k, 0:w], flat(yT[:, bass.ds(f, 1), p * W:p * W + w])).then_inc(staged, 1)

                for k in range(2):
                    stage(k, k, KF * p + k)
                with pool.Fori(1, KF // 2) as i:
                    for k in range(2):
                        stage(2 * i + k, k, 2 * i + k + KF * p)
                for n, rows in enumerate(sizes):
                    t = TP * p + n
                    k = t % 2
                    pool.wait_ge(sq_set, t + 1)
                    pool.tensor_scalar(ss[0:rows, k, 1:2], ss[0:rows, k, 0:1], 1.0 / D, EPS, ALU.mult, ALU.add)\
                        .then_inc(r_chain, 1)
                    pool.wait_ge(r_chain, t + 1)
                    pool.tensor_tensor(ss[0:rows, k, 2:3], ss[0:rows, k, 1:2], mhalf[0:rows], ALU.pow).then_inc(r_set, 1)

        @block.tensor
        def _(pe):
            for p in range(NPASS):
                _, sizes = width(p)
                for f in range(KF):
                    g = KF * p + f
                    pe.wait_ge(w_in[g % RING], 16 * (g // RING + 1))
                    pe.wait_ge(staged, g + 1)
                    at = 0
                    for n, rows in enumerate(sizes):
                        if f == 0 and p:
                            pe.wait_ge(out_chain, TP * (p - 1) + n + 1)
                        for c in range(0, D, 512):
                            last = pe.matmul(ps[n][0:rows, c:c + 512], ys[:, g % 2, at:at + rows], wd[:, g % RING, c:c + 512],
                                             start=(f == 0), stop=(f == KF - 1))
                        at += rows
                        if f == KF - 1 and n < TP - 1:
                            last.then_inc(acc, 1)
                    last.then_inc(mm, 1)

        def store(act, t):
            rows = P if t < NT else NSAMP
            act.wait_ge(out_set, t + 1)
            act.dma_start(K.y[t * P:t * P + rows], yo[0:rows, t % 2]).then_inc(y_out[t % 2], 16)

        @block.scalar
        def _(act):
            for p in range(NPASS):
                for n, rows in enumerate(width(p)[1]):
                    t = TP * p + n
                    if n < TP - 1:
                        act.wait_ge(acc, (TP - 1) * p + n + 1)
                    else:
                        act.wait_ge(mm, KF * (p + 1))
                    after(act, sq_set, t)
                    after(act, out_chain, t - 1)
                    act.activation(junk[0:rows], ps[n][0:rows, :], ACT.Square, accum_out=ss[0:rows, t % 2, 0:1])\
                        .then_inc(sq_set, 1)
                    if t:
                        store(act, t - 1)
            store(act, NT)
            act.wait_ge(y_out[0], 16 * (NT // 2 + 1))
            act.wait_ge(y_out[1], 16 * (NT // 2))

        @block.vector
        def _(dve):
            dve.wait_ge(g_in, 16 * (2 + NBATCH))
            dve.tensor_tensor(gg[:, 0], gg[:, 0], gp[:], ALU.mult)
            dve.tensor_tensor(gg[0:NSAMP, 1], gg[0:NSAMP, 1], gp[0:NSAMP], ALU.mult).then_inc(gg_set, 1)
            dve.wait_ge(gg_set, 1)
            for t in range(NT + 1):
                rows = P if t < NT else NSAMP
                n, k = t % TP, t % 2
                dve.wait_ge(r_set, t + 1)
                after(dve, y_out[k], 16 * (t // 2))
                dve.scalar_tensor_tensor(yo[0:rows, k], ps[n][0:rows, :], ss[0:rows, k, 2:3], gg[0:rows, 0 if t < NT else 1],
                                         ALU.mult, ALU.mult).then_inc(out_chain, 1)
                dve.wait_ge(out_chain, t + 1)
                dve.wait_ge(x_in, 16 * (t // TP + 1) * TP)
                dve.tensor_tensor(yo[0:rows, k], yo[0:rows, k], x1[0:rows, n], ALU.add).then_inc(out_set, 1)


def build(nc, A, O):
    K = Kernel()
    with ExitStack() as ctx:
        sb = lambda stack, n, s, d=F32: stack.enter_context(nc.sbuf_tensor(n, s, d))
        sem = lambda n: ctx.enter_context(nc.semaphore(n))
        K.x, K.cT, K.w_ada, K.b_ada, K.cst_d, K.gpre_d = A["x"], A["cT"], A["w_ada"], A["b_ada"], A["cst"], A["gpre"]
        K.w_tm_d, K.gn_d, K.lng_d, K.lnb_d, K.wsT_d, K.wsT8_d, K.bs_d = (A[n] for n in "w_tm gn lng lnb wsT wsT8 bs".split())
        K.w_fm_d, K.gprev_d, K.gconv_d, K.bias_d, K.reset_d = (A[n] for n in "w_fm gprev gconv bias reset".split())
        K.page_table, K.ckT, K.cv, K.clf, K.s0_d = (A[n] for n in "page_table ckT cv clf s0".split())
        K.w_out_d, K.gpost_d, K.w_up_d, K.fprev_d, K.fconv_d, K.w_down_d = (
            A[n] for n in "w_out gpost w_up fprev fconv w_down".split())
        K.y, K.v_out, K.chunk_v, K.p_gconv, K.s_gconv, K.k_out, K.logf_out, K.p_S, K.s_S, K.p_fconv, K.s_fconv = (
            O[n] for n in "y v chunk_v p_gconv s_gconv k logf p_S s_S p_fconv s_fconv".split())
        K.scr = nc.dram_tensor("scr_mod", (NSEQ, 6 * D), F32).ap()
        K.scr_x = nc.dram_tensor("scr_x1", (TOK, D), F32).ap()
        K.cst = sb(ctx, "cst", [P, C_END])
        K.gpre = sb(ctx, "gpre", [P, 2, KD])
        K.gain = sb(ctx, "gain", [P, 2, KD, NSEQ])
        K.shift = sb(ctx, "shift", [P, 2, KD, NSEQ])
        K.ident, K.tri = K.cst[:, C_ID:C_ID + P], K.cst[:, C_TRI:C_TRI + P]
        K.tri8 = K.cst[0:NSAMP, C_TRI8:C_TRI8 + NSAMP]
        K.cst_in, K.w_tm_in = sem("cst_in"), sem("w_tm_in")
        K.hT = sb(ctx, "hT", [P, KD, TOK])
        with ExitStack() as mix:
            K.tok = sb(mix, "tok", [P, NT + 1, W_A + W_B])
            K.vc = sb(mix, "vc", [P, NT + 1, W_C])
            with ExitStack() as wide:
                K.w_tm = sb(wide, "w_tm", [P, KD, TM_COLS])
                modulation(nc, ctx, K)
                token_projection(nc, ctx, K)
            K.qkv = sb(mix, "qkv", [P, FT_A, TOK])
            K.rows = sb(mix, "rows", [P, TOK])
            K.gr = sb(mix, "gr", [H_A, TOK])
            K.tm = sb(mix, "tm", [P, NT + 1, 4, H_A])
            K.ec = sb(mix, "ec", [P, 2, NT + 1, H_A])
            K.gl = sb(mix, "gl", [P, PAIRS, 16])
            with ExitStack() as group_c:
                K.qkc = sb(group_c, "qkc", [P, FT_C, TOK])
                K.nd = sb(group_c, "nd", [H_C, TOK])
                feature_projection(nc, ctx, K)
                forgetting_attention(nc, ctx, K)
                cached_attention(nc, ctx, K)
            delta_rule(nc, ctx, K)
        output_projection(nc, ctx, K)
        with ExitStack() as ffn:
            yT = sb(ffn, "yT", [P, KF, TOK])
            ffn_up(nc, ctx, K, yT)
            ffn_down(nc, ctx, K, yT)


OUTS = {
    "y": (TOK, D), "v": (TOK, W_C), "chunk_v": (NSAMP, W_B), "p_gconv": (P, FT_A, TAPS_A - 1),
    "s_gconv": (P, FT_A, NBATCH, TAPS_A - 1), "k": (P, PAIRS, TOK), "logf": (H_C, TOK), "p_S": (P, PAIRS, HD),
    "s_S": (P, PAIRS, NBATCH, HD), "p_fconv": (P, 2 * KF, TAPS_F - 1), "s_fconv": (P, 2 * KF, NBATCH, TAPS_F - 1),
}


def kernel(**inputs):
    import concourse.bacc as bacc
    from concourse.bass_utils import run_bass_kernel_spmd

    a = {n: np.asarray(v) for n, v in inputs.items()}
    tile = lambda w: np.ascontiguousarray(w.reshape(KD, P, -1, P).transpose(2, 1, 0, 3))
    part = lambda v: v.reshape(-1, P).T
    w_in = a["w_in"][0]
    o = np.cumsum([0, 3 * W_A, H_A, H_A, W_A, 2 * W_B, W_C, W_C, W_C, H_C])
    qkv_a, beta, decay, gate, uv, qc, kc, vc, forget = (w_in[:, o[i]:o[i + 1]] for i in range(9))
    narrow = np.zeros((D, P), np.float32)
    narrow[:, 0:H_A], narrow[:, 32:32 + H_A], narrow[:, 64:64 + H_C] = beta, decay, forget
    bias = np.zeros((P, 2), np.float32)
    bias[32:32 + H_A, 0], bias[64:64 + H_C, 0] = a["gdn_dt_bias"][0], a["fox_f_bias"][0]
    bias[32:32 + H_A, 1] = a["gdn_A_log"][0]
    ws = a["chunk_w_s"][0]
    bs = np.zeros((P, 2, G_B), np.float32)
    bs[:, 0], bs[:NSAMP, 1] = a["chunk_b_s"][0].T, np.tile(a["chunk_b_s"][0][:, :SSEQ].T, (NBATCH, 1))
    up = a["w_up"][0].reshape(D, 2, KF, P).transpose(0, 2, 1, 3).reshape(D, 2 * D_FF)
    turn = lambda v: v.reshape(*v.shape[:-1], 2, KF, P).swapaxes(-3, -2).reshape(v.shape)
    conv = lambda w: np.ascontiguousarray(w.reshape(w.shape[0], -1, P).transpose(2, 1, 0))
    before = lambda s: np.ascontiguousarray(s.reshape(*s.shape[:2], -1, P).transpose(3, 2, 0, 1))
    arrays = {
        "x": np.concatenate([a["x_prompt"][0], a["x_sample"].reshape(NSAMP, D)]),
        "cT": np.concatenate([a["c_prompt"], a["c_sample"]]).reshape(NSEQ, KD, P).transpose(2, 1, 0),
        "w_ada": a["w_ada"][0].reshape(KD, P, NGRP, 512).transpose(2, 1, 0, 3),
        "b_ada": a["b_ada"].reshape(NGRP, 512),
        "cst": constants(), "reset": reset_rows(),
        "gpre": np.stack([part(a["g_pre_mix"][0]), part(a["g_pre_ffn"][0])], 1),
        "gpost": np.concatenate([a["g_post_mix"], a["g_post_ffn"]]),
        "w_tm": np.concatenate([gate, uv, vc], 1).reshape(KD, P, TM_COLS).transpose(1, 0, 2),
        "gn": a["gdn_norm_g"], "lng": a["chunk_ln_g"], "lnb": a["chunk_ln_b"],
        "wsT": ws.transpose(2, 0, 1),
        "wsT8": np.tile(ws[:, :SSEQ, :SSEQ].transpose(2, 0, 1), (NBATCH, 1, NBATCH)),
        "bs": bs,
        "w_fm": tile(np.concatenate([qkv_a, qc, kc, narrow], 1)),
        "gprev": before(a["state_gdn_conv"][0]), "gconv": conv(a["gdn_conv_w"][0]), "bias": bias,
        "page_table": a["page_table"].reshape(1, -1),
        "ckT": a["cache_fox_k"][0].reshape(NPOOL, PAGE, PAIRS, P).transpose(0, 3, 2, 1),
        "cv": a["cache_fox_v"][0].reshape(NPOOL, PAGE, W_C),
        "clf": a["cache_fox_logf"][0].transpose(0, 2, 1),
        "s0": a["state_gdn_S"][0].reshape(NBATCH, PAIRS, P, HD).transpose(2, 1, 0, 3),
        "w_out": a["w_out"][0].reshape(KD, P, D).transpose(1, 0, 2),
        "w_up": tile(up), "fprev": before(turn(a["state_ffn_conv"][0])), "fconv": conv(turn(a["ffn_conv_w"][0])),
        "w_down": a["w_down"][0].reshape(KF, P, D),
    }
    nc = bacc.Bacc("TRN2", target_bir_lowering=False, num_devices=1)
    A, O, feed = {}, {}, {}
    for name, v in arrays.items():
        v = np.ascontiguousarray(v)
        feed[f"in_{name}"] = v
        A[name] = nc.dram_tensor(f"in_{name}", v.shape, mybir.dt.from_np(v.dtype), kind="ExternalInput").ap()
    for name, shape in OUTS.items():
        O[name] = nc.dram_tensor(f"out_{name}", shape, F32, kind="ExternalOutput").ap()
    build(nc, A, O)
    r = run_bass_kernel_spmd(nc, [feed], core_ids=[0]).results[0]
    r = {n: np.asarray(r[f"out_{n}"]) for n in OUTS}

    rows = lambda v: v.transpose(2, 1, 0).reshape(1, 1, v.shape[2], -1)
    srows = lambda v: v.transpose(2, 3, 1, 0).reshape(1, NBATCH, v.shape[3], -1)
    back = lambda v: v.reshape(*v.shape[:-1], KF, 2, P).swapaxes(-3, -2).reshape(v.shape)
    k = r["k"].transpose(2, 1, 0).reshape(TOK, H_C, HD)
    v = r["v"].reshape(TOK, H_C, HD)
    lf = r["logf"].T
    c = lambda v: np.ascontiguousarray(v)
    pg, smp = (1, 1, NT, P), (1, NBATCH, SSEQ)
    return (
        r["y"][:SEQ].reshape(1, SEQ, D), r["y"][SEQ:].reshape(NBATCH, SSEQ, D),
        c(rows(r["p_gconv"])), c(r["p_S"].transpose(1, 0, 2).reshape(1, 1, H_A, HD, HD)),
        c(k[:SEQ].reshape(*pg, H_C, HD)), c(v[:SEQ].reshape(*pg, H_C, HD)), c(lf[:SEQ].reshape(*pg, H_C)),
        c(back(rows(r["p_fconv"]))),
        c(srows(r["s_gconv"])), c(r["s_S"].transpose(2, 1, 0, 3).reshape(1, NBATCH, H_A, HD, HD)),
        c(k[SEQ:].reshape(*smp, H_C, HD)), c(v[SEQ:].reshape(*smp, H_C, HD)), c(lf[SEQ:].reshape(*smp, H_C)),
        c(r["chunk_v"].reshape(*smp, W_B)), c(back(srows(r["s_fconv"]))),
    )
```

```python
from contextlib import ExitStack

import concourse.bass as bass
import numpy as np
from concourse import mybir

F32 = mybir.dt.float32
BF16 = mybir.dt.bfloat16
F32R = mybir.dt.float32r
I32 = mybir.dt.int32
ACT = mybir.ActivationFunctionType
ALU = mybir.AluOpType
AX = mybir.AxisListType

P = 128
D = 1024
KD = D // P
SEQ = 1024
NT = SEQ // P
NBATCH = 8
SSEQ = 8
NSAMP = NBATCH * SSEQ
TOK = SEQ + NSAMP
HD = 64
H_A, G_B, H_C = 6, 4, 6
W_A, W_B, W_C = H_A * HD, G_B * HD, H_C * HD
PAIRS = H_A // 2
PAGE = 128
NPAGE = 2
NPOOL = 20
PAST = NPAGE * PAGE
D_FF = 2816
KF = D_FF // P
TAPS_A, TAPS_F = 4, 3
EPS = 1e-6
NSEQ = 1 + NBATCH
NGRP = 6 * D // 512
LEVELS = 7
FT_A = 3 * W_A // P
FT_C = 2 * W_C // P
FT = FT_A + FT_C + 1
TM_COLS = W_A + 2 * W_B + W_C
THIRD = 364
REST = SEQ - 2 * THIRD
NEG = -1e30

C_ID = 0
C_MASK = C_ID + P
C_TRI = C_MASK + P
C_LVL = C_TRI + P
C_TRI8 = C_LVL + LEVELS * P
C_HEAD = C_TRI8 + NSAMP
C_PAIR = C_HEAD + H_A * P
C_ROW48 = C_PAIR + PAIRS * P
C_CAUS = C_ROW48 + H_C * SSEQ
C_OWN = C_CAUS + NBATCH * NSAMP
C_PICK = C_OWN + W_C
C_BLK = C_PICK + SSEQ
C_HALF = C_BLK + NBATCH
C_END = C_HALF + 2


def constants():
    c = np.zeros((P, C_END), np.float32)
    c[:, C_MASK:C_MASK + P] = np.where(np.arange(P)[None, :] <= np.arange(P)[:, None], 0.0, NEG)
    i, j = np.arange(P)[:, None], np.arange(P)[None, :]
    c[:, C_ID:C_ID + P] = i == j
    c[:, C_TRI:C_TRI + P] = j >= i
    for n in range(LEVELS):
        s = 1 << n
        c[:, C_LVL + n * P:C_LVL + (n + 1) * P] = ((j // s) % 2 == 1) & (i // s == j // s - 1)
    c[:, C_TRI8:C_TRI8 + NSAMP] = ((j >= i) & (j // SSEQ == i // SSEQ))[:, :NSAMP]
    for q in range(4):
        for h in range(H_A):
            c[32 * q + h, C_HEAD + h * P:C_HEAD + (h + 1) * P] = 1
            o = C_PAIR + (h // 2) * P + (h % 2) * HD
            c[32 * q + h, o:o + HD] = 1
            c[32 * q + h, C_ROW48 + h * SSEQ:C_ROW48 + (h + 1) * SSEQ] = 1
    for h in range(H_C):
        for q in range(SSEQ):
            r = h * SSEQ + q
            caus = np.full((NBATCH, NBATCH, SSEQ), NEG, np.float32)
            for b in range(NBATCH):
                caus[b, b, :q + 1] = 0
            c[r, C_CAUS:C_CAUS + NBATCH * NSAMP] = caus.reshape(-1)
            c[r, C_OWN + h * HD:C_OWN + (h + 1) * HD] = 1
            c[r, C_PICK + q] = 1
    for t in range(NSAMP):
        c[t, C_BLK + t // SSEQ] = 1
    c[0:HD, C_HALF] = c[HD:P, C_HALF + 1] = 1
    return c


def reset_rows():
    r = np.ones((2 * H_A, TOK), np.float32)
    r[:H_A, 0:SEQ:P] = 0
    r[:, SEQ::SSEQ] = 0
    r[H_A:, 0] = 0
    return r


class Chain:

    def __init__(self, eng, sem, base=0):
        self.eng, self.sem, self.base, self.n = eng, sem, base, 0

    def link(self, ins, K=None):
        self.n += 1
        ins.then_inc(self.sem, 1)
        if K:
            wait_apart(self.eng, K, (self.sem, self.base + self.n))
        else:
            self.eng.wait_ge(self.sem, self.base + self.n)


def wait_apart(eng, K, *waits):
    waits = [(sem, n if isinstance(n, int) else eng.snap(eng.to_reg(n))) for sem, n in waits]
    eng.wait_ge(K.cst_in, 32)
    for sem, n in waits:
        eng.wait_ge(sem, n)


def after(eng, sem, n):
    if not (isinstance(n, int) and n <= 0):
        eng.wait_ge(sem, n)


def stage_semaphores(nc, own):
    taken = []

    def clear():
        nc.clear_and_free_semaphores(taken)
        nc.all_engine_barrier()

    own.callback(clear)

    def sem(name, ahead=0):
        taken.append(nc.alloc_semaphore(name=name))
        if ahead:
            nc.sync.sem_inc(taken[-1], ahead)
        return taken[-1]

    return sem


def flat(ap):
    return ap.rearrange("p a n -> p (a n)")


class Kernel:
    pass


def modulation(nc, ctx, K):
    with ExitStack() as own:
        sem = stage_semaphores(nc, own)
        sb = lambda n, s, d=F32: own.enter_context(nc.sbuf_tensor(n, s, d))
        wa = sb("wa", [P, 2, KD, 512])
        ba = sb("ba", [1, 2, 512])
        ones = sb("mod_ones", [1, NSEQ])
        cT = sb("cT", [P, KD, NSEQ])
        csT = sb("csT", [P, KD, NSEQ])
        mr = sb("mr", [NSEQ, 2, 512])
        modT = sb("modT", [P, 6 * KD, NSEQ])
        ps = [own.enter_context(nc.psum_tensor(f"mod_ps{i}", [P, 512], F32)) for i in range(2)]
        psT = own.enter_context(nc.psum_tensor("mod_psT", [P, 512], F32))
        c_in, c_silu = sem("c_in"), sem("c_silu")
        wa_in = [sem("wa_in0"), sem("wa_in1")]
        mod_mm, mod_out, modT_mm, modT_out = sem("mod_mm"), sem("mod_out"), sem("modT_mm"), sem("modT_out")
        scr_out = [sem("scr_out0"), sem("scr_out1")]
        g_done, ones_set = sem("g_done"), sem("mod_ones_set")
        block = own.enter_context(nc.Block())

        @block.sync
        def _(sp):
            sp.dma_start(cT[:], K.cT).then_inc(c_in, 16)

            def load(g, k):
                sp.dma_start(wa[:, k], K.w_ada[bass.ds(g, 1)].rearrange("a p k n -> (a p) k n")).then_inc(wa_in[k], 16)
                sp.dma_start(ba[:, k], K.b_ada[bass.ds(g, 1)]).then_inc(wa_in[k], 16)

            for k in range(2):
                load(k, k)
            sp.dma_start(K.cst[:], K.cst_d).then_inc(K.cst_in, 16)
            sp.dma_start(K.gpre[:], K.gpre_d).then_inc(K.cst_in, 16)
            with sp.Fori(1, NGRP // 2) as i:
                for k in range(2):
                    sp.wait_ge(mod_mm, 2 * i + k - 1)
                    load(2 * i + k, k)
            sp.dma_start(K.w_tm[:], K.w_tm_d).then_inc(K.w_tm_in, 16)

        @block.gpsimd
        def _(pool):
            pool.memset(ones[:], 1.0).then_inc(ones_set, 1)
            with pool.Fori(0, NGRP // 2) as i:
                for k in range(2):
                    pool.wait_ge(mod_out, 2 * i + k + 1)
                    pool.dma_start(K.scr[:, bass.ds((2 * i + k) * 512, 512)], mr[:, k]).then_inc(scr_out[k], 16)
            for k in range(2):
                pool.wait_ge(scr_out[k], 16 * (NGRP // 2))

        @block.tensor
        def _(pe):
            def project(g, k, first):
                pe.wait_ge(wa_in[k], 16 * (g - k) + 32)
                if not first:
                    pe.wait_ge(mod_out, g - 1)
                for kk in range(KD):
                    pe.matmul(ps[k][0:NSEQ, :], csT[:, kk, :], wa[:, k, kk, :], start=(kk == 0), stop=False)
                pe.matmul(ps[k][0:NSEQ, :], ones[:], ba[:, k, :], start=False, stop=True).then_inc(mod_mm, 1)

            def turn(g, k, first=False):
                wait_apart(pe, K, (mod_out, g + 1), *([] if first else [(modT_out, g)]))
                for c in range(4):
                    last = pe.transpose(psT[:, c * NSEQ:(c + 1) * NSEQ], mr[:, k, c * P:(c + 1) * P],
                                        K.ident[0:NSEQ, 0:NSEQ])
                last.then_inc(modT_mm, 1)

            pe.wait_ge(c_silu, 1)
            pe.wait_ge(ones_set, 1)
            project(0, 0, True)
            project(1, 1, True)
            pe.wait_ge(K.cst_in, 32)
            turn(0, 0, True)
            with pe.Fori(1, NGRP // 2) as i:
                for k in range(2):
                    project(2 * i + k, k, False)
                    turn(2 * i + k - 1, 1 - k)
            turn(NGRP - 1, 1)

        @block.scalar
        def _(act):
            act.wait_ge(c_in, 16)
            act.activation(csT[:], cT[:], ACT.Silu).then_inc(c_silu, 1)

            def evict(g, k, first):
                act.wait_ge(mod_mm, g + 1)
                if not first:
                    act.wait_ge(modT_mm, g - 1)
                    act.wait_ge(scr_out[k], 8 * (g - k))
                act.activation(mr[:, k], ps[k][0:NSEQ, :], ACT.Copy).then_inc(mod_out, 1)

            evict(0, 0, True)
            evict(1, 1, True)
            with act.Fori(1, NGRP // 2) as i:
                for k in range(2):
                    evict(2 * i + k, k, False)

        @block.vector
        def _(dve):
            with dve.Fori(0, NGRP) as g:
                dve.wait_ge(modT_mm, g + 1)
                dve.tensor_copy(modT[:, bass.ds(4 * g, 4), :],
                                psT[:, 0:4 * NSEQ].rearrange("p (c n) -> p c n", c=4)).then_inc(modT_out, 1)
            dve.wait_ge(modT_out, NGRP)
            dve.wait_ge(K.cst_in, 32)
            for n, (shift, scale) in enumerate(((0, 1), (3, 4))):
                dve.scalar_tensor_tensor(
                    K.gain[:, n], modT[:, scale * KD:(scale + 1) * KD, :], 1.0,
                    K.gpre[:, n, :].unsqueeze(2).broadcast_to([P, KD, NSEQ]), ALU.add, ALU.mult).then_inc(g_done, 1)
                dve.tensor_copy(K.shift[:, n], modT[:, shift * KD:(shift + 1) * KD, :]).then_inc(g_done, 1)
            dve.wait_ge(g_done, 4)



def gain_shift(dve, K, n, psx, out, rows):
    if rows == P:
        for k in range(KD):
            last = dve.tensor_scalar(out[:, k, 0:P], psx[:, k, :], K.gain[:, n, k, 0:1], K.shift[:, n, k, 0:1],
                                     ALU.mult, ALU.add)
        return [last]
    steps = []
    for k in range(0, KD, 4):
        o = out[:, k:k + 4, 0:NSAMP].rearrange("p k (b s) -> p k b s", s=SSEQ)
        x = psx[:, k:k + 4, 0:NSAMP].rearrange("p k (b s) -> p k b s", s=SSEQ)
        for kk in range(4):
            g = K.gain[:, n, k + kk, 1:NSEQ].unsqueeze(2).broadcast_to([P, NBATCH, SSEQ])
            steps.append((o[:, kk], x[:, kk], g, ALU.mult))
    for k in range(KD):
        o = out[:, k, 0:NSAMP].rearrange("p (b s) -> p b s", s=SSEQ)
        s = K.shift[:, n, k, 1:NSEQ].unsqueeze(2).broadcast_to([P, NBATCH, SSEQ])
        steps.append((o, o, s, ALU.add))
    return steps


def token_projection(nc, ctx, K):
    with ExitStack() as own:
        sem = stage_semaphores(nc, own)
        sb = lambda n, s, d=F32: own.enter_context(nc.sbuf_tensor(n, s, d))
        xt = sb("tp_x", [P, 2, D])
        junk = sb("tp_junk", [P, D])
        hs = sb("tp_hs", [P, 2, KD, P])
        uv = sb("tp_uv", [P, 2, 2 * W_B])
        ss = sb("tp_ss", [P, 2, 4])
        mhalf = sb("tp_mhalf", [P, 1])
        st = sb("tp_st", [P, 6])
        mv = sb("tp_mv", [P, 4])
        gn = sb("tp_gn", [P, HD])
        lng = sb("tp_lng", [P, W_B])
        lnb = sb("tp_lnb", [P, W_B])
        wsT = sb("tp_wsT", [P, G_B, P])
        wsT8 = sb("tp_wsT8", [NSAMP, G_B, NSAMP])
        bs = sb("tp_bs", [P, 2, G_B])
        psX = own.enter_context(nc.psum_tensor("tp_psX", [P, KD, P], F32))
        psG = own.enter_context(nc.psum_tensor("tp_psG", [P, 512], F32))
        psU = own.enter_context(nc.psum_tensor("tp_psU", [P, 512], F32))
        psV = own.enter_context(nc.psum_tensor("tp_psV", [P, 512], F32))
        psM = own.enter_context(nc.psum_tensor("tp_psM", [P, 512], F32))
        x_in = [sem("x_in0"), sem("x_in1")]
        small_in = sem("tp_small_in")
        sumsq, ms_set, r_set, xn_set, x_turned = sem("sumsq"), sem("ms_set"), sem("r_set"), sem("xn_set"), sem("x_turned")
        h_set, h_chain, h_copied = sem("h_set"), sem("h_chain"), sem("h_copied")
        uv_mm, gate_mm, vc_mm, mix_mm = sem("uv_mm"), sem("gate_mm"), sem("vc_mm"), sem("mix_mm")
        uv_set, gate_set, vc_set = sem("uv_set"), sem("gate_set"), sem("vc_set")
        ln_chain, ln_var, ln_v, ln_r, vln_set, ob_set = (sem("ln_chain"), sem("ln_var"), sem("ln_v"), sem("ln_r"),
                                                         sem("vln_set"), sem("ob_set"))
        half_set, ws_set, v_out, cv_out = sem("half_set"), sem("ws_set"), sem("v_out"), sem("cv_out")
        block = own.enter_context(nc.Block())

        @block.sync
        def _(sp):
            def load(t, k, rows=P):
                sp.dma_start(xt[0:rows, k], K.x[bass.ds(t * P, rows)]).then_inc(x_in[k], 16)

            load(0, 0)
            for dst, src in ((gn[:], K.gn_d.broadcast_to([P, HD])), (lng[:], K.lng_d.broadcast_to([P, W_B])),
                             (lnb[:], K.lnb_d.broadcast_to([P, W_B])), (wsT[:], K.wsT_d), (wsT8[:], K.wsT8_d),
                             (bs[:], K.bs_d)):
                sp.dma_start(dst, src).then_inc(small_in, 16)
            load(1, 1)

            def step(t, k, rows, nxt):
                if nxt:
                    sp.wait_ge(x_turned, t + 1)
                    load(t + 2, k, nxt)
                sp.wait_ge(vc_set, t + 1)
                sp.dma_start(K.v_out[bass.ds(t * P, rows)], K.vc[0:rows, bass.ds(t, 1)].rearrange("p a n -> p (a n)"))\
                    .then_inc(v_out, 16)

            with sp.Fori(0, NT // 2 - 1) as i:
                for k in range(2):
                    step(2 * i + k, k, P, P)
            step(NT - 2, 0, P, NSAMP)
            step(NT - 1, 1, P, 0)
            step(NT, 0, NSAMP, 0)
            sp.wait_ge(vln_set, NT + 1)
            sp.dma_start(K.chunk_v, uv[0:NSAMP, 0, W_B:2 * W_B]).then_inc(cv_out, 16)
            sp.wait_ge(cv_out, 16)
            sp.wait_ge(v_out, 16 * (NT + 1))

        def tiles(eng, stage, step):
            stage(0, 0, P)
            step(0, 0, P, P)
            step(1, 1, P, P)
            with eng.Fori(1, NT // 2 - 1) as i:
                for k in range(2):
                    step(2 * i + k, k, P, P)
            step(NT - 2, 0, P, P)
            step(NT - 1, 1, P, NSAMP)
            step(NT, 0, NSAMP, 0)

        @block.gpsimd
        def _(pool):
            pool.memset(mhalf[:], -0.5).then_inc(half_set, 1)
            pool.wait_ge(small_in, 96)
            pool.tensor_tensor(wsT[:], wsT[:], K.tri.unsqueeze(1).broadcast_to([P, G_B, P]), ALU.mult).then_inc(ws_set, 1)
            pool.tensor_tensor(wsT8[:], wsT8[:], K.tri8.unsqueeze(1).broadcast_to([NSAMP, G_B, NSAMP]), ALU.mult)\
                .then_inc(ws_set, 1)
            pool.wait_ge(half_set, 1)

            def stage(t, k, rows):
                wait_apart(pool, K, (sumsq, t + 1))
                pool.tensor_scalar(ss[0:rows, k, 1:2], ss[0:rows, k, 0:1], 1.0 / D, EPS, ALU.mult, ALU.add).then_inc(ms_set, 1)
                pool.wait_ge(ms_set, t + 1)
                pool.tensor_tensor(ss[0:rows, k, 2:3], ss[0:rows, k, 1:2], mhalf[0:rows], ALU.pow).then_inc(r_set, 1)

            def copy_h(t, k, rows):
                pool.wait_ge(h_set, t + 1)
                pool.tensor_copy(K.hT[:, :, bass.ds(t * P, rows)], hs[:, k, :, 0:rows]).then_inc(h_copied, 1)

            def step(t, k, rows, nxt):
                if nxt:
                    stage(t + 1, 1 - k, nxt)
                wait_apart(pool, K, (ln_var, t + 1))
                pool.tensor_scalar(mv[0:rows, 2:3], mv[0:rows, 1:2], EPS, None, ALU.add).then_inc(ln_v, 1)
                pool.wait_ge(ln_v, t + 1)
                pool.tensor_tensor(mv[0:rows, 3:4], mv[0:rows, 2:3], mhalf[0:rows], ALU.pow).then_inc(ln_r, 1)
                copy_h(t, k, rows)

            tiles(pool, stage, step)

        @block.scalar
        def _(act):
            def stage(t, k, rows):
                act.wait_ge(x_in[k], 8 * (t - k) + 16)
                act.activation(junk[0:rows], xt[0:rows, k], ACT.Square, accum_out=ss[0:rows, k, 0:1]).then_inc(sumsq, 1)
                act.wait_ge(r_set, t + 1)
                act.activation(xt[0:rows, k], xt[0:rows, k], ACT.Copy, scale=ss[0:rows, k, 2:3]).then_inc(xn_set, 1)

            def step(t, k, rows, nxt):
                if nxt:
                    stage(t + 1, 1 - k, nxt)
                act.wait_ge(uv_mm, t + 1)
                after(act, ob_set, t - 1)
                act.activation(uv[0:rows, k], psU[0:rows, :], ACT.Gelu_apprx_tanh).then_inc(uv_set, 1)
                act.wait_ge(gate_mm, t + 1)
                act.activation(K.tok[0:rows, bass.ds(t, 1), 0:W_A].rearrange("p a n -> p (a n)"), psG[0:rows, 0:W_A],
                               ACT.Silu).then_inc(gate_set, 1)
                act.wait_ge(vc_mm, t + 1)
                act.activation(K.vc[0:rows, bass.ds(t, 1)].rearrange("p a n -> p (a n)"), psV[0:rows, 0:W_C],
                               ACT.Copy).then_inc(vc_set, 1)

            tiles(act, stage, step)

        @block.vector
        def _(dve):
            def stage(t, k, rows):
                dve.wait_ge(x_turned, t + 1)
                after(dve, vc_mm, t - 1)
                after(dve, h_copied, t - 1)
                made = gain_shift(dve, K, 0, psX, hs[:, k], rows)
                if rows == P:
                    made[0].then_inc(h_set, 1)
                else:
                    chain = Chain(dve, h_chain)
                    half = len(made) // 2
                    for n, (o, a, b, op) in enumerate(made):
                        ins = dve.tensor_tensor(o, a, b, op)
                        if n == half - 1:
                            chain.link(ins)
                    ins.then_inc(h_set, 1)

            def step(t, k, rows, nxt):
                if nxt:
                    stage(t + 1, 1 - k, nxt)
                chain = Chain(dve, ln_chain, t * 4)
                v = uv[0:rows, k, W_B:2 * W_B]
                dve.wait_ge(uv_set, t + 1)
                chain.link(dve.bn_stats(st[0:rows], v), K)
                dve.bn_aggr(mv[0:rows, 0:2], st[0:rows]).then_inc(ln_var, 1)
                gate = K.tok[0:rows, bass.ds(t, 1), 0:W_A].rearrange("p a (h d) -> p (a h) d", d=HD)
                dve.wait_ge(gate_set, t + 1)
                dve.tensor_tensor(gate, gate, gn[0:rows].unsqueeze(1).broadcast_to([rows, H_A, HD]), ALU.mult)
                dve.wait_ge(ln_r, t + 1)
                chain.link(dve.tensor_scalar(v, v, mv[0:rows, 0:1], mv[0:rows, 3:4], ALU.subtract, ALU.mult))
                chain.link(dve.tensor_tensor(v, v, lng[0:rows], ALU.mult))
                dve.tensor_tensor(v, v, lnb[0:rows], ALU.add).then_inc(vln_set, 1)
                ob = K.tok[0:rows, bass.ds(t, 1), W_A:W_A + W_B].rearrange("p a n -> p (a n)")
                b = bs[0:rows, 0 if rows == P else 1, :].unsqueeze(2).broadcast_to([rows, G_B, HD])
                dve.wait_ge(mix_mm, t + 1)
                chain.link(dve.tensor_tensor(ob.rearrange("p (g d) -> p g d", g=G_B),
                                             psM[0:rows, 0:W_B].rearrange("p (g d) -> p g d", g=G_B), b, ALU.add))
                dve.tensor_tensor(ob, ob, uv[0:rows, k, 0:W_B], ALU.mult).then_inc(ob_set, 1)

            dve.wait_ge(small_in, 96)
            tiles(dve, stage, step)

        @block.tensor
        def _(pe):
            def stage(t, k, rows):
                pe.wait_ge(xn_set, t + 1)
                after(pe, h_set, t)
                for kk in range(KD):
                    last = pe.transpose(psX[:, kk, 0:rows], xt[0:rows, k, kk * P:(kk + 1) * P],
                                        K.ident[0:rows, 0:rows])
                last.then_inc(x_turned, 1)

            def gemm(ps, k, rows, c0, n, sem_):
                for kk in range(KD):
                    last = pe.matmul(ps[0:rows, 0:n], hs[:, k, kk, 0:rows], K.w_tm[:, kk, c0:c0 + n],
                                     start=(kk == 0), stop=(kk == KD - 1))
                last.then_inc(sem_, 1)

            def step(t, k, rows, nxt):
                pe.wait_ge(h_set, t + 1)
                after(pe, uv_set, t)
                gemm(psU, k, rows, W_A, 2 * W_B, uv_mm)
                if nxt:
                    stage(t + 1, 1 - k, nxt)
                after(pe, gate_set, t)
                gemm(psG, k, rows, 0, W_A, gate_mm)
                after(pe, vc_set, t)
                gemm(psV, k, rows, W_A + 2 * W_B, W_C, vc_mm)
                pe.wait_ge(vln_set, t + 1)
                after(pe, ob_set, t)
                for g in range(G_B):
                    w = wsT[:, g, :] if rows == P else wsT8[:, g, :]
                    last = pe.matmul(psM[0:rows, g * HD:(g + 1) * HD], w,
                                     uv[0:rows, k, W_B + g * HD:W_B + (g + 1) * HD], start=True, stop=True)
                last.then_inc(mix_mm, 1)

            pe.wait_ge(K.w_tm_in, 16)
            pe.wait_ge(ws_set, 2)
            tiles(pe, stage, step)


def feature_projection(nc, ctx, K):
    with ExitStack() as own:
        sem = stage_semaphores(nc, own)
        sb = lambda n, s, d=F32: own.enter_context(nc.sbuf_tensor(n, s, d))
        RING = 4
        wf = sb("fp_w", [P, RING, KD, P])
        zp = sb("fp_zp", [P, 2, TAPS_A - 1 + SEQ])
        zs = sb("fp_zs", [P, 2, NBATCH, TAPS_A - 1 + SSEQ])
        prev = sb("fp_prev", [P, FT_A, NBATCH, TAPS_A - 1])
        cw = sb("fp_cw", [P, FT_A, TAPS_A])
        pst = sb("fp_pst", [P, FT_A, TAPS_A - 1])
        sst = sb("fp_sst", [P, FT_A, NBATCH, TAPS_A - 1])
        bias = sb("fp_bias", [P, 2])
        nexpA = sb("fp_nexpA", [P, 1])
        reset = sb("fp_reset", [P, TOK])
        rowx = sb("fp_rowx", [P, TOK])
        rowe = sb("fp_rowe", [P, TOK])
        logf = sb("fp_logf", [P, TOK])
        ps = [own.enter_context(nc.psum_tensor(f"fp_ps{i}", [P, 3, 512], F32)) for i in range(2)]
        psR = own.enter_context(nc.psum_tensor("fp_psR", [P, 512], F32))
        w_in = [sem(f"fp_w_in{k}") for k in range(RING)]
        small_in, fm_mm, fm_out, halo_set = sem("fp_small_in"), sem("fm_mm"), sem("fm_out"), sem("halo_set")
        conv_chain, conv_set, silu_set, st_copied, st_out = (sem("conv_chain"), sem("conv_set"), sem("silu_set"),
                                                             sem("st_copied"), sem("st_out"))
        zero_set, row_act, row_dve, row_mm, row_tm, fin = (sem("zero_set"), sem("row_act"), sem("row_dve"), sem("row_mm"),
                                                           sem("row_tm"), sem("fp_fin"))
        k_out = sem("k_out")
        block = own.enter_context(nc.Block())

        @block.sync
        def _(sp):
            for k in range(RING):
                sp.dma_start(wf[:, k], K.w_fm_d[k]).then_inc(w_in[k], 16)
            for dst, src in ((prev[:], K.gprev_d), (cw[:], K.gconv_d), (bias[:], K.bias_d), (reset[32:32 + H_A], K.reset_d[0:H_A]),
                             (reset[64:64 + H_A], K.reset_d[H_A:])):
                sp.dma_start(dst, src).then_inc(small_in, 16)
            with sp.Fori(1, FT // RING) as i:
                for k in range(RING):
                    sp.wait_ge(fm_mm, RING * (i - 1) + k + 1)
                    sp.dma_start(wf[:, k], K.w_fm_d[bass.ds(RING * i + k, 1)].rearrange("a p k n -> (a p) k n"))\
                        .then_inc(w_in[k], 16)
            sp.wait_ge(st_copied, 2 * FT_A)
            sp.dma_start(K.p_gconv, pst[:]).then_inc(st_out, 16)
            sp.dma_start(K.s_gconv, sst[:]).then_inc(st_out, 16)
            sp.wait_ge(fm_out, FT)
            sp.dma_start(K.k_out, K.qkc[:, PAIRS:2 * PAIRS]).then_inc(k_out, 16)
            sp.wait_ge(row_dve, 9)
            sp.dma_start(K.logf_out, logf[64:64 + H_C]).then_inc(k_out, 16)
            sp.wait_ge(st_out, 32)
            sp.wait_ge(k_out, 32)

        @block.tensor
        def _(pe):
            def tile(i, slot, turn):
                pe.wait_ge(w_in[slot], 4 * (i - slot) + 16)
                after(pe, fm_out, i - 1)
                for kk in range(KD):
                    for n, (c, w) in enumerate(((0, 512), (512, 512), (SEQ, NSAMP))):
                        last = pe.matmul(ps[turn][:, n, 0:w], wf[:, slot, kk, :], K.hT[:, kk, c:c + w],
                                         start=(kk == 0), stop=(kk == KD - 1))
                last.then_inc(fm_mm, 1)

            for i in range(RING):
                tile(i, i, i % 2)
            with pe.Fori(1, FT // RING) as i:
                for k in range(RING):
                    tile(RING * i + k, k, k % 2)
            pe.wait_ge(row_dve, 9)
            for t in range(NT + 1):
                n = P if t < NT else NSAMP
                after(pe, row_tm, t)
                pe.transpose(psR[0:n, 0:P], K.rows[:, t * P:t * P + n], K.ident).then_inc(row_mm, 1)
            pe.wait_ge(row_tm, NT + 1)
            for j in range(PAIRS):
                w = K.cst[32:32 + H_A, C_PAIR + j * P:C_PAIR + (j + 1) * P]
                pe.matmul(psR[:, 16 * j:16 * j + NT], w, K.rows[32:32 + H_A, P - 1:SEQ:P], start=True, stop=True)
                last = pe.matmul(psR[:, 16 * j + 8:16 * j + 16], w, K.rows[32:32 + H_A, SEQ + SSEQ - 1:TOK:SSEQ],
                                 start=True, stop=True)
            last.then_inc(row_mm, 1)

        @block.gpsimd
        def _(pool):
            for k in range(2):
                pool.memset(zp[:, k, 0:TAPS_A - 1], 0.0).then_inc(zero_set, 1)
            pool.wait_ge(zero_set, 2)
            pool.memset(K.tm[NSAMP:P, NT], 0.0).then_inc(zero_set, 1)
            pool.wait_ge(zero_set, 3)
            pool.wait_ge(small_in, 80)

            def tile(i, k):
                after(pool, conv_set, i - 1)
                pool.tensor_copy(zs[:, k, :, 0:TAPS_A - 1], prev[:, bass.ds(i, 1)].rearrange("p a b n -> p (a b) n"))\
                    .then_inc(halo_set, 1)
                pool.wait_ge(fm_out, i + 2)
                pool.tensor_copy(flat(pst[:, bass.ds(i, 1)]), zp[:, k, SEQ:SEQ + TAPS_A - 1]).then_inc(st_copied, 1)
                pool.tensor_copy(sst[:, bass.ds(i, 1)].rearrange("p a b n -> p (a b) n"), zs[:, k, :, SSEQ:])\
                    .then_inc(st_copied, 1)

            tile(0, 0)
            tile(1, 1)
            with pool.Fori(1, FT_A // 2) as i:
                for k in range(2):
                    tile(2 * i + k, k)
            tile(FT_A - 1, 0)

        @block.scalar
        def _(act):
            act.wait_ge(zero_set, 3)

            def evict(i, k):
                act.wait_ge(fm_mm, i + 2)
                after(act, conv_set, i - 1)
                after(act, st_copied, 2 * (i - 1))
                act.activation(zp[:, k, TAPS_A - 1:], ps[1 - k][:, 0:2, :].rearrange("p a n -> p (a n)"), ACT.Copy)
                act.activation(zs[:, k, :, TAPS_A - 1:], ps[1 - k][:, 2, 0:NSAMP].rearrange("p (b s) -> p b s", s=SSEQ),
                               ACT.Copy).then_inc(fm_out, 1)

            def silu(i):
                act.wait_ge(conv_set, i + 1)
                act.activation(flat(K.qkv[:, bass.ds(i, 1)]), flat(K.qkv[:, bass.ds(i, 1)]), ACT.Silu).then_inc(silu_set, 1)

            act.wait_ge(small_in, 80)
            i = 0
            act.wait_ge(fm_mm, i + 1)
            chain = Chain(act, row_act)
            x, e = rowx[:], rowe[:]
            p2 = ps[i % 2][:, 0:2, :].rearrange("p a n -> p (a n)")
            act.activation(K.rows[0:32, 0:SEQ], p2[0:32], ACT.Sigmoid)
            act.activation(K.rows[0:32, SEQ:TOK], ps[i % 2][0:32, 2, 0:NSAMP], ACT.Sigmoid)
            act.activation(x[:, 0:SEQ], p2, ACT.Identity, bias=bias[:, 0:1])
            chain.link(act.activation(x[:, SEQ:TOK], ps[i % 2][:, 2, 0:NSAMP], ACT.Identity, bias=bias[:, 0:1]))
            act.sem_inc(fm_out, 1)
            chain.link(act.activation(e, x, ACT.Abs))
            chain.link(act.activation(e, e, ACT.Exp, scale=-1.0))
            act.activation(nexpA[32:64], bias[32:64, 1:2], ACT.Exp)
            chain.link(act.activation(e, e, ACT.Ln, bias=1.0))
            evict(0, 0)
            evict(1, 1)
            silu(0)
            with act.Fori(1, FT_A // 2) as i:
                for k in range(2):
                    evict(2 * i + k, k)
                    silu(2 * i + k - 1)
            evict(FT_A - 1, 0)
            silu(FT_A - 2)
            silu(FT_A - 1)
            for c in range(FT_C):
                i = FT_A + 1 + c
                act.wait_ge(fm_mm, i + 1)
                scale = HD ** -0.5 if c < PAIRS else 1.0
                act.activation(K.qkc[:, c, 0:SEQ], ps[i % 2][:, 0:2, :].rearrange("p a n -> p (a n)"), ACT.Copy, scale=scale)
                act.activation(K.qkc[:, c, SEQ:TOK], ps[i % 2][:, 2, 0:NSAMP], ACT.Copy, scale=scale).then_inc(fm_out, 1)
            act.wait_ge(row_tm, NT + 1)
            act.activation(K.ec[:, 0], K.tm[:, :, 1, :], ACT.Exp)
            act.activation(K.ec[:, 1], K.tm[:, :, 3, :], ACT.Exp)
            act.wait_ge(row_mm, NT + 2)
            act.activation(K.gl[:], psR[:, 0:PAIRS * 16].rearrange("p (j n) -> p j n", j=PAIRS), ACT.Exp).then_inc(fin, 1)

        @block.vector
        def _(dve):
            dve.wait_ge(small_in, 80)

            def conv(i, k):
                chain = Chain(dve, conv_chain, i * 6)
                yp = flat(K.qkv[:, bass.ds(i, 1), 0:SEQ])
                ys = K.qkv[:, bass.ds(i, 1), SEQ:TOK].rearrange("p a (b s) -> p (a b) s", s=SSEQ)
                dve.wait_ge(fm_out, i + 2)
                dve.wait_ge(halo_set, i + 1)
                for tap in range(TAPS_A):
                    w = flat(cw[:, bass.ds(i, 1), tap:tap + 1])
                    a, b = zp[:, k, tap:tap + SEQ], zs[:, k, :, tap:tap + SSEQ]
                    if tap == 0:
                        one = dve.tensor_scalar(yp, a, w, None, ALU.mult)
                        two = dve.tensor_scalar(ys, b, w, None, ALU.mult)
                    else:
                        one = dve.scalar_tensor_tensor(yp, a, w, yp, ALU.mult, ALU.add)
                        two = dve.scalar_tensor_tensor(ys, b, w, ys, ALU.mult, ALU.add)
                    if tap < TAPS_A - 1:
                        one.then_inc(conv_chain, 1)
                        chain.n += 1
                        chain.link(two)
                two.then_inc(conv_set, 1)

            chain = Chain(dve, row_dve)
            x, e = rowx[:], rowe[:]
            r = slice(32, 32 + H_A)
            f = slice(64, 64 + H_C)
            dve.wait_ge(row_act, 4)
            dve.memset(K.rows[96:128, :], 0.0)
            chain.link(dve.scalar_tensor_tensor(K.rows[32:64, :], x[32:64], 0.0, e[32:64], ALU.max, ALU.add))
            chain.link(dve.scalar_tensor_tensor(logf[64:96], x[64:96], 0.0, e[64:96], ALU.min, ALU.subtract))
            chain.link(dve.tensor_scalar(K.rows[32:64, :], K.rows[32:64, :], nexpA[32:64], -1.0, ALU.mult, ALU.mult))
            chain.link(dve.tensor_scalar(K.rows[64:96, :], logf[64:96], -1.0, None, ALU.mult))
            chain.link(dve.tensor_copy(x[32:32 + H_A], K.rows[r, :]))
            chain.link(dve.tensor_copy(x[64:64 + H_C], K.rows[f, :]))
            chain.link(dve.tensor_tensor_scan(K.rows[r, :], reset[r], x[r], 0.0, ALU.mult, ALU.add))
            chain.link(dve.tensor_tensor_scan(K.rows[f, :], reset[f], x[f], 0.0, ALU.mult, ALU.add))
            g = K.rows[r, 0:SEQ].rearrange("p (t n) -> p t n", n=P)
            dve.tensor_tensor(K.rows[96:96 + H_A, 0:SEQ].rearrange("p (t n) -> p t n", n=P),
                              g[:, :, P - 1:P].broadcast_to([H_A, NT, P]), g, ALU.subtract)
            g = K.rows[r, SEQ:TOK].rearrange("p (t n) -> p t n", n=SSEQ)
            chain.link(dve.tensor_tensor(K.rows[96:96 + H_A, SEQ:TOK].rearrange("p (t n) -> p t n", n=SSEQ),
                                         g[:, :, SSEQ - 1:SSEQ].broadcast_to([H_A, NBATCH, SSEQ]), g, ALU.subtract))
            conv(0, 0)
            conv(1, 1)
            with dve.Fori(1, FT_A // 2) as i:
                for k in range(2):
                    conv(2 * i + k, k)
            conv(FT_A - 1, 0)
            for t in range(NT + 1):
                n = P if t < NT else NSAMP
                dve.wait_ge(row_mm, t + 1)
                dve.tensor_copy(K.tm[0:n, t], psR[0:n, 0:P].rearrange("p (q h) -> p q h", q=4)[:, :, 0:H_A])\
                    .then_inc(row_tm, 1)


def forgetting_attention(nc, ctx, K):
    with ExitStack() as own:
        sem = stage_semaphores(nc, own)
        sb = lambda n, s, d=F32: own.enter_context(nc.sbuf_tensor(n, s, d))
        U = 2 * NT
        FAR = NT - 4
        qs = sb("fa_q", [P, SEQ])
        ks = sb("fa_k", [P, SEQ])
        sel = sb("fa_sel", [H_C, 2, P])
        nb = sb("fa_nb", [P, 2, SEQ])
        pb = sb("fa_p", [P, 2, SEQ])
        pt = sb("fa_pt", [P, 2, NT, P])
        st = sb("fa_st", [P, 4, 4])
        ost = sb("fa_o", [P, 2, P])
        c16 = sb("fa_c16", [P, 2 * P], BF16)
        psS = [own.enter_context(nc.psum_tensor(f"fa_psS{i}", [P, SEQ], F32)) for i in range(2)]
        psT = own.enter_context(nc.psum_tensor("fa_psT", [P, NT, P], F32))
        psO = own.enter_context(nc.psum_tensor("fa_psO", [P, 512], F32))
        psOT = own.enter_context(nc.psum_tensor("fa_psOT", [P, 512], F32))
        staged, nb_mm, nb_set, s_mm, p_set = (sem("fa_" + n) for n in "staged nb_mm nb_set s_mm p_set".split())
        max_set, t_mm, near_set, far_set, pv_mm, o_set, ot_mm, ot_set = (
            sem("fa_" + n, 1) for n in "max_set t_mm near_set far_set pv_mm o_set ot_mm ot_set".split())
        at_chain, nd_set = sem("at_chain"), sem("nd_set")
        block = own.enter_context(nc.Block())

        @block.gpsimd
        def _(pool):
            def stage(j):
                after(pool, s_mm, j * U)
                pool.tensor_copy(sel[:], K.cst[0:H_C, bass.ds(j * 2 * P + C_HEAD, 2 * P)].rearrange("p (a n) -> p a n", a=2))
                pool.tensor_copy(qs[:], flat(K.qkc[:, bass.ds(j, 1), 0:SEQ]))
                pool.tensor_copy(ks[:], flat(K.qkc[:, bass.ds(j + PAIRS, 1), 0:SEQ])).then_inc(staged, 1)

            stage(0)
            with pool.Fori(1, PAIRS) as j:
                stage(j)

        @block.tensor
        def _(pe):
            pe.wait_ge(nd_set, 1)
            with pe.Fori(0, PAIRS) as j:
                pe.wait_ge(staged, j + 1)
                pe.wait_ge(max_set, U * j + 1)
                for hh in range(2):
                    for c in range(0, SEQ, 512):
                        last = pe.matmul(psS[hh][:, c:c + 512], sel[:, hh, :], K.nd[:, c:c + 512], start=True, stop=True)
                    last.then_inc(nb_mm, 1)

                def scores(u):
                    i, hh = u // 2, u % 2
                    r = slice(hh * HD, (hh + 1) * HD)
                    if u < 2:
                        pe.wait_ge(nb_set, 2 * j + hh + 1)
                    else:
                        pe.wait_ge(max_set, U * j + u)
                    n = (i + 1) * P
                    for c in range(0, n, 512):
                        w = min(512, n - c)
                        pe.matmul(psS[hh][:, c:c + w], qs[r, i * P:(i + 1) * P], ks[r, c:c + w], start=True,
                                  stop=(c + w < n))
                    pe.matmul(psS[hh][:, i * P:n], c16[:, 0:P], c16[:, P:2 * P], start=False, stop=True)\
                        .then_inc(s_mm, 1)

                def turn(u):
                    i = u // 2
                    pe.wait_ge(p_set, U * j + u + 1)
                    pe.wait_ge(near_set, U * j + u + 1)
                    if i >= 4:
                        pe.wait_ge(far_set, 2 * FAR * j + u - 7)
                    for b in range(i + 1):
                        last = pe.transpose(psT[:, b, :], pb[:, u % 2, b * P:(b + 1) * P], K.ident)
                    last.then_inc(t_mm, 1)

                def values(u):
                    i, hh = u // 2, u % 2
                    pe.wait_ge(near_set, U * j + u + 2)
                    if i >= 4:
                        pe.wait_ge(far_set, 2 * FAR * j + u - 6)
                    pe.wait_ge(o_set, U * j + u + 1)
                    for b in range(i + 1):
                        last = pe.matmul(psO[:, 0:HD], pt[:, u % 2, b, :],
                                         K.vc[:, b, bass.ds(j * P + hh * HD, HD)], start=(b == 0), stop=(b == i))
                    last.then_inc(pv_mm, 1)
                    if hh:
                        pe.wait_ge(o_set, U * j + u + 2)
                        pe.wait_ge(ot_set, NT * j + i + 1)
                        pe.transpose(psOT[:, 0:P], ost[:, i % 2, :], K.ident).then_inc(ot_mm, 1)

                scores(0)
                for u in range(U):
                    if u + 1 < U:
                        scores(u + 1)
                    turn(u)
                    if u:
                        values(u - 1)
                values(U - 1)

        @block.scalar
        def _(act):
            with act.Fori(0, PAIRS) as j:
                for hh in range(2):
                    act.wait_ge(nb_mm, 2 * j + hh + 1)
                    act.activation(nb[:, hh], psS[hh][:], ACT.Copy).then_inc(nb_set, 1)

                def out(i):
                    act.wait_ge(ot_mm, NT * j + i + 2)
                    act.activation(flat(K.hT[:, bass.ds(j + 5, 1), i * P:(i + 1) * P]), psOT[:, 0:P], ACT.Copy)\
                        .then_inc(ot_set, 1)

                for u in range(U):
                    i = u // 2
                    n = (i + 1) * P
                    act.wait_ge(max_set, U * j + u + 2)
                    p = pb[:, u % 2, 0:n]
                    act.activation(p, p, ACT.Exp, bias=st[:, u % 4, 1:2], accum_out=st[:, u % 4, 2:3]).then_inc(p_set, 1)
                    act.wait_ge(t_mm, U * j + u + 2)
                    if u < 2:
                        act.wait_ge(pv_mm, U * j + 1)
                    else:
                        act.wait_ge(pv_mm, U * j + u)
                    b = min(i + 1, 4)
                    act.activation(pt[:, u % 2, 0:b, :], psT[:, 0:b, :], ACT.Copy).then_inc(near_set, 1)
                    if u % 2 == 1 and u > 1:
                        out(i - 1)
                out(NT - 1)

        @block.vector
        def _(dve):
            dve.tensor_copy(c16[:], K.cst[:, C_ID:C_ID + 2 * P])
            dve.tensor_copy(K.nd[:], K.rows[64:64 + H_C, :]).then_inc(nd_set, 1)
            with dve.Fori(0, PAIRS) as j:
                chain = Chain(dve, at_chain, j * (2 * U))

                def maximum(u):
                    i, hh = u // 2, u % 2
                    n = (i + 1) * P
                    wait_apart(dve, K, (s_mm, U * j + u + 1), (t_mm, U * j + max(0, u - 1) + 1),
                               *([(nb_set, 2 * j + hh + 1)] if u < 2 else []))
                    chain.link(dve.tensor_tensor_reduce(pb[:, u % 2, 0:n], psS[hh][:, 0:n], nb[:, hh, 0:n], 1.0, -3e38,
                                                        ALU.add, ALU.max, st[:, u % 4, 0:1]))
                    dve.tensor_scalar(st[:, u % 4, 1:2], st[:, u % 4, 0:1], -1.0, None, ALU.mult).then_inc(max_set, 1)

                def far(u):
                    i = u // 2
                    if i >= 4:
                        dve.wait_ge(t_mm, U * j + u + 2)
                        dve.wait_ge(pv_mm, U * j + u)
                        dve.tensor_copy(pt[:, u % 2, 4:i + 1, :], psT[:, 4:i + 1, :]).then_inc(far_set, 1)

                def output(u):
                    i, hh = u // 2, u % 2
                    dve.wait_ge(p_set, U * j + u + 1)
                    chain.link(dve.reciprocal(st[:, u % 4, 3:4], st[:, u % 4, 2:3]))
                    dve.wait_ge(pv_mm, U * j + u + 2)
                    if hh == 0 and i >= 2:
                        dve.wait_ge(ot_mm, NT * j + i)
                    elif hh == 0:
                        dve.wait_ge(ot_mm, NT * j + 1)
                    dve.tensor_scalar(ost[:, i % 2, hh * HD:(hh + 1) * HD], psO[:, 0:HD], st[:, u % 4, 3:4], None, ALU.mult)\
                        .then_inc(o_set, 1)

                maximum(0)
                for u in range(U):
                    if u + 1 < U:
                        maximum(u + 1)
                    far(u)
                    if u:
                        output(u - 1)
                output(U - 1)


def cached_attention(nc, ctx, K):
    with ExitStack() as own:
        sem = stage_semaphores(nc, own)
        sb = lambda n, s, d=F32: own.enter_context(nc.sbuf_tensor(n, s, d))
        R = H_C * SSEQ
        KEYS = PAST + NSAMP
        table = sb("ca_table", [1, NBATCH * NPAGE], I32)
        kp = sb("ca_k", [P, 2, PAIRS, PAST])
        vp = sb("ca_v", [P, 2, NPAGE, W_C])
        lf = sb("ca_lf", [H_C, 2, PAST])
        one = sb("ca_one", [H_C, PAST])
        dn = sb("ca_dn", [H_C, 2, KEYS])
        qb = sb("ca_q", [P, 2, PAIRS, R])
        mk = sb("ca_mk", [R, 2, KEYS])
        pb = sb("ca_p", [R, 2, KEYS])
        pt = sb("ca_pt", [P, 2, 3, R])
        om = sb("ca_om", [R, 2, W_C])
        st = sb("ca_st", [R, 2, 4])
        psS = [own.enter_context(nc.psum_tensor(f"ca_psS{i}", [P, 512], F32)) for i in range(2)]
        psT = [own.enter_context(nc.psum_tensor(f"ca_psT{i}", [P, 512], F32)) for i in range(2)]
        psV = [own.enter_context(nc.psum_tensor(f"ca_psV{i}", [P, 512], F32)) for i in range(2)]
        psO = [own.enter_context(nc.psum_tensor(f"ca_psO{i}", [P, 512], F32)) for i in range(2)]
        table_in, halves = sem("table_in"), sem("halves")
        page_in = [sem("page_in0"), sem("page_in1")]
        clear, clear_d, q_set, d_set, ca_exp, ca_norm, ca_chain = (
            sem("ca_" + n) for n in "clear clear_d q_set d_set exp norm chain".split())
        ca_s, ca_p, ca_t, ca_pt, ca_v, ca_om, ca_o, ca_out = (
            sem("ca_" + n, 1) for n in "s p t pt v om o out".split())
        block = own.enter_context(nc.Block())

        @block.sync
        def _(sp):
            sp.dma_start(table[:], K.page_table).then_inc(table_in, 16)
            sp.wait_ge(table_in, 16)

            def load(b, k):
                after(sp, ca_v, b)
                for pg in range(NPAGE):
                    v = sp.value_load(table[0:1, bass.ds(b * NPAGE + pg, 1)], min_val=0, max_val=NPOOL - 1)
                    rows = slice(pg * PAGE, (pg + 1) * PAGE)
                    sp.dma_start(kp[:, k, :, rows], K.ckT[bass.ds(v, 1)].rearrange("a p j n -> (a p) j n")).then_inc(page_in[k], 16)
                    sp.dma_start(vp[:, k, pg, :], K.cv[bass.ds(v, 1)].rearrange("a p n -> (a p) n")).then_inc(page_in[k], 16)
                    sp.dma_start(lf[:, k, rows], K.clf[bass.ds(v, 1)].rearrange("a p n -> (a p) n")).then_inc(page_in[k], 16)

            load(0, 0)
            load(1, 1)
            with sp.Fori(1, NBATCH // 2) as i:
                for k in range(2):
                    load(2 * i + k, k)

        LOADS = 3 * NPAGE * 16

        @block.gpsimd
        def _(pool):
            pool.memset(qb[:], 0.0)
            pool.memset(mk[:], 0.0).then_inc(clear, 1)
            pool.wait_ge(clear, 1)

            def stage(b, k):
                after(pool, ca_s, b)
                after(pool, ca_p, b)
                for e in range(2):
                    r = slice(e * HD, (e + 1) * HD)
                    for j in range(PAIRS):
                        h = 2 * j + e
                        last = pool.tensor_copy(qb[r, k, j, h * SSEQ:(h + 1) * SSEQ],
                                                K.qkc[r, j, bass.ds(b * SSEQ + SEQ, SSEQ)])
                    last.then_inc(halves, 1)
                    pool.wait_ge(halves, 2 * b + e + 1)
                pool.tensor_copy(mk[:, k, PAST:KEYS], K.cst[0:R, bass.ds(b * NSAMP + C_CAUS, NSAMP)]).then_inc(q_set, 1)

            stage(0, 0)
            stage(1, 1)
            with pool.Fori(1, NBATCH // 2) as i:
                for k in range(2):
                    stage(2 * i + k, k)

        @block.tensor
        def _(pe):
            with pe.Fori(0, NBATCH // 2) as i:
                for k in range(2):
                    b = 2 * i + k
                    pe.wait_ge(page_in[k], LOADS * i + LOADS)
                    pe.wait_ge(q_set, b + 1)
                    pe.wait_ge(d_set, b + 1)
                    pe.wait_ge(ca_p, 2 * i + 1)
                    s = psS[k][0:R, 0:KEYS]
                    pe.matmul(s, K.cst[0:H_C, C_ROW48:C_ROW48 + R], dn[:, k, :], start=True, stop=False)
                    for j in range(PAIRS):
                        pe.matmul(s[:, 0:PAST], qb[:, k, j, :], kp[:, k, j, :], start=False, stop=False)
                        last = pe.matmul(s[:, PAST:KEYS], qb[:, k, j, :], K.qkc[:, PAIRS + j, SEQ:TOK], start=False,
                                         stop=(j == PAIRS - 1))
                    last.then_inc(ca_s, 1)
                for k in range(2):
                    b = 2 * i + k
                    wait_apart(pe, K, (ca_norm, b + 1), (ca_pt, 2 * i + 1))
                    for c in range(3):
                        n = P if c < NPAGE else NSAMP
                        last = pe.transpose(psT[k][0:n, c * R:(c + 1) * R], pb[:, k, c * P:c * P + n], K.ident[0:R, 0:R])
                    last.then_inc(ca_t, 1)
                for k in range(2):
                    b = 2 * i + k
                    pe.wait_ge(ca_pt, b + 2)
                    pe.wait_ge(ca_om, 2 * i + 1)
                    for c in range(NPAGE):
                        pe.matmul(psV[k][0:R, 0:W_C], pt[:, k, c, :], vp[:, k, c, :], start=(c == 0), stop=False)
                    pe.matmul(psV[k][0:R, 0:W_C], pt[0:NSAMP, k, NPAGE, :], K.vc[0:NSAMP, NT, :], start=False, stop=True)\
                        .then_inc(ca_v, 1)
                for k in range(2):
                    b = 2 * i + k
                    pe.wait_ge(ca_om, b + 2)
                    pe.wait_ge(ca_out, 2 * i + 1)
                    for j in range(PAIRS):
                        last = pe.matmul(psO[k][:, j * SSEQ:(j + 1) * SSEQ], om[:, k, j * P:(j + 1) * P],
                                         K.cst[0:R, C_PICK:C_PICK + SSEQ], start=True, stop=True)
                    last.then_inc(ca_o, 1)

        @block.scalar
        def _(act):
            with act.Fori(0, NBATCH // 2) as i:
                for k in range(2):
                    b = 2 * i + k
                    act.wait_ge(ca_p, b + 2)
                    act.activation(pb[:, k], pb[:, k], ACT.Exp, bias=st[:, k, 1:2], accum_out=st[:, k, 2:3]).then_inc(ca_exp, 1)
                for k in range(2):
                    b = 2 * i + k
                    act.wait_ge(ca_t, b + 2)
                    act.wait_ge(ca_v, 2 * i + 1)
                    act.activation(pt[:, k, 0:NPAGE, :], psT[k][:, 0:NPAGE * R].rearrange("p (c r) -> p c r", c=NPAGE), ACT.Copy)
                    act.activation(pt[0:NSAMP, k, NPAGE, :], psT[k][0:NSAMP, NPAGE * R:3 * R], ACT.Copy).then_inc(ca_pt, 1)
                for k in range(2):
                    b = 2 * i + k
                    act.wait_ge(ca_o, b + 2)
                    act.activation(K.hT[:, 5:8, bass.ds(b * SSEQ + SEQ, SSEQ)],
                                   psO[k][:, 0:PAIRS * SSEQ].rearrange("p (j s) -> p j s", j=PAIRS), ACT.Copy)\
                        .then_inc(ca_out, 1)

        @block.vector
        def _(dve):
            dve.memset(one[:], 1.0).then_inc(clear_d, 1)
            dve.wait_ge(clear_d, 1)
            with dve.Fori(0, NBATCH // 2) as i:
                chain = Chain(dve, ca_chain, i * 6)
                for k in range(2):
                    b = 2 * i + k
                    dve.wait_ge(page_in[k], LOADS * i + LOADS)
                    dve.wait_ge(ca_s, 2 * i + 1)
                    chain.link(dve.tensor_tensor_scan(dn[:, k, 0:PAST], one[:], lf[:, k], 0.0, ALU.mult, ALU.subtract))
                    dve.tensor_scalar(dn[:, k, PAST:KEYS], K.nd[:, SEQ:TOK], dn[:, k, PAST - 1:PAST], None, ALU.add)\
                        .then_inc(d_set, 1)
                for k in range(2):
                    b = 2 * i + k
                    wait_apart(dve, K, (ca_s, b + 2), (q_set, b + 1), (ca_t, 2 * i + 1))
                    chain.link(dve.tensor_tensor_reduce(pb[:, k], psS[k][0:R, 0:KEYS], mk[:, k], 1.0, -3e38, ALU.add, ALU.max,
                                                        st[:, k, 0:1]))
                    dve.tensor_scalar(st[:, k, 1:2], st[:, k, 0:1], -1.0, None, ALU.mult).then_inc(ca_p, 1)
                for k in range(2):
                    b = 2 * i + k
                    dve.wait_ge(ca_exp, b + 1)
                    chain.link(dve.reciprocal(st[:, k, 3:4], st[:, k, 2:3]))
                    dve.tensor_scalar(pb[:, k], pb[:, k], st[:, k, 3:4], None, ALU.mult).then_inc(ca_norm, 1)
                for k in range(2):
                    b = 2 * i + k
                    dve.wait_ge(ca_v, b + 2)
                    dve.wait_ge(ca_o, 2 * i + 1)
                    dve.tensor_tensor(om[:, k], psV[k][0:R, 0:W_C], K.cst[0:R, C_OWN:C_OWN + W_C], ALU.mult).then_inc(ca_om, 1)


def delta_rule(nc, ctx, K):
    with ExitStack() as own:
        sem = stage_semaphores(nc, own)
        sb = lambda n, s, d=F32: own.enter_context(nc.sbuf_tensor(n, s, d))
        H, G3 = H_A, 3
        stg = sb("dr_stg", [P, FT_A, P])
        obs = sb("dr_obs", [P, W_B])
        nexp = sb("dr_nexp", [P, NT + 1, H])
        rn = sb("dr_rn", [P, NT + 1, 2, H])
        sq = sb("dr_sq", [P, H, HD])
        ss = sb("dr_ss", [P, 3, H])
        mhalf = sb("dr_mhalf", [P, (NT + 1) * 2 * H])
        qk = sb("dr_qk", [P, 2, H, HD])
        kx = sb("dr_kx", [P, 5, H, HD])
        tr = sb("dr_tr", [P, 4, PAIRS, P])
        ex = sb("dr_ex", [P, H, P])
        lt = sb("dr_lt", [P, H, P])
        at = sb("dr_at", [P, H, P])
        ot = sb("dr_ot", [P, 2, H, P])
        T = sb("dr_T", [P, H, P])
        TT = sb("dr_TT", [P, H, P])
        X = sb("dr_X", [P, H, P])
        wT = sb("dr_wT", [P, PAIRS, P])
        vn = sb("dr_vn", [P, H, HD])
        osb = sb("dr_o", [P, H, HD])
        oo = sb("dr_oo", [P, H, HD])
        S = sb("dr_S", [P, PAIRS, HD])
        S2 = sb("dr_S2", [P, PAIRS, HD])
        S0 = sb("dr_S0", [P, PAIRS, NBATCH, HD])
        pick = sb("dr_pick", [NSAMP, 2, NBATCH, HD])
        sel = sb("dr_selv", [NSAMP, 2, H, HD])
        A = [own.enter_context(nc.psum_tensor(f"dr_A{g}", [P, 512], F32)) for g in range(2)]
        B = [own.enter_context(nc.psum_tensor(f"dr_B{g}", [P, 512], F32)) for g in range(2)]
        C = [own.enter_context(nc.psum_tensor(f"dr_C{g}", [P, 512], F32)) for g in range(2)]
        M = [own.enter_context(nc.psum_tensor(f"dr_M{g}", [P, 512], F32)) for g in range(2)]
        (g_staged, o_staged, nsq_set, nsq_mm, n_chain, rn_set, nexp_set, vb_set, qk_set, kb_set, kx_set, gcb_mm, dd_set, e_set, tr_mm,
         tra_set, trd_set, lt_mm, lt_set, ata_set, at_set, ot_set, t1_mm, x_mm, x_set, y_mm, t_set, tt_set, w_mm, w_set, vn_mm, vn_set,
         o_mm, o_out, s_mm, osq_set, oms_set, orn_set, chain_s, own_chain_s, scaled, gr_set, init, s0_in,
         own_mm, own_set, s_out) = (sem("dr_" + n) for n in (
             "staged o_staged nsq_set nsq_mm n_chain rn_set nexp_set vb_set qk_set kb_set kx_set gcb_mm dd_set e_set tr_mm tra_set "
             "trd_set lt_mm lt_set ata_set at_set ot_set t1_mm x_mm x_set y_mm t_set tt_set w_mm w_set vn_mm vn_set o_mm o_out s_mm "
             "osq_set oms_set orn_set chain own_chain scaled gr_set init s0_in own_mm own_set s_out"
         ).split())
        qkv_turned, s_set, oo_set, ot2_mm, mixed_set = (
            sem("dr_" + n, 1) for n in "qkv_turned s_set oo_set ot2_mm mixed_set".split())
        HALVES = ((0, NT // 2), (NT // 2, NT + 1))
        LV = LEVELS
        LV8 = 3
        block = own.enter_context(nc.Block())

        def heads(ap, n):
            return ap.rearrange("p (h c) -> p h c", h=G3)

        def cols(t0, t1):
            return t0 * P, min(t1 * P, TOK)

        @block.sync
        def _(sp):
            sp.dma_start(S0[:], K.s0_d).then_inc(s0_in, 16)
            sp.wait_ge(s_set, NT + 1)
            sp.dma_start(K.p_S, S[:]).then_inc(s_out, 16)
            sp.wait_ge(s_set, NT + H + 1)
            sp.dma_start(K.s_S, S0[:]).then_inc(s_out, 16)
            sp.wait_ge(s_out, 32)

        @block.gpsimd
        def _(pool):
            def stage(t, n):
                after(pool, qkv_turned, 3 * t + 1)
                pool.tensor_copy(stg[:, :, 0:n], K.qkv[:, :, bass.ds(t * P, n)]).then_inc(g_staged, 1)

            stage(0, P)
            pool.memset(mhalf[:], -0.5)
            pool.memset(S[:], 0.0).then_inc(init, 1)
            pool.tensor_scalar(nexp[:], K.ec[:, 0], -1.0, None, ALU.mult).then_inc(nexp_set, 1)
            pool.wait_ge(init, 1)
            pool.wait_ge(n_chain, 1)
            full, last = rn[:, 0:NT].rearrange("p t a h -> p (t a h)"), rn[0:NSAMP, NT].rearrange("p a h -> p (a h)")
            pool.tensor_tensor(full, full, mhalf[:, 0:NT * 2 * H], ALU.pow)
            pool.tensor_tensor(last, last, mhalf[0:NSAMP, 0:2 * H], ALU.pow).then_inc(n_chain, 1)
            pool.wait_ge(n_chain, 2)
            pool.tensor_scalar(rn[:, 0:NT, 0], rn[:, 0:NT, 0], HD ** -0.5, None, ALU.mult)
            pool.tensor_scalar(rn[0:NSAMP, NT, 0], rn[0:NSAMP, NT, 0], HD ** -0.5, None, ALU.mult).then_inc(rn_set, 1)
            pool.wait_ge(nexp_set, 1)

            def out_norm(t, n):
                wait_apart(pool, K, (osq_set, 2 * t + 2))
                pool.tensor_scalar(ss[0:n, 1], ss[0:n, 0], 1.0 / HD, EPS, ALU.mult, ALU.add).then_inc(oms_set, 1)
                pool.wait_ge(oms_set, t + 1)
                pool.tensor_tensor(ss[0:n, 2], ss[0:n, 1], mhalf[0:n, 0:H], ALU.pow).then_inc(orn_set, 1)

            def tile(t, n, nl, tri, before=True, staged=0):
                def by(ap):
                    return flat(ap).unsqueeze(2).broadcast_to([n, H, HD])

                pool.wait_ge(qk_set, t + 1)
                pool.tensor_tensor(kx[0:n, 0], qk[0:n, 1], by(K.tm[0:n, bass.ds(t, 1), 0, :]), ALU.mult).then_inc(kb_set, 1)
                pool.tensor_tensor(kx[0:n, 1], qk[0:n, 0], by(K.ec[0:n, 0, bass.ds(t, 1), :]), ALU.mult).then_inc(kb_set, 1)
                if before:
                    out_norm(t - 1, P)
                pool.wait_ge(kb_set, 2 * t + 2)
                pool.tensor_tensor(kx[0:n, 2], kx[0:n, 0], by(nexp[0:n, bass.ds(t, 1), :]), ALU.mult)
                pool.tensor_tensor(kx[0:n, 3], qk[0:n, 1], by(K.ec[0:n, 1, bass.ds(t, 1), :]), ALU.mult).then_inc(kx_set, 1)
                for g in range(2):
                    pool.wait_ge(lt_set, 2 * t + g + 1)
                    mask = K.cst[0:n, C_LVL:C_LVL + n].unsqueeze(1).broadcast_to([n, G3, n])
                    last = pool.tensor_tensor(ot[0:n, 0, g::2, 0:n], lt[0:n, g::2, 0:n], mask, ALU.mult)
                last.then_inc(ot_set, 1)
                for l in range(1, nl):
                    if l >= 2:
                        pool.wait_ge(x_mm, 2 * (LV - 1) * t + max(1, 2 * (l - 2)))
                    mask = K.cst[0:n, C_LVL + l * P:C_LVL + l * P + n].unsqueeze(1).broadcast_to([n, H, n])
                    pool.tensor_tensor(ot[0:n, l % 2, :, 0:n], lt[0:n, :, 0:n], mask, ALU.mult).then_inc(ot_set, 1)
                    if l == 1:
                        pool.wait_ge(ata_set, t + 1)
                        pool.tensor_tensor(at[0:n, :, 0:n], at[0:n, :, 0:n], tri.unsqueeze(1).broadcast_to([n, H, n]), ALU.mult)\
                            .then_inc(at_set, 1)
                if staged:
                    stage(t + 1, staged)
                pool.wait_ge(ot2_mm, t + 1)
                pool.tensor_copy(obs[0:n], flat(K.tok[0:n, bass.ds(t, 1), W_A:W_A + W_B])).then_inc(o_staged, 1)

            tile(0, P, LV, K.tri, before=False, staged=P)
            with pool.Fori(1, NT - 1) as t:
                tile(t, P, LV, K.tri, staged=P)
            tile(NT - 1, P, LV, K.tri, staged=NSAMP)
            tile(NT, NSAMP, LV8, K.tri8)
            out_norm(NT, NSAMP)

        @block.tensor
        def _(pe):
            def finish(t, n, now):
                pe.wait_ge(oo_set, t + 2)
                pe.wait_ge(o_staged, t + 1)
                pe.wait_ge(tra_set, 2 * now + 1)
                pe.wait_ge(trd_set, 2 * now + 2)
                o = oo[0:n].rearrange("p h d -> p (h d)")
                for j in range(PAIRS):
                    last = pe.transpose(B[0][:, j * n:(j + 1) * n], o[:, j * P:(j + 1) * P], K.ident[0:n, 0:n])
                for j in range(2):
                    last = pe.transpose(B[1][:, j * n:(j + 1) * n], obs[0:n, j * P:(j + 1) * P], K.ident[0:n, 0:n])
                last.then_inc(ot2_mm, 1)

            for m in range(12):
                f, (t0, t1) = m // 2, HALVES[m % 2]
                pe.wait_ge(nsq_set, m + 1)
                for t in range(t0, t1):
                    n = P if t < NT else NSAMP
                    last = pe.matmul(C[1][0:n, (t * 6 + f) * 2:(t * 6 + f) * 2 + 2],
                                     flat((T, TT)[m % 2])[:, (t - t0) * P:(t - t0) * P + n], K.cst[:, C_HALF:C_HALF + 2],
                                     start=True, stop=True)
                last.then_inc(nsq_mm, 1)

            def intra(t, n, nl, before=True):
                pe.wait_ge(g_staged, t + 1)
                after(pe, o_out, t)
                for i, bank in enumerate((A[0], A[1], B[0])):
                    for j in range(PAIRS):
                        last = pe.transpose(bank[0:n, j * P:(j + 1) * P], stg[:, PAIRS * i + j, 0:n], K.ident)
                    last.then_inc(qkv_turned, 1)
                for h in range(H):
                    last = pe.matmul(M[h % 2][0:n, (h // 2) * n:(h // 2 + 1) * n],
                                     K.cst[0:H, C_HEAD + h * P:C_HEAD + h * P + n], K.gr[:, bass.ds(t * P, n)],
                                     start=True, stop=True)
                last.then_inc(gcb_mm, 1)
                for i, (src, bank, s, v) in enumerate(((qk[0:n, 0], B[1], qk_set, t + 1), (qk[0:n, 1], C[0], qk_set, t + 1),
                                                       (kx[0:n, 0], C[1], kb_set, 2 * t + 1), (kx[0:n, 1], B[0], kb_set, 2 * t + 2))):
                    pe.wait_ge(s, v)
                    if i == 1:
                        pe.wait_ge(s_set, t + 1)
                    if i == 3:
                        pe.wait_ge(vb_set, t + 1)
                    x = src.rearrange("p h d -> p (h d)")
                    for j in range(PAIRS):
                        last = pe.transpose(bank[:, j * n:(j + 1) * n], x[:, j * P:(j + 1) * P], K.ident[0:n, 0:n])
                    last.then_inc(tr_mm, 1)
                pe.wait_ge(tra_set, 2 * t + 2)
                pe.wait_ge(trd_set, 2 * t + 1)
                pe.wait_ge(dd_set, t + 1)
                for dst, rhs in ((A, 2), (M, 0)):
                    for g in range(2):
                        for x in range(G3):
                            h = 2 * x + g
                            r = slice((h % 2) * HD, (h % 2 + 1) * HD)
                            last = pe.matmul(dst[g][0:n, x * n:(x + 1) * n], tr[r, 1, h // 2, 0:n], tr[r, rhs, h // 2, 0:n],
                                             start=True, stop=True)
                        last.then_inc(lt_mm, 1)
                if before:
                    finish(t - 1, P, t)
                pe.wait_ge(ot_set, LV * t + 1)
                for g in range(2):
                    for x in range(G3):
                        last = pe.transpose(A[g][0:n, x * n:(x + 1) * n], ot[0:n, 0, 2 * x + g, 0:n], K.ident[0:n, 0:n])
                    last.then_inc(t1_mm, 1)
                X0 = 2 * (LV - 1) * t
                for l in range(1, nl):
                    pe.wait_ge(ot_set, LV * t + l + 1)
                    for g in range(2):
                        pe.wait_ge(t_set, X0 + 2 * l + g - 1)
                        for x in range(G3):
                            h = 2 * x + g
                            last = pe.matmul(A[g][0:n, x * n:(x + 1) * n], ot[0:n, l % 2, h, 0:n], T[0:n, h, 0:n],
                                             start=True, stop=True)
                        last.then_inc(x_mm, 1)
                    if l == 1 and before:
                        pe.wait_ge(mixed_set, 2 * t + 1)
                    for g in range(2):
                        pe.wait_ge(x_set, X0 + 2 * (l - 1) + g + 1)
                        if l > 1:
                            pe.wait_ge(tt_set, X0 + 2 * l + g - 3)
                        hs = [2 * x + g for x in range(G3)]
                        if l < nl - 1:
                            for x, h in enumerate(hs):
                                last = pe.matmul(B[g][0:n, x * n:(x + 1) * n], TT[0:n, h, 0:n], X[0:n, h, 0:n],
                                                 start=True, stop=True)
                            last.then_inc(y_mm, 1)
                        for x, h in enumerate(hs):
                            last = pe.matmul(C[g][0:n, x * n:(x + 1) * n], X[0:n, h, 0:n], TT[0:n, h, 0:n],
                                             start=True, stop=True)
                        last.then_inc(y_mm, 1 if l < nl - 1 else 2)

            def weights(t, n, nl):
                pe.wait_ge(tt_set, 2 * (LV - 1) * t + 2 * (nl - 1))
                pe.wait_ge(kx_set, t + 1)
                pe.wait_ge(ata_set, t + 1)
                for h in range(H):
                    r = slice((h % 2) * HD, (h % 2 + 1) * HD)
                    last = pe.matmul(M[0][r, (h // 2) * n:(h // 2 + 1) * n], kx[0:n, 2, h, :], TT[0:n, h, 0:n],
                                     start=True, stop=True)
                last.then_inc(w_mm, 1)

            pe.wait_ge(gr_set, 1)
            pe.wait_ge(init, 1)
            def tile(t, before=True):
                intra(t, P, LV, before)
                weights(t, P, LV)
                pairs = [(h, slice((h % 2) * HD, (h % 2 + 1) * HD), slice((h // 2) * HD, (h // 2 + 1) * HD)) for h in range(H)]
                for h, r, c in pairs:
                    pe.matmul((M[1], B[0])[h % 2][:, c], TT[:, h, :], kx[:, 4, h, :], start=(h < 2), stop=False)
                pe.wait_ge(w_set, t + 1)
                for h, r, c in pairs:
                    last = pe.matmul((M[1], B[0])[h % 2][:, c], wT[r, h // 2, :], S[r, h // 2, :], start=False, stop=(h >= H - 2))
                last.then_inc(vn_mm, 1)
                pe.wait_ge(trd_set, 2 * t + 2)
                for h, r, c in pairs:
                    pe.matmul(A[h % 2][:, c], tr[r, 3, h // 2, :], S[r, h // 2, :], start=(h < 2), stop=False)
                pe.wait_ge(vn_set, t + 1)
                pe.wait_ge(at_set, t + 1)
                for h, r, c in pairs:
                    last = pe.matmul(A[h % 2][:, c], at[:, h, :], vn[:, h, :], start=False, stop=(h >= H - 2))
                last.then_inc(o_mm, 1)
                for h in range(H):
                    r = slice((h % 2) * HD, (h % 2 + 1) * HD)
                    last = pe.matmul(C[0][r, (h // 2) * HD:(h // 2 + 1) * HD], kx[:, 3, h, :], vn[:, h, :],
                                     start=True, stop=True)
                last.then_inc(s_mm, 1)

            tile(0, False)
            with pe.Fori(1, NT) as t:
                tile(t)

            t, n = NT, NSAMP
            intra(t, n, LV8)
            weights(t, n, LV8)
            for h in range(H):
                last = pe.matmul(M[1][0:n, h * HD:(h + 1) * HD], TT[0:n, h, 0:n], kx[0:n, 4, h, :], start=True, stop=True)
            last.then_inc(vn_mm, 1)
            pe.wait_ge(w_set, t + 1)
            pe.wait_ge(trd_set, 2 * t + 2)
            pe.wait_ge(s0_in, 16)
            banks = (B[0], B[1])
            for m in range(2 * H):
                h, src = m % H, (wT[:] if m < H else tr[:, 3])
                r = slice((h % 2) * HD, (h % 2 + 1) * HD)
                if m >= 2:
                    pe.wait_ge(own_set, m - 1)
                pe.matmul(banks[m % 2][0:n, :], src[r, h // 2, 0:n], S0[r, h // 2].rearrange("p b v -> p (b v)"),
                          start=True, stop=True).then_inc(own_mm, 1)
            pe.wait_ge(vn_set, t + 1)
            pe.wait_ge(at_set, t + 1)
            for h in range(H):
                last = pe.matmul(A[0][0:n, h * HD:(h + 1) * HD], at[0:n, h, 0:n], vn[0:n, h, :], start=True, stop=True)
            last.then_inc(o_mm, 1)
            for h in range(H):
                r = slice((h % 2) * HD, (h % 2 + 1) * HD)
                pe.wait_ge(own_set, 2 * H + h + 1)
                if h >= 2:
                    pe.wait_ge(s_set, NT + h)
                pe.matmul(C[h % 2][r, :], kx[0:n, 3, h, :], pick[:, h % 2].rearrange("p b v -> p (b v)"),
                          start=True, stop=True).then_inc(s_mm, 1)
            finish(t, n, t)

        @block.scalar
        def _(act):
            for m in range(12):
                c0, c1 = cols(*HALVES[m % 2])
                after(act, nsq_mm, m - 1)
                act.activation(flat((T, TT)[m % 2])[:, 0:c1 - c0], K.qkv[:, m // 2, c0:c1], ACT.Square).then_inc(nsq_set, 1)

            def finish(t, n):
                act.wait_ge(ot2_mm, t + 2)
                act.activation(K.hT[:, 0:3, bass.ds(t * P, n)], B[0][:, 0:3 * n].rearrange("p (j c) -> p j c", j=3), ACT.Copy)\
                    .then_inc(mixed_set, 1)
                act.activation(K.hT[:, 3:5, bass.ds(t * P, n)], B[1][:, 0:2 * n].rearrange("p (j c) -> p j c", j=2), ACT.Copy)\
                    .then_inc(mixed_set, 1)

            def tile(t, n, nl, before=True):
                for i, bank in ((0, B[1]), (2, C[1])):
                    if i:
                        act.wait_ge(dd_set, t + 1)
                        act.activation(ex[0:n, :, 0:n], ex[0:n, :, 0:n], ACT.Exp).then_inc(e_set, 1)
                    act.wait_ge(tr_mm, 4 * t + i + 1)
                    act.activation(tr[:, i, :, 0:n], bank[:, 0:PAIRS * n].rearrange("p (j c) -> p j c", j=PAIRS), ACT.Copy)\
                        .then_inc(tra_set, 1)
                if before:
                    finish(t - 1, P)
                X0 = 2 * (LV - 1) * t
                for l in range(1, nl):
                    for g in range(2):
                        act.wait_ge(x_mm, X0 + 2 * (l - 1) + g + 1)
                        act.activation(X[0:n, g::2, 0:n], heads(A[g][0:n, 0:G3 * n], n), ACT.Copy)\
                            .then_inc(x_set, 1)
                act.wait_ge(w_mm, t + 1)
                act.activation(wT[:, :, 0:n], M[0][:, 0:PAIRS * n].rearrange("p (j c) -> p j c", j=PAIRS), ACT.Copy)\
                    .then_inc(w_set, 1)

            def chunk(t, before=True):
                tile(t, P, LV, before)
                act.wait_ge(vn_mm, t + 1)
                for g, bank in enumerate((M[1], B[0])):
                    last = act.activation(vn[:, g::2, :], heads(bank[:, 0:G3 * HD], P), ACT.Copy)
                last.then_inc(vn_set, 1)
                act.wait_ge(o_mm, t + 1)
                after(act, oo_set, t + 1)
                for g in range(2):
                    last = act.activation(osb[:, g::2, :], heads(A[g][:, 0:G3 * HD], P), ACT.Copy)
                last.then_inc(o_out, 1)
                act.wait_ge(o_out, t + 1)
                act.activation(sq[:], osb[:], ACT.Square).then_inc(osq_set, 1)

            chunk(0, False)
            with act.Fori(1, NT) as t:
                chunk(t)
            tile(NT, NSAMP, LV8)
            act.wait_ge(scaled, 1)
            act.activation(sq[0:NSAMP], osb[0:NSAMP], ACT.Square).then_inc(osq_set, 1)
            finish(NT, NSAMP)

        @block.vector
        def _(dve):
            dve.tensor_copy(K.gr[:], K.rows[32:32 + H, :]).then_inc(gr_set, 1)

            dve.wait_ge(nsq_mm, 12)
            full, last = rn[:, 0:NT].rearrange("p t a h -> p (t a h)"), rn[0:NSAMP, NT].rearrange("p a h -> p (a h)")
            dve.tensor_scalar(full, C[1][:, 0:NT * 2 * H], EPS, None, ALU.add)
            dve.tensor_scalar(last, C[1][0:NSAMP, NT * 2 * H:(NT + 1) * 2 * H], EPS, None, ALU.add).then_inc(n_chain, 1)
            dve.wait_ge(rn_set, 1)

            def sums(t, n):
                dve.wait_ge(osq_set, 2 * t + 1)
                dve.tensor_reduce(ss[0:n, 0], sq[0:n], AX.X, ALU.add).then_inc(osq_set, 1)

            def finish(t, n, chain):
                dve.wait_ge(orn_set, t + 1)
                dve.wait_ge(ot2_mm, t + 1)
                chain.link(dve.tensor_tensor(oo[0:n], osb[0:n], ss[0:n, 2].unsqueeze(2).broadcast_to([n, H, HD]), ALU.mult))
                dve.tensor_tensor(oo[0:n].rearrange("p h d -> p (h d)"), oo[0:n].rearrange("p h d -> p (h d)"),
                                  flat(K.tok[0:n, bass.ds(t, 1), 0:W_A]), ALU.mult).then_inc(oo_set, 1)

            def intra(t, n, nl, before=True):
                chain = Chain(dve, chain_s, 4 * t - before)

                dve.wait_ge(qkv_turned, 3 * t + 4)
                for i in range(2):
                    r = rn[0:n, bass.ds(t, 1), i, :].rearrange("p a h -> p (a h)").unsqueeze(2).broadcast_to([n, H, HD])
                    last = dve.tensor_tensor(qk[0:n, i], A[i][0:n, 0:W_A].rearrange("p (h d) -> p h d", h=H), r, ALU.mult)
                last.then_inc(qk_set, 1)
                beta = flat(K.tm[0:n, bass.ds(t, 1), 0, :]).unsqueeze(2).broadcast_to([n, H, HD])
                dve.tensor_tensor(kx[0:n, 4], B[0][0:n, 0:W_A].rearrange("p (h d) -> p h d", h=H), beta, ALU.mult)\
                    .then_inc(vb_set, 1)
                dve.wait_ge(gcb_mm, t + 1)
                for g in range(2):
                    gc = flat(K.tm[0:n, bass.ds(t, 1), 1, :])[:, g::2].unsqueeze(2).broadcast_to([n, G3, n])
                    ins = dve.tensor_tensor(ex[0:n, g::2, 0:n], heads(M[g][0:n, 0:G3 * n], n), gc, ALU.subtract)
                chain.link(ins)
                dve.tensor_scalar(ex[0:n, :, 0:n], ex[0:n, :, 0:n], 0.0, None, ALU.min).then_inc(dd_set, 1)
                for i, bank in ((1, C[0]), (3, B[0])):
                    if i == 3 and before:
                        finish(t - 1, P, chain)
                    dve.wait_ge(tr_mm, 4 * t + i + 1)
                    dve.tensor_copy(tr[:, i, :, 0:n], bank[:, 0:PAIRS * n].rearrange("p (j c) -> p j c", j=PAIRS))\
                        .then_inc(trd_set, 1)
                dve.wait_ge(e_set, t + 1)
                for g in range(2):
                    hs = slice(g, H, 2)
                    dve.wait_ge(lt_mm, 4 * t + g + 1)
                    dve.tensor_tensor(lt[0:n, hs, 0:n], heads(A[g][0:n, 0:G3 * n], n), ex[0:n, hs, 0:n], ALU.mult)\
                        .then_inc(lt_set, 1)
                for g in range(2):
                    hs = slice(g, H, 2)
                    dve.wait_ge(lt_mm, 4 * t + g + 3)
                    ins = dve.tensor_tensor(at[0:n, hs, 0:n], heads(M[g][0:n, 0:G3 * n], n), ex[0:n, hs, 0:n], ALU.mult)
                ins.then_inc(ata_set, 1)
                dve.wait_ge(ot_set, LV * t + 1)
                eye = K.ident[0:n, 0:n].unsqueeze(1)
                chain.link(dve.tensor_tensor(TT[0:n, :, 0:n], eye.broadcast_to([n, H, n]), ot[0:n, 0, :, 0:n], ALU.subtract))
                for g in range(2):
                    hs = slice(g, H, 2)
                    dve.wait_ge(t1_mm, 2 * t + g + 1)
                    dve.tensor_tensor(T[0:n, hs, 0:n], eye.broadcast_to([n, G3, n]), heads(A[g][0:n, 0:G3 * n], n),
                                      ALU.subtract).then_inc(t_set, 1)
                X0 = 2 * (LV - 1) * t
                for l in range(1, nl):
                    for g in range(2):
                        hs = slice(g, H, 2)
                        y = 2 * X0 + 4 * (l - 1) + 2 * g
                        if l < nl - 1:
                            dve.wait_ge(y_mm, y + 1)
                            dve.tensor_tensor(T[0:n, hs, 0:n], T[0:n, hs, 0:n], heads(B[g][0:n, 0:G3 * n], n), ALU.subtract)\
                                .then_inc(t_set, 1)
                        dve.wait_ge(y_mm, y + 2)
                        dve.tensor_tensor(TT[0:n, hs, 0:n], TT[0:n, hs, 0:n], heads(C[g][0:n, 0:G3 * n], n), ALU.subtract)\
                            .then_inc(tt_set, 1)
                return chain

            dve.wait_ge(init, 1)
            def tile(t, before=True):
                chain = intra(t, P, LV, before)
                gl = K.gl[:, :, bass.ds(t, 1)].broadcast_to([P, PAIRS, HD])
                chain.link(dve.tensor_tensor(S2[:], S[:], gl, ALU.mult))
                dve.wait_ge(o_mm, t + 1)
                dve.wait_ge(s_mm, t + 1)
                dve.tensor_tensor(S[:], S2[:], C[0][:, 0:PAIRS * HD].rearrange("p (j v) -> p j v", j=PAIRS), ALU.add)\
                    .then_inc(s_set, 1)
                sums(t, P)

            tile(0, False)
            with dve.Fori(1, NT) as t:
                tile(t)

            t, n = NT, NSAMP
            intra(t, n, LV8)
            blk = K.cst[0:n, C_BLK:C_BLK + NBATCH].unsqueeze(2).broadcast_to([n, NBATCH, HD])
            banks = (B[0], B[1])
            own_chain = Chain(dve, own_chain_s)
            for m in range(2 * H):
                dve.wait_ge(own_mm, m + 1)
                own_chain.link(dve.tensor_tensor(pick[:, m % 2], banks[m % 2][0:n, :].rearrange("p (b v) -> p b v", b=NBATCH),
                                                 blk, ALU.mult))
                dve.tensor_reduce(sel[:, m // H, m % H], pick[:, m % 2].rearrange("p b v -> p v b"), AX.X, ALU.add)\
                    .then_inc(own_set, 1)
            dve.wait_ge(own_set, 2 * H)
            dve.wait_ge(vn_mm, t + 1)
            dve.tensor_tensor(vn[0:n], M[1][0:n, 0:W_A].rearrange("p (h d) -> p h d", h=H), sel[:, 0], ALU.add)\
                .then_inc(vn_set, 1)
            dve.wait_ge(vn_set, t + 1)
            for h in range(H):
                r = slice((h % 2) * HD, (h % 2 + 1) * HD)
                if h >= 2:
                    dve.wait_ge(s_mm, NT + h - 1)
                dve.tensor_tensor(pick[:, h % 2], vn[0:n, h, :].unsqueeze(1).broadcast_to([n, NBATCH, HD]), blk, ALU.mult)\
                    .then_inc(own_set, 1)
                gl = K.gl[r, h // 2, 8:16].unsqueeze(2).broadcast_to([HD, NBATCH, HD])
                own_chain.link(dve.tensor_tensor(S0[r, h // 2], S0[r, h // 2], gl, ALU.mult))
                dve.wait_ge(s_mm, NT + h + 1)
                dve.tensor_tensor(S0[r, h // 2], S0[r, h // 2], C[h % 2][r, :].rearrange("p (b v) -> p b v", b=NBATCH), ALU.add)\
                    .then_inc(s_set, 1)
            dve.wait_ge(o_mm, t + 1)
            dve.tensor_tensor(osb[0:n], A[0][0:n, 0:W_A].rearrange("p (h d) -> p h d", h=H), sel[:, 1], ALU.add)\
                .then_inc(scaled, 1)
            sums(t, n)
            finish(t, n, own_chain)


def output_projection(nc, ctx, K):
    with ExitStack() as own:
        sem = stage_semaphores(nc, own)
        sb = lambda n, s, d=F32: own.enter_context(nc.sbuf_tensor(n, s, d))
        wo = sb("op_w", [P, KD, D])
        ms = sb("op_m", [P, 2, KD, P])
        hf = sb("op_h", [P, KD, P])
        xt = sb("op_x", [P, 2, D])
        x1 = sb("op_x1", [P, 2, D])
        xn = sb("op_xn", [P, 2, D])
        junk = sb("op_junk", [P, D])
        ss = sb("op_ss", [P, 2, 8])
        mhalf = sb("op_mhalf", [P, 1])
        gg = sb("op_gg", [P, 2, D])
        gp = sb("op_gp", [P, D])
        psO = [own.enter_context(nc.psum_tensor(f"op_psO{i}", [P, D], F32)) for i in range(2)]
        psX = own.enter_context(nc.psum_tensor("op_psX", [P, KD, P], F32))
        w_in = [sem(f"op_w_in{kk}") for kk in range(KD)]
        (g_in, staged, mm, sq_set, r_chain, r_set, x1_chain, x1_set, sq1_set, r1_set, xn_set, turned, h2_set, h2_chain,
         gg_set, half_set, hi_set, lo_set) = (sem("op_" + n) for n in (
             "g_in staged mm sq_set r_chain r_set x1_chain x1_set sq1_set r1_set xn_set turned h2_set h2_chain gg_set "
             "half_set hi_set lo_set").split())
        x_in = [sem("op_x_in0"), sem("op_x_in1")]
        x1_out = [sem("op_x1_out0"), sem("op_x1_out1")]
        block = own.enter_context(nc.Block())

        def tiles(eng, step):
            step(0, 0, P)
            step(1, 1, P)
            with eng.Fori(1, NT // 2) as i:
                for k in range(2):
                    step(2 * i + k, k, P)
            step(NT, 0, NSAMP)

        @block.sync
        def _(sp):
            for kk in range(KD):
                sp.dma_start(wo[:, kk], K.w_out_d[:, kk]).then_inc(w_in[kk], 16)
            sp.dma_start(gp[:], K.gpost_d[0:1].broadcast_to([P, D])).then_inc(g_in, 16)
            sp.dma_start(gg[:, 0], K.scr[0:1, 2 * D:3 * D].broadcast_to([P, D])).then_inc(g_in, 16)
            for b in range(NBATCH):
                sp.dma_start(gg[b * SSEQ:(b + 1) * SSEQ, 1], K.scr[b + 1:b + 2, 2 * D:3 * D].broadcast_to([SSEQ, D]))\
                    .then_inc(g_in, 16)

            def step(t, k, rows):
                after(sp, x1_set, t - 1)
                sp.dma_start(xt[0:rows, k], K.x[bass.ds(t * P, rows)]).then_inc(x_in[k], 16)

            tiles(sp, step)

        @block.gpsimd
        def _(pool):
            pool.memset(mhalf[:], -0.5).then_inc(half_set, 1)
            pool.wait_ge(half_set, 1)

            def stage(t, k, rows):
                after(pool, mm, t - 1)
                pool.tensor_copy(ms[:, k, :, 0:rows], K.hT[:, :, bass.ds(t * P, rows)]).then_inc(staged, 1)

            def step(t, k, rows):
                for i, (ready, out) in enumerate(((sq_set, r_set), (sq1_set, r1_set))):
                    c = 4 * i
                    wait_apart(pool, K, (ready, t + 1))
                    pool.tensor_scalar(ss[0:rows, k, c + 1:c + 2], ss[0:rows, k, c:c + 1], 1.0 / D, EPS, ALU.mult, ALU.add)\
                        .then_inc(r_chain, 1)
                    pool.wait_ge(r_chain, 2 * t + i + 1)
                    pool.tensor_tensor(ss[0:rows, k, c + 2:c + 3], ss[0:rows, k, c + 1:c + 2], mhalf[0:rows], ALU.pow)\
                        .then_inc(out, 1)

            def lo(t, rows):
                pool.wait_ge(hi_set, t + 1)
                pool.tensor_tensor(K.h_lo[:, :, bass.ds(t * P, rows)], hf[:, :, 0:rows],
                                   K.h_hi[:, :, bass.ds(t * P, rows)], ALU.subtract).then_inc(lo_set, 1)

            stage(0, 0, P)
            stage(1, 1, P)
            step(0, 0, P)
            stage(2, 0, P)
            step(1, 1, P)
            stage(3, 1, P)
            lo(0, P)
            with pool.Fori(1, NT // 2 - 1) as i:
                for k in range(2):
                    step(2 * i + k, k, P)
                    stage(2 * i + k + 2, k, P)
                    lo(2 * i + k - 1, P)
            step(NT - 2, 0, P)
            stage(NT, 0, NSAMP)
            lo(NT - 3, P)
            step(NT - 1, 1, P)
            lo(NT - 2, P)
            step(NT, 0, NSAMP)
            lo(NT - 1, P)
            lo(NT, NSAMP)

        @block.tensor
        def _(pe):
            def gemm(t, k, rows):
                pe.wait_ge(staged, t + 1)
                after(pe, x1_chain, t - 1)
                for kk in range(KD):
                    if isinstance(t, int) and t == 0:
                        pe.wait_ge(w_in[kk], 16)
                    for c in range(0, D, 512):
                        last = pe.matmul(psO[k][0:rows, c:c + 512], ms[:, k, kk, 0:rows], wo[:, kk, c:c + 512],
                                         start=(kk == 0), stop=(kk == KD - 1))
                last.then_inc(mm, 1)

            def turn(t, k, rows):
                pe.wait_ge(xn_set, t + 1)
                after(pe, h2_set, t)
                for kk in range(KD):
                    last = pe.transpose(psX[:, kk, 0:rows], xn[0:rows, k, kk * P:(kk + 1) * P], K.ident[0:rows, 0:rows])
                last.then_inc(turned, 1)

            gemm(0, 0, P)
            gemm(1, 1, P)
            turn(0, 0, P)
            with pe.Fori(1, NT // 2) as i:
                for k in range(2):
                    gemm(2 * i + k, k, P)
                    turn(2 * i + k - 1, 1 - k, P)
            gemm(NT, 0, NSAMP)
            turn(NT - 1, 1, P)
            turn(NT, 0, NSAMP)

        @block.scalar
        def _(act):
            def step(t, k, rows):
                act.wait_ge(mm, t + 1)
                act.activation(junk[0:rows], psO[k][0:rows, :], ACT.Square, accum_out=ss[0:rows, k, 0:1]).then_inc(sq_set, 1)
                act.wait_ge(x1_set, t + 1)
                act.activation(junk[0:rows], x1[0:rows, k], ACT.Square, accum_out=ss[0:rows, k, 4:5]).then_inc(sq1_set, 1)
                act.dma_start(K.scr_x[bass.ds(t * P, rows)], x1[0:rows, k]).then_inc(x1_out[k], 16)
                act.wait_ge(r1_set, t + 1)
                after(act, turned, t - 1)
                act.activation(xn[0:rows, k], x1[0:rows, k], ACT.Copy, scale=ss[0:rows, k, 6:7]).then_inc(xn_set, 1)

            def hi(t, rows):
                act.wait_ge(h2_set, t + 1)
                act.activation(K.h_hi[:, :, bass.ds(t * P, rows)], hf[:, :, 0:rows], ACT.Copy).then_inc(hi_set, 1)

            step(0, 0, P)
            step(1, 1, P)
            hi(0, P)
            with act.Fori(1, NT // 2) as i:
                for k in range(2):
                    step(2 * i + k, k, P)
                    hi(2 * i + k - 1, P)
            step(NT, 0, NSAMP)
            hi(NT - 1, P)
            hi(NT, NSAMP)
            act.wait_ge(x1_out[0], 16 * (NT // 2 + 1))
            act.wait_ge(x1_out[1], 16 * (NT // 2))

        @block.vector
        def _(dve):
            dve.wait_ge(g_in, 16 * (2 + NBATCH))
            dve.tensor_tensor(gg[:, 0], gg[:, 0], gp[:], ALU.mult)
            dve.tensor_tensor(gg[0:NSAMP, 1], gg[0:NSAMP, 1], gp[0:NSAMP], ALU.mult).then_inc(gg_set, 1)
            dve.wait_ge(gg_set, 1)

            def residual(t, k, rows):
                dve.wait_ge(r_set, t + 1)
                after(dve, xn_set, t - 1)
                if not isinstance(t, int) or t >= 2:
                    dve.wait_ge(x1_out[k], 8 * (t - k))
                g = gg[0:rows, 0 if rows == P else 1]
                dve.scalar_tensor_tensor(x1[0:rows, k], psO[k][0:rows, :], ss[0:rows, k, 2:3], g, ALU.mult, ALU.mult)\
                    .then_inc(x1_chain, 1)
                dve.wait_ge(x1_chain, t + 1)
                dve.wait_ge(x_in[k], 8 * (t - k) + 16)
                dve.tensor_tensor(x1[0:rows, k], x1[0:rows, k], xt[0:rows, k], ALU.add).then_inc(x1_set, 1)

            def h2(t, k, rows):
                dve.wait_ge(turned, t + 1)
                after(dve, lo_set, t)
                made = gain_shift(dve, K, 1, psX, hf, rows)
                if rows == P:
                    made[0].then_inc(h2_set, 1)
                else:
                    chain = Chain(dve, h2_chain)
                    for n, (o, a, b, op) in enumerate(made):
                        ins = dve.tensor_tensor(o, a, b, op)
                        if n == len(made) // 2 - 1:
                            chain.link(ins)
                    ins.then_inc(h2_set, 1)

            residual(0, 0, P)
            residual(1, 1, P)
            h2(0, 0, P)
            with dve.Fori(1, NT // 2) as i:
                for k in range(2):
                    residual(2 * i + k, k, P)
                    h2(2 * i + k - 1, 1 - k, P)
            residual(NT, 0, NSAMP)
            h2(NT - 1, 1, P)
            h2(NT, 0, NSAMP)


def ffn_up(nc, ctx, K, yT):
    with ExitStack() as own:
        sem = stage_semaphores(nc, own)
        sb = lambda n, s, d=F32: own.enter_context(nc.sbuf_tensor(n, s, d))
        RING = 2
        NTILE = 2 * KF
        wu = sb("fu_w", [P, RING, KD, P])
        w_hi = sb("fu_whi", [P, RING, KD, P], F32R)
        w_lo = sb("fu_wlo", [P, RING, KD, P], F32R)
        zp = sb("fu_zp", [P, 2, TAPS_F - 1 + SEQ])
        zs = sb("fu_zs", [P, 2, NBATCH, TAPS_F - 1 + SSEQ])
        cb = sb("fu_cb", [P, TOK])
        prev = sb("fu_prev", [P, NTILE, NBATCH, TAPS_F - 1])
        cw = sb("fu_cw", [P, NTILE, TAPS_F])
        pst = sb("fu_pst", [P, NTILE, TAPS_F - 1])
        ps = [own.enter_context(nc.psum_tensor(f"fu_ps{i}", [P, 3, 512], F32)) for i in range(2)]
        w_in = [sem(f"fu_w_in{k}") for k in range(RING)]
        w_hi_set, w_lo_set, small_in, mm, out, halo, chain_s, gelu_set, y_set, zero_set, st_out = (sem("fu_" + n) for n in (
            "w_hi_set w_lo_set small_in mm out halo chain gelu_set y_set zero_set st_out").split())
        conv_set, copied = sem("fu_conv_set", 1), sem("fu_copied", 1)
        block = own.enter_context(nc.Block())

        def pairs(eng, tile):
            for k in range(2):
                tile(k, k)
            with eng.Fori(1, KF) as i:
                for k in range(2):
                    tile(2 * i + k, k)

        @block.sync
        def _(sp):
            for k in range(RING):
                sp.dma_start(wu[:, k], K.w_up_d[k]).then_inc(w_in[k], 16)
            sp.dma_start(prev[:], K.fprev_d).then_inc(small_in, 16)
            sp.dma_start(cw[:], K.fconv_d).then_inc(small_in, 16)
            with sp.Fori(1, NTILE // RING) as i:
                for k in range(RING):
                    sp.wait_ge(w_lo_set, RING * (i - 1) + k + 1)
                    sp.dma_start(wu[:, k], K.w_up_d[bass.ds(RING * i + k, 1)].rearrange("a p k n -> (a p) k n"))\
                        .then_inc(w_in[k], 16)
            sp.wait_ge(copied, 2 * NTILE + 1)
            sp.dma_start(K.p_fconv, pst[:]).then_inc(st_out, 16)
            sp.dma_start(K.s_fconv, prev[:]).then_inc(st_out, 16)
            sp.wait_ge(st_out, 32)

        @block.tensor
        def _(pe):
            def tile(i, slot):
                pe.wait_ge(w_hi_set, i + 1)
                pe.wait_ge(w_lo_set, i + 1)
                after(pe, out, i - 1)
                for kk in range(KD):
                    for m, (w, h) in enumerate(((w_hi, K.h_hi), (w_hi, K.h_lo), (w_lo, K.h_hi))):
                        for n in range(3):
                            size = min(THIRD, TOK - n * THIRD)
                            last = pe.matmul(ps[slot][:, n, 0:size], w[:, slot, kk, :], h[:, kk, n * THIRD:n * THIRD + size],
                                             start=(kk == 0 and m == 0), stop=(kk == KD - 1 and m == 2))
                last.then_inc(mm, 1)

            pairs(pe, tile)

        @block.gpsimd
        def _(pool):
            for k in range(2):
                pool.memset(zp[:, k, 0:TAPS_F - 1], 0.0).then_inc(zero_set, 1)
            def split(i, k):
                pool.wait_ge(w_hi_set, i + 1)
                after(pool, mm, i - 1)
                pool.tensor_tensor(w_lo[:, k], wu[:, k], w_hi[:, k], ALU.subtract).then_inc(w_lo_set, 1)

            def tile(i, k):
                after(pool, conv_set, i)
                pool.tensor_copy(zs[:, k, :, 0:TAPS_F - 1], prev[:, bass.ds(i, 1)].rearrange("p a b n -> p (a b) n"))\
                    .then_inc(halo, 1)
                pool.wait_ge(halo, i + 1)
                pool.wait_ge(out, i + 1)
                pool.tensor_copy(flat(pst[:, bass.ds(i, 1)]), zp[:, k, SEQ:SEQ + TAPS_F - 1]).then_inc(copied, 1)
                pool.tensor_copy(prev[:, bass.ds(i, 1)].rearrange("p a b n -> p (a b) n"), zs[:, k, :, SSEQ:])\
                    .then_inc(copied, 1)

            split(0, 0)
            split(1, 1)
            pool.wait_ge(small_in, 32)
            tile(0, 0)
            with pool.Fori(1, KF) as i:
                split(2 * i, 0)
                tile(2 * i - 1, 1)
                split(2 * i + 1, 1)
                tile(2 * i, 0)
            tile(NTILE - 1, 1)

        @block.scalar
        def _(act):
            act.wait_ge(zero_set, 2)

            def split(i, k):
                act.wait_ge(w_in[k], 8 * (i - k) + 16)
                after(act, mm, i - 1)
                act.activation(w_hi[:, k], wu[:, k], ACT.Copy).then_inc(w_hi_set, 1)

            def evict(i, k):
                act.wait_ge(mm, i + 1)
                after(act, conv_set, i)
                after(act, copied, 2 * i - 1)
                act.activation(zp[:, k, TAPS_F - 1:TAPS_F - 1 + 2 * THIRD].rearrange("p (a n) -> p a n", a=2),
                               ps[k][:, 0:2, 0:THIRD], ACT.Copy)
                act.activation(zp[:, k, TAPS_F - 1 + 2 * THIRD:], ps[k][:, 2, 0:REST], ACT.Copy)
                act.activation(zs[:, k, :, TAPS_F - 1:], ps[k][:, 2, REST:REST + NSAMP].rearrange("p (b s) -> p b s", s=SSEQ),
                               ACT.Copy).then_inc(out, 1)

            def gelu(j):
                act.wait_ge(conv_set, 2 * j + 2)
                act.activation(flat(yT[:, bass.ds(j, 1)]), flat(yT[:, bass.ds(j, 1)]), ACT.Gelu_apprx_tanh).then_inc(gelu_set, 1)

            split(0, 0)
            split(1, 1)
            evict(0, 0)
            with act.Fori(1, KF) as j:
                split(2 * j, 0)
                evict(2 * j - 1, 1)
                gelu(j - 1)
                split(2 * j + 1, 1)
                evict(2 * j, 0)
            evict(NTILE - 1, 1)
            gelu(KF - 1)

        @block.vector
        def _(dve):
            dve.wait_ge(small_in, 32)

            def conv(j, k):
                i = 2 * j + k
                chain = Chain(dve, chain_s, i * 4)
                y = yT[:, bass.ds(j, 1)] if k == 0 else cb[:].unsqueeze(1)
                yp = flat(y[:, :, 0:SEQ])
                ys = y[:, :, SEQ:TOK].rearrange("p a (b s) -> p (a b) s", s=SSEQ)
                dve.wait_ge(out, i + 1)
                dve.wait_ge(halo, i + 1)
                for tap in range(TAPS_F):
                    w = flat(cw[:, bass.ds(i, 1), tap:tap + 1])
                    a, b = zp[:, k, tap:tap + SEQ], zs[:, k, :, tap:tap + SSEQ]
                    if tap == 0:
                        one = dve.tensor_scalar(yp, a, w, None, ALU.mult)
                        two = dve.tensor_scalar(ys, b, w, None, ALU.mult)
                    else:
                        one = dve.scalar_tensor_tensor(yp, a, w, yp, ALU.mult, ALU.add)
                        two = dve.scalar_tensor_tensor(ys, b, w, ys, ALU.mult, ALU.add)
                    if tap < TAPS_F - 1:
                        one.then_inc(chain_s, 1)
                        chain.n += 1
                        chain.link(two)
                two.then_inc(conv_set, 1)

            def pair(j):
                conv(j, 0)
                conv(j, 1)
                dve.wait_ge(conv_set, 2 * j + 3)
                dve.wait_ge(gelu_set, j + 1)
                y = flat(yT[:, bass.ds(j, 1)])
                dve.tensor_tensor(y, y, cb[:], ALU.mult).then_inc(y_set, 1)

            pair(0)
            with dve.Fori(1, KF) as j:
                pair(j)


def ffn_down(nc, ctx, K, yT):
    with ExitStack() as own:
        sem = stage_semaphores(nc, own)
        sb = lambda n, s, d=F32: own.enter_context(nc.sbuf_tensor(n, s, d))
        RING = 2
        NPASS, TP = 3, 3
        W = TP * P
        wd = sb("fd_w", [P, RING, D])
        w_hi = sb("fd_whi", [P, RING, D], F32R)
        w_lo = sb("fd_wlo", [P, RING, D], F32R)
        y_hi = sb("fd_yhi", [P, RING, W], F32R)
        y_lo = sb("fd_ylo", [P, RING, W], F32R)
        x1 = sb("fd_x1", [P, TP, D])
        yo = sb("fd_yo", [P, 2, D])
        junk = sb("fd_junk", [P, D])
        ss = sb("fd_ss", [P, 2, 4])
        mhalf = sb("fd_mhalf", [P, 1])
        gg = sb("fd_gg", [P, 2, D])
        gp = sb("fd_gp", [P, D])
        ps = [own.enter_context(nc.psum_tensor(f"fd_ps{i}", [P, D], F32)) for i in range(TP)]
        w_in = [sem(f"fd_w_in{k}") for k in range(RING)]
        (g_in, x_in, w_hi_set, y_hi_set, lo_set, mm, acc, sq_set, r_chain, r_set, out_chain, out_set, gg_set, half_set) = (
            sem("fd_" + n) for n in "g_in x_in w_hi_set y_hi_set lo_set mm acc sq_set r_chain r_set out_chain out_set gg_set half_set".split())
        y_out = [sem("fd_y_out0"), sem("fd_y_out1")]
        block = own.enter_context(nc.Block())

        def width(p):
            sizes = [P if TP * p + n < NT else NSAMP for n in range(TP)]
            return sum(sizes), sizes

        @block.sync
        def _(sp):
            def load(f, k, g):
                after(sp, lo_set, g - RING + 1)
                sp.dma_start(wd[:, k], K.w_down_d[bass.ds(f, 1)].rearrange("a p n -> (a p) n")).then_inc(w_in[k], 16)

            load(0, 0, 0)
            load(1, 1, 1)
            sp.dma_start(gp[:], K.gpost_d[1:2].broadcast_to([P, D])).then_inc(g_in, 16)
            sp.dma_start(gg[:, 0], K.scr[0:1, 5 * D:6 * D].broadcast_to([P, D])).then_inc(g_in, 16)
            for b in range(NBATCH):
                sp.dma_start(gg[b * SSEQ:(b + 1) * SSEQ, 1], K.scr[b + 1:b + 2, 5 * D:6 * D].broadcast_to([SSEQ, D]))\
                    .then_inc(g_in, 16)
            for p in range(NPASS):
                with sp.Fori(1, KF // 2) as i:
                    for k in range(2):
                        load(2 * i + k, k, 2 * i + k + KF * p)
                if p + 1 < NPASS:
                    for k in range(2):
                        load(k, k, k + KF * (p + 1))
                for n, rows in enumerate(width(p)[1]):
                    t = TP * p + n
                    after(sp, out_set, t - TP + 1)
                    sp.dma_start(x1[0:rows, n], K.scr_x[t * P:t * P + rows]).then_inc(x_in, 16)

        def slices(eng, part, finish):
            part(0, 0, 0, 0)
            for p in range(NPASS):
                part(1, 1, 1 + KF * p, p)
                with eng.Fori(1, KF // 2) as i:
                    for k in range(2):
                        part(2 * i + k, k, 2 * i + k + KF * p, p)
                if p + 1 < NPASS:
                    part(0, 0, KF * (p + 1), p + 1)
                for n, rows in enumerate(width(p)[1]):
                    finish(p, n, rows)

        @block.gpsimd
        def _(pool):
            pool.memset(mhalf[:], -0.5).then_inc(half_set, 1)
            pool.wait_ge(half_set, 1)
            def part(f, k, g, p):
                w = width(p)[0]
                after(pool, mm, g - 1)
                pool.tensor_copy(y_hi[:, k, 0:w], flat(yT[:, bass.ds(f, 1), p * W:p * W + w])).then_inc(y_hi_set, 1)

            def finish(p, n, rows):
                t = TP * p + n
                k = t % 2
                pool.wait_ge(sq_set, t + 1)
                pool.tensor_scalar(ss[0:rows, k, 1:2], ss[0:rows, k, 0:1], 1.0 / D, EPS, ALU.mult, ALU.add)\
                    .then_inc(r_chain, 1)
                pool.wait_ge(r_chain, t + 1)
                pool.tensor_tensor(ss[0:rows, k, 2:3], ss[0:rows, k, 1:2], mhalf[0:rows], ALU.pow).then_inc(r_set, 1)

            slices(pool, part, finish)

        @block.tensor
        def _(pe):
            def slice_of(p, k, g, first=False, end=False):
                pe.wait_ge(lo_set, g + 1)
                for n in range(TP):
                    if first and p:
                        pe.wait_ge(out_chain, TP * (p - 1) + n + 1)
                    for m, (w, y) in enumerate(((w_hi, y_hi), (w_hi, y_lo), (w_lo, y_hi))):
                        for c in range(0, D, 512):
                            last = pe.matmul(ps[n][:, c:c + 512], y[:, k, n * P:(n + 1) * P], w[:, k, c:c + 512],
                                             start=(first and m == 0), stop=(end and m == 2))
                    if end and n < TP - 1:
                        last.then_inc(acc, 1)
                last.then_inc(mm, 1)

            for p in range(NPASS):
                slice_of(p, 0, KF * p, first=True)
                slice_of(p, 1, KF * p + 1)
                with pe.Fori(1, KF // 2 - 1) as i:
                    for k in range(2):
                        slice_of(p, k, 2 * i + k + KF * p)
                slice_of(p, 0, KF * p + KF - 2)
                slice_of(p, 1, KF * p + KF - 1, end=True)

        def store(act, t):
            rows = P if t < NT else NSAMP
            act.wait_ge(out_set, t + 1)
            act.dma_start(K.y[t * P:t * P + rows], yo[0:rows, t % 2]).then_inc(y_out[t % 2], 16)

        @block.scalar
        def _(act):
            def part(f, k, g, p):
                act.wait_ge(w_in[k], 8 * (g - k) + 16)
                after(act, mm, g - 1)
                act.activation(w_hi[:, k], wd[:, k], ACT.Copy).then_inc(w_hi_set, 1)

            def finish(p, n, rows):
                t = TP * p + n
                if n < TP - 1:
                    act.wait_ge(acc, (TP - 1) * p + n + 1)
                else:
                    act.wait_ge(mm, KF * (p + 1))
                after(act, sq_set, t)
                after(act, out_chain, t - 1)
                act.activation(junk[0:rows], ps[n][0:rows, :], ACT.Square, accum_out=ss[0:rows, t % 2, 0:1])\
                    .then_inc(sq_set, 1)
                if t:
                    store(act, t - 1)

            slices(act, part, finish)
            store(act, NT)
            act.wait_ge(y_out[0], 16 * (NT // 2 + 1))
            act.wait_ge(y_out[1], 16 * (NT // 2))

        @block.vector
        def _(dve):
            def part(f, k, g, p):
                w = width(p)[0]
                dve.wait_ge(y_hi_set, g + 1)
                after(dve, mm, g - 1)
                dve.tensor_tensor(y_lo[:, k, 0:w], flat(yT[:, bass.ds(f, 1), p * W:p * W + w]), y_hi[:, k, 0:w], ALU.subtract)
                dve.wait_ge(w_hi_set, g + 1)
                dve.tensor_tensor(w_lo[:, k], wd[:, k], w_hi[:, k], ALU.subtract).then_inc(lo_set, 1)

            def finish(p, n, rows):
                t = TP * p + n
                k = t % 2
                if t == 0:
                    dve.wait_ge(g_in, 16 * (2 + NBATCH))
                    dve.tensor_tensor(gg[:, 0], gg[:, 0], gp[:], ALU.mult)
                    dve.tensor_tensor(gg[0:NSAMP, 1], gg[0:NSAMP, 1], gp[0:NSAMP], ALU.mult).then_inc(gg_set, 1)
                    dve.wait_ge(gg_set, 1)
                dve.wait_ge(r_set, t + 1)
                after(dve, y_out[k], 16 * (t // 2))
                dve.scalar_tensor_tensor(yo[0:rows, k], ps[n][0:rows, :], ss[0:rows, k, 2:3], gg[0:rows, 0 if t < NT else 1],
                                         ALU.mult, ALU.mult).then_inc(out_chain, 1)
                dve.wait_ge(out_chain, t + 1)
                dve.wait_ge(x_in, 16 * (t // TP + 1) * TP)
                dve.tensor_tensor(yo[0:rows, k], yo[0:rows, k], x1[0:rows, n], ALU.add).then_inc(out_set, 1)

            slices(dve, part, finish)


def build(nc, A, O):
    K = Kernel()
    with ExitStack() as ctx:
        sb = lambda stack, n, s, d=F32, side="left": stack.enter_context(nc.sbuf_tensor(n, s, d, side=side))
        sem = lambda n: ctx.enter_context(nc.semaphore(n))
        K.x, K.cT, K.w_ada, K.b_ada, K.cst_d, K.gpre_d = A["x"], A["cT"], A["w_ada"], A["b_ada"], A["cst"], A["gpre"]
        K.w_tm_d, K.gn_d, K.lng_d, K.lnb_d, K.wsT_d, K.wsT8_d, K.bs_d = (A[n] for n in "w_tm gn lng lnb wsT wsT8 bs".split())
        K.w_fm_d, K.gprev_d, K.gconv_d, K.bias_d, K.reset_d = (A[n] for n in "w_fm gprev gconv bias reset".split())
        K.page_table, K.ckT, K.cv, K.clf, K.s0_d = (A[n] for n in "page_table ckT cv clf s0".split())
        K.w_out_d, K.gpost_d, K.w_up_d, K.fprev_d, K.fconv_d, K.w_down_d = (
            A[n] for n in "w_out gpost w_up fprev fconv w_down".split())
        K.y, K.v_out, K.chunk_v, K.p_gconv, K.s_gconv, K.k_out, K.logf_out, K.p_S, K.s_S, K.p_fconv, K.s_fconv = (
            O[n] for n in "y v chunk_v p_gconv s_gconv k logf p_S s_S p_fconv s_fconv".split())
        K.scr = nc.dram_tensor("scr_mod", (NSEQ, 6 * D), F32).ap()
        K.scr_x = nc.dram_tensor("scr_x1", (TOK, D), F32).ap()
        K.cst_in, K.w_tm_in = sem("cst_in"), sem("w_tm_in")
        with ExitStack() as mixer, ExitStack() as up:
            K.cst = sb(mixer, "cst", [P, C_END], side="right")
            K.gpre = sb(mixer, "gpre", [P, 2, KD], side="right")
            K.gain = sb(mixer, "gain", [P, 2, KD, NSEQ], side="right")
            K.shift = sb(mixer, "shift", [P, 2, KD, NSEQ], side="right")
            K.hT = sb(mixer, "hT", [P, KD, TOK], side="right")
            K.ident, K.tri = K.cst[:, C_ID:C_ID + P], K.cst[:, C_TRI:C_TRI + P]
            K.tri8 = K.cst[0:NSAMP, C_TRI8:C_TRI8 + NSAMP]
            with ExitStack() as mix:
                K.tok = sb(mix, "tok", [P, NT + 1, W_A + W_B])
                K.vc = sb(mix, "vc", [P, NT + 1, W_C])
                with ExitStack() as wide:
                    K.w_tm = sb(wide, "w_tm", [P, KD, TM_COLS])
                    modulation(nc, ctx, K)
                    token_projection(nc, ctx, K)
                K.qkv = sb(mix, "qkv", [P, FT_A, TOK])
                K.rows = sb(mix, "rows", [P, TOK])
                K.gr = sb(mix, "gr", [H_A, TOK])
                K.tm = sb(mix, "tm", [P, NT + 1, 4, H_A])
                K.ec = sb(mix, "ec", [P, 2, NT + 1, H_A])
                K.gl = sb(mix, "gl", [P, PAIRS, 16])
                with ExitStack() as group_c:
                    K.qkc = sb(group_c, "qkc", [P, FT_C, TOK])
                    K.nd = sb(group_c, "nd", [H_C, TOK])
                    feature_projection(nc, ctx, K)
                    forgetting_attention(nc, ctx, K)
                    cached_attention(nc, ctx, K)
                delta_rule(nc, ctx, K)
            K.h_hi, K.h_lo = (sb(up, n, [P, KD, TOK], F32R) for n in ("h_hi", "h_lo"))
            output_projection(nc, ctx, K)
            mixer.close()
            with ExitStack() as ffn:
                yT = sb(ffn, "yT", [P, KF, TOK], side="right")
                ffn_up(nc, ctx, K, yT)
                up.close()
                ffn_down(nc, ctx, K, yT)


OUTS = {
    "y": (TOK, D), "v": (TOK, W_C), "chunk_v": (NSAMP, W_B), "p_gconv": (P, FT_A, TAPS_A - 1),
    "s_gconv": (P, FT_A, NBATCH, TAPS_A - 1), "k": (P, PAIRS, TOK), "logf": (H_C, TOK), "p_S": (P, PAIRS, HD),
    "s_S": (P, PAIRS, NBATCH, HD), "p_fconv": (P, 2 * KF, TAPS_F - 1), "s_fconv": (P, 2 * KF, NBATCH, TAPS_F - 1),
}


def kernel(**inputs):
    import concourse.bacc as bacc
    from concourse.bass_utils import run_bass_kernel_spmd

    a = {n: np.asarray(v) for n, v in inputs.items()}
    tile = lambda w: np.ascontiguousarray(w.reshape(KD, P, -1, P).transpose(2, 1, 0, 3))
    part = lambda v: v.reshape(-1, P).T
    w_in = a["w_in"][0]
    o = np.cumsum([0, 3 * W_A, H_A, H_A, W_A, 2 * W_B, W_C, W_C, W_C, H_C])
    qkv_a, beta, decay, gate, uv, qc, kc, vc, forget = (w_in[:, o[i]:o[i + 1]] for i in range(9))
    narrow = np.zeros((D, P), np.float32)
    narrow[:, 0:H_A], narrow[:, 32:32 + H_A], narrow[:, 64:64 + H_C] = beta, decay, forget
    bias = np.zeros((P, 2), np.float32)
    bias[32:32 + H_A, 0], bias[64:64 + H_C, 0] = a["gdn_dt_bias"][0], a["fox_f_bias"][0]
    bias[32:32 + H_A, 1] = a["gdn_A_log"][0]
    ws = a["chunk_w_s"][0]
    bs = np.zeros((P, 2, G_B), np.float32)
    bs[:, 0], bs[:NSAMP, 1] = a["chunk_b_s"][0].T, np.tile(a["chunk_b_s"][0][:, :SSEQ].T, (NBATCH, 1))
    up = a["w_up"][0].reshape(D, 2, KF, P).transpose(0, 2, 1, 3).reshape(D, 2 * D_FF)
    turn = lambda v: v.reshape(*v.shape[:-1], 2, KF, P).swapaxes(-3, -2).reshape(v.shape)
    conv = lambda w: np.ascontiguousarray(w.reshape(w.shape[0], -1, P).transpose(2, 1, 0))
    before = lambda s: np.ascontiguousarray(s.reshape(*s.shape[:2], -1, P).transpose(3, 2, 0, 1))
    arrays = {
        "x": np.concatenate([a["x_prompt"][0], a["x_sample"].reshape(NSAMP, D)]),
        "cT": np.concatenate([a["c_prompt"], a["c_sample"]]).reshape(NSEQ, KD, P).transpose(2, 1, 0),
        "w_ada": a["w_ada"][0].reshape(KD, P, NGRP, 512).transpose(2, 1, 0, 3),
        "b_ada": a["b_ada"].reshape(NGRP, 512),
        "cst": constants(), "reset": reset_rows(),
        "gpre": np.stack([part(a["g_pre_mix"][0]), part(a["g_pre_ffn"][0])], 1),
        "gpost": np.concatenate([a["g_post_mix"], a["g_post_ffn"]]),
        "w_tm": np.concatenate([gate, uv, vc], 1).reshape(KD, P, TM_COLS).transpose(1, 0, 2),
        "gn": a["gdn_norm_g"], "lng": a["chunk_ln_g"], "lnb": a["chunk_ln_b"],
        "wsT": ws.transpose(2, 0, 1),
        "wsT8": np.tile(ws[:, :SSEQ, :SSEQ].transpose(2, 0, 1), (NBATCH, 1, NBATCH)),
        "bs": bs,
        "w_fm": tile(np.concatenate([narrow, qkv_a, qc, kc], 1)),
        "gprev": before(a["state_gdn_conv"][0]), "gconv": conv(a["gdn_conv_w"][0]), "bias": bias,
        "page_table": a["page_table"].reshape(1, -1),
        "ckT": a["cache_fox_k"][0].reshape(NPOOL, PAGE, PAIRS, P).transpose(0, 3, 2, 1),
        "cv": a["cache_fox_v"][0].reshape(NPOOL, PAGE, W_C),
        "clf": a["cache_fox_logf"][0].transpose(0, 2, 1),
        "s0": a["state_gdn_S"][0].reshape(NBATCH, PAIRS, P, HD).transpose(2, 1, 0, 3),
        "w_out": a["w_out"][0].reshape(KD, P, D).transpose(1, 0, 2),
        "w_up": tile(up), "fprev": before(turn(a["state_ffn_conv"][0])), "fconv": conv(turn(a["ffn_conv_w"][0])),
        "w_down": a["w_down"][0].reshape(KF, P, D),
    }
    nc = bacc.Bacc("TRN2", target_bir_lowering=False, num_devices=1)
    A, O, feed = {}, {}, {}
    for name, v in arrays.items():
        v = np.ascontiguousarray(v)
        feed[f"in_{name}"] = v
        A[name] = nc.dram_tensor(f"in_{name}", v.shape, mybir.dt.from_np(v.dtype), kind="ExternalInput").ap()
    for name, shape in OUTS.items():
        O[name] = nc.dram_tensor(f"out_{name}", shape, F32, kind="ExternalOutput").ap()
    build(nc, A, O)
    r = run_bass_kernel_spmd(nc, [feed], core_ids=[0]).results[0]
    r = {n: np.asarray(r[f"out_{n}"]) for n in OUTS}

    rows = lambda v: v.transpose(2, 1, 0).reshape(1, 1, v.shape[2], -1)
    srows = lambda v: v.transpose(2, 3, 1, 0).reshape(1, NBATCH, v.shape[3], -1)
    back = lambda v: v.reshape(*v.shape[:-1], KF, 2, P).swapaxes(-3, -2).reshape(v.shape)
    k = r["k"].transpose(2, 1, 0).reshape(TOK, H_C, HD)
    v = r["v"].reshape(TOK, H_C, HD)
    lf = r["logf"].T
    c = lambda v: np.ascontiguousarray(v)
    pg, smp = (1, 1, NT, P), (1, NBATCH, SSEQ)
    return (
        r["y"][:SEQ].reshape(1, SEQ, D), r["y"][SEQ:].reshape(NBATCH, SSEQ, D),
        c(rows(r["p_gconv"])), c(r["p_S"].transpose(1, 0, 2).reshape(1, 1, H_A, HD, HD)),
        c(k[:SEQ].reshape(*pg, H_C, HD)), c(v[:SEQ].reshape(*pg, H_C, HD)), c(lf[:SEQ].reshape(*pg, H_C)),
        c(back(rows(r["p_fconv"]))),
        c(srows(r["s_gconv"])), c(r["s_S"].transpose(2, 1, 0, 3).reshape(1, NBATCH, H_A, HD, HD)),
        c(k[SEQ:].reshape(*smp, H_C, HD)), c(v[SEQ:].reshape(*smp, H_C, HD)), c(lf[SEQ:].reshape(*smp, H_C)),
        c(r["chunk_v"].reshape(*smp, W_B)), c(back(srows(r["s_fconv"]))),
    )
```
